# Optimizing a Trainium2 kernel written in Bass

```python
import math
import jax, jax.numpy as jnp
from jax import lax
import numpy as np

D_MODEL = 1024
BATCH = 1
SEQ = 256
DEPTH = 1

GRID_W = 64
CTX_LEN = 256
EPS = 1e-6
N_MOD = 6

GLA_HEADS = 4
GLA_DK = D_MODEL // 2
GLA_DV = D_MODEL
GLA_HEAD_K = GLA_DK // GLA_HEADS
GLA_HEAD_V = GLA_DV // GLA_HEADS
GLA_GATE_RANK = 16
GLA_GATE_NORM = 16.0
GLA_CHUNK = 64

HY_WIDTH = D_MODEL
HY_SHORT = 3
HY_EMB = 33
HY_ORDER = 64
HY_FAST_DECAY = 0.3
HY_SLOW_DECAY = 1.5
HY_TARGET = 1e-2

N_EXPERTS = 32
TOP_K = 4
D_FF = D_MODEL
SWIGLU_LIMIT = 7.0
SWIGLU_ALPHA = 1.702

IN_SIZES = (GLA_DK, GLA_DK, GLA_DV, GLA_DV, GLA_GATE_RANK, GLA_GATE_RANK, 3 * HY_WIDTH, D_MODEL, D_MODEL)
IN_COLS = GLA_DK * 2 + GLA_DV * 2 + GLA_GATE_RANK * 2 + 3 * HY_WIDTH + 2 * D_MODEL

kernel_name = "hybrid_gla_hyena_moe_dit_block"

def rms_norm(x, w):
    xf = x.astype(jnp.float32)
    y = xf * lax.rsqrt(jnp.mean(xf * xf, axis=-1, keepdims=True) + EPS)
    return (y * w.astype(jnp.float32)).astype(x.dtype)

def ada_params(cvec, w_ada, b_ada):
    m = jax.nn.silu(cvec) @ w_ada + b_ada
    return jnp.split(m[:, None, :], N_MOD, axis=-1)

def split_proj(p):
    idx = np.cumsum(np.array(IN_SIZES))[:-1].tolist()
    return jnp.split(p, idx, axis=-1)

def gla_scan(q, k, v, log_g, s0):
    B, H, L, dk = q.shape
    dv = v.shape[-1]
    n = L // GLA_CHUNK
    C = GLA_CHUNK
    q = q.reshape(B, H, n, C, dk)
    k = k.reshape(B, H, n, C, dk)
    v = v.reshape(B, H, n, C, dv)
    b = jnp.cumsum(log_g.reshape(B, H, n, C, dk), axis=3)
    b_last = b[:, :, :, -1:, :]
    q_dec = q * jnp.exp(b)
    k_inv = k * jnp.exp(-b)
    k_upd = k * jnp.exp(b_last - b)
    mask = jnp.tril(jnp.ones((C, C), dtype=bool))
    att = jnp.where(mask, jnp.einsum('bhnid,bhnjd->bhnij', q_dec, k_inv), 0.0)
    o_intra = jnp.einsum('bhnij,bhnjv->bhniv', att, v)
    upd = jnp.einsum('bhncd,bhncv->bhndv', k_upd, v)
    decay = jnp.exp(b_last[:, :, :, 0, :])

    def step(s, xs):
        q_c, dec_c, upd_c = xs
        o_c = jnp.einsum('bhcd,bhdv->bhcv', q_c, s)
        s = dec_c[..., None] * s + upd_c
        return s, o_c

    xs = (jnp.moveaxis(q_dec, 2, 0), jnp.moveaxis(decay, 2, 0), jnp.moveaxis(upd, 2, 0))
    s_final, o_inter = lax.scan(step, s0, xs)
    o = o_intra + jnp.moveaxis(o_inter, 0, 2)
    return o.reshape(B, H, L, dv), s_final

def gla_bidir(q, k, v, g_f, g_b, s0_f, s0_b):
    o_f, s_f = gla_scan(q, k, v, g_f, s0_f)
    flip = lambda t: jnp.flip(t, axis=2)
    o_b, s_b = gla_scan(flip(q), flip(k), flip(v), flip(g_b), s0_b)
    return o_f + flip(o_b), s_f, s_b

def gla_inputs(q, k, v, r_f, r_b, w_gk_f, b_gk_f, w_gk_b, b_gk_b):
    B, L, _ = q.shape
    heads = lambda t, d: jnp.moveaxis(t.astype(jnp.float32).reshape(B, L, GLA_HEADS, d), 2, 1)
    qh = heads(q, GLA_HEAD_K) * (GLA_HEAD_K ** -0.5)
    kh = heads(k, GLA_HEAD_K)
    vh = heads(v, GLA_HEAD_V)
    g_f = jax.nn.log_sigmoid((r_f @ w_gk_f + b_gk_f).astype(jnp.float32)) / GLA_GATE_NORM
    g_b = jax.nn.log_sigmoid((r_b @ w_gk_b + b_gk_b).astype(jnp.float32)) / GLA_GATE_NORM
    return qh, kh, vh, heads(g_f, GLA_HEAD_K), heads(g_b, GLA_HEAD_K)

def short_conv(u, w, b):
    L = u.shape[1]
    up = jnp.pad(u, ((0, 0), (1, 1), (0, 0)))
    return up[:, :L] * w[0] + up[:, 1:L + 1] * w[1] + up[:, 2:] * w[2] + b

def hyena_kernel(L, w1, b1, w2, b2, w3, b3, w4, freq):
    f32 = jnp.float32
    bands = (HY_EMB - 1) // 2
    pos = jnp.arange(L, dtype=f32)[:, None]
    t = pos / max(L - 1, 1)
    f = jnp.linspace(1e-4, bands - 1, bands, dtype=f32)[None]
    ang = (2.0 * math.pi / L) * pos * f
    z = jnp.concatenate([t, jnp.cos(ang), -jnp.sin(ang)], axis=-1)
    fr = freq.astype(f32)
    h = jnp.sin(fr * (z @ w1.astype(f32) + b1.astype(f32)))
    h = jnp.sin(fr * (h @ w2.astype(f32) + b2.astype(f32)))
    h = jnp.sin(fr * (h @ w3.astype(f32) + b3.astype(f32)))
    h = h @ w4.astype(f32)
    deltas = jnp.abs(jnp.linspace(math.log(HY_TARGET) / HY_SLOW_DECAY,
                                  math.log(HY_TARGET) / HY_FAST_DECAY, HY_WIDTH, dtype=f32))
    window = jnp.exp(-t * deltas[None])
    h_f = h[:, :HY_WIDTH] * window
    h_b = h[:, HY_WIDTH:] * window
    return jnp.concatenate([h_f, jnp.zeros((1, HY_WIDTH), f32), jnp.flip(h_b[1:], axis=0)], axis=0)

def long_conv_bidir(u, k2l, bias):
    L = u.shape[1]
    uf = u.astype(jnp.float32)
    spec = jnp.fft.rfft(uf, n=2 * L, axis=1) * jnp.fft.rfft(k2l, axis=0)[None]
    y = jnp.fft.irfft(spec, n=2 * L, axis=1)[:, :L]
    return y + uf * bias.astype(jnp.float32)

def hyena_branch(u3, grid_rows, lp):
    B, L, C3 = u3.shape
    if grid_rows is not None:
        uc = short_conv(u3.reshape(B * grid_rows, GRID_W, C3), lp["hy_conv_w"], lp["hy_conv_b"]).reshape(B, L, C3)
    else:
        uc = short_conv(u3, lp["hy_conv_w"], lp["hy_conv_b"])
    x0, x1, v = jnp.split(uc, 3, axis=-1)
    k2l = hyena_kernel(L, lp["hy_f_w1"], lp["hy_f_b1"], lp["hy_f_w2"], lp["hy_f_b2"],
                       lp["hy_f_w3"], lp["hy_f_b3"], lp["hy_f_w4"], lp["hy_sin_freq"])
    z = long_conv_bidir(v * x1, k2l, lp["hy_bias"])
    y = x0 * z.astype(x0.dtype)
    return y @ lp["w_hy_out"]

def mixer_pre(h, lp):
    q, k, v, og, r_f, r_b, hy, m_a, m_b = split_proj(h @ lp["w_in"])
    gla_in = gla_inputs(q, k, v, r_f, r_b, lp["w_gk_f"], lp["b_gk_f"], lp["w_gk_b"], lp["b_gk_b"])
    return gla_in, (og, hy, m_a, m_b)

def mixer_post(o_gla, rest, grid_rows, lp):
    og, hy, m_a, m_b = rest
    B, L, _ = og.shape
    o = jnp.moveaxis(o_gla, 1, 2)
    o = rms_norm(o, lp["gla_norm"]).reshape(B, L, GLA_DV).astype(og.dtype)
    branch_a = (o * jax.nn.silu(og)) @ lp["w_gla_out"]
    branch_b = hyena_branch(hy, grid_rows, lp)
    y = jax.nn.sigmoid(m_a) * branch_a + jax.nn.sigmoid(m_b) * branch_b
    return y @ lp["w_out"]

def moe(h, w_router, b_router, w_up, b_up, w_down, b_down):
    B, L, D = h.shape
    t = h.reshape(B * L, D)
    logits = (t @ w_router + b_router).astype(jnp.float32)
    top_val, top_idx = lax.top_k(logits, TOP_K)
    top_w = jax.nn.softmax(top_val, axis=-1)
    gates = jnp.einsum('nk,nke->ne', top_w, jax.nn.one_hot(top_idx, N_EXPERTS, dtype=jnp.float32))
    out = jnp.zeros((B * L, D), jnp.float32)
    for e in range(N_EXPERTS):
        u = t @ w_up[e] + b_up[e]
        glu = jnp.minimum(u[:, 0::2], SWIGLU_LIMIT)
        lin = jnp.clip(u[:, 1::2], -SWIGLU_LIMIT, SWIGLU_LIMIT)
        a = glu * jax.nn.sigmoid(SWIGLU_ALPHA * glu) * (lin + 1.0)
        out = out + gates[:, e:e + 1] * (a @ w_down[e] + b_down[e])
    return out.astype(h.dtype).reshape(B, L, D)

def setup_inputs(seed: int = 0) -> dict:
    key = jax.random.key(seed)
    ks = iter(jax.random.split(key, 40))
    nrm = lambda shape, s: jax.random.normal(next(ks), shape, jnp.float32) * s
    Dp = DEPTH
    E = N_EXPERTS
    return {
        "x": nrm((BATCH, SEQ, D_MODEL), 1.0),
        "c": nrm((BATCH, D_MODEL), 1.0),
        "ctx": nrm((BATCH, CTX_LEN, D_MODEL), 1.0),
        "c_ctx": nrm((D_MODEL,), 1.0),
        "w_ada": nrm((Dp, D_MODEL, N_MOD * D_MODEL), D_MODEL ** -0.5),
        "b_ada": nrm((Dp, N_MOD * D_MODEL), 0.02),
        "norm_mix": 1.0 + nrm((Dp, D_MODEL), 0.02),
        "norm_ffn": 1.0 + nrm((Dp, D_MODEL), 0.02),
        "w_in": nrm((Dp, D_MODEL, IN_COLS), D_MODEL ** -0.5),
        "w_gk_f": nrm((Dp, GLA_GATE_RANK, GLA_DK), GLA_GATE_RANK ** -0.5),
        "b_gk_f": nrm((Dp, GLA_DK), 0.1),
        "w_gk_b": nrm((Dp, GLA_GATE_RANK, GLA_DK), GLA_GATE_RANK ** -0.5),
        "b_gk_b": nrm((Dp, GLA_DK), 0.1),
        "gla_norm": 1.0 + nrm((Dp, GLA_HEAD_V), 0.02),
        "w_gla_out": nrm((Dp, GLA_DV, D_MODEL), GLA_DV ** -0.5),
        "hy_conv_w": nrm((Dp, HY_SHORT, 3 * HY_WIDTH), HY_SHORT ** -0.5),
        "hy_conv_b": nrm((Dp, 3 * HY_WIDTH), 0.02),
        "hy_f_w1": nrm((Dp, HY_EMB, HY_ORDER), HY_EMB ** -0.5),
        "hy_f_b1": nrm((Dp, HY_ORDER), 0.1),
        "hy_f_w2": nrm((Dp, HY_ORDER, HY_ORDER), HY_ORDER ** -0.5),
        "hy_f_b2": nrm((Dp, HY_ORDER), 0.1),
        "hy_f_w3": nrm((Dp, HY_ORDER, HY_ORDER), HY_ORDER ** -0.5),
        "hy_f_b3": nrm((Dp, HY_ORDER), 0.1),
        "hy_f_w4": nrm((Dp, HY_ORDER, 2 * HY_WIDTH), 0.02),
        "hy_sin_freq": 1.0 + nrm((Dp, HY_ORDER), 0.02),
        "hy_bias": nrm((Dp, HY_WIDTH), 0.5),
        "w_hy_out": nrm((Dp, HY_WIDTH, D_MODEL), HY_WIDTH ** -0.5),
        "w_out": nrm((Dp, D_MODEL, D_MODEL), D_MODEL ** -0.5),
        "w_router": nrm((Dp, D_MODEL, E), D_MODEL ** -0.5),
        "b_router": nrm((Dp, E), 0.01),
        "w_up": nrm((Dp, E, D_MODEL, 2 * D_FF), D_MODEL ** -0.5),
        "b_up": nrm((Dp, E, 2 * D_FF), 0.02),
        "w_down": nrm((Dp, E, D_FF, D_MODEL), D_FF ** -0.5),
        "b_down": nrm((Dp, E, D_MODEL), 0.02),
        "norm_final": 1.0 + nrm((D_MODEL,), 0.02),
    }

def reference(x, c, ctx, c_ctx, w_ada, b_ada, norm_mix, norm_ffn, w_in, w_gk_f, b_gk_f, w_gk_b, b_gk_b,
              gla_norm, w_gla_out, hy_conv_w, hy_conv_b, hy_f_w1, hy_f_b1, hy_f_w2, hy_f_b2, hy_f_w3, hy_f_b3,
              hy_f_w4, hy_sin_freq, hy_bias, w_hy_out, w_out, w_router, b_router, w_up, b_up, w_down, b_down,
              norm_final):
    params = dict(w_ada=w_ada, b_ada=b_ada, norm_mix=norm_mix, norm_ffn=norm_ffn, w_in=w_in,
                  w_gk_f=w_gk_f, b_gk_f=b_gk_f, w_gk_b=w_gk_b, b_gk_b=b_gk_b, gla_norm=gla_norm,
                  w_gla_out=w_gla_out, hy_conv_w=hy_conv_w, hy_conv_b=hy_conv_b, hy_f_w1=hy_f_w1,
                  hy_f_b1=hy_f_b1, hy_f_w2=hy_f_w2, hy_f_b2=hy_f_b2, hy_f_w3=hy_f_w3, hy_f_b3=hy_f_b3,
                  hy_f_w4=hy_f_w4, hy_sin_freq=hy_sin_freq, hy_bias=hy_bias, w_hy_out=w_hy_out, w_out=w_out,
                  w_router=w_router, b_router=b_router, w_up=w_up, b_up=b_up, w_down=w_down, b_down=b_down)
    B = x.shape[0]
    rows = x.shape[1] // GRID_W
    xc = ctx
    for i in range(DEPTH):
        lp = {name: arr[i] for name, arr in params.items()}
        last = i == DEPTH - 1
        sh1, sc1, g1, sh2, sc2, g2 = ada_params(c, lp["w_ada"], lp["b_ada"])
        csh1, csc1, cg1, csh2, csc2, cg2 = ada_params(c_ctx[None], lp["w_ada"], lp["b_ada"])

        hx = rms_norm(x, lp["norm_mix"]) * (1.0 + sc1) + sh1
        hc = rms_norm(xc, lp["norm_mix"]) * (1.0 + csc1) + csh1
        gla_x, rest_x = mixer_pre(hx, lp)
        gla_c, rest_c = mixer_pre(hc, lp)
        zero = jnp.zeros((B, GLA_HEADS, GLA_HEAD_K, GLA_HEAD_V), jnp.float32)
        o_c, s_ctx_f, s_ctx_b = gla_bidir(*gla_c, zero, zero)
        o_x, _, _ = gla_bidir(*gla_x, s_ctx_f, s_ctx_b)
        x = x + g1 * mixer_post(o_x, rest_x, rows, lp)

        hx2 = rms_norm(x, lp["norm_ffn"]) * (1.0 + sc2) + sh2
        x = x + g2 * moe(hx2, lp["w_router"], lp["b_router"], lp["w_up"], lp["b_up"], lp["w_down"], lp["b_down"])

        if not last:
            xc = xc + cg1 * mixer_post(o_c, rest_c, None, lp)
            hc2 = rms_norm(xc, lp["norm_ffn"]) * (1.0 + csc2) + csh2
            xc = xc + cg2 * moe(hc2, lp["w_router"], lp["b_router"], lp["w_up"], lp["b_up"], lp["w_down"], lp["b_down"])
    return rms_norm(x, norm_final)


_drawn_inputs = setup_inputs


def setup_inputs(seed=0):
    import zlib

    import numpy as np

    out = dict(_drawn_inputs(seed))
    spreads = {}
    factors = {'gla_norm': 3.405,
     'hy_sin_freq': 3.231,
     'b_up': 6.939,
     'b_down': 8.0,
     'norm_final': 8.109,
     'hy_conv_b': 2.781,
     'b_router': 3.972}
    for name, (base, spread) in spreads.items():
        noise = np.random.default_rng([zlib.crc32(name.encode()), seed]).standard_normal(out[name].shape)
        drawn = base * np.exp(spread * noise) if base else spread * noise
        out[name] = __import__('jax').numpy.asarray(drawn.astype(out[name].dtype))
    for name, factor in factors.items():
        out[name] = (out[name] * factor).astype(out[name].dtype)
    return out
```

```python
from contextlib import ExitStack

import numpy as np

import concourse.bass as bass
from concourse import mybir

F32 = mybir.dt.float32
BF16 = mybir.dt.bfloat16
I32 = mybir.dt.int32
U32 = mybir.dt.uint32
ALU = mybir.AluOpType
ACT = mybir.ActivationFunctionType
AX_X = mybir.AxisListType.X

P = 128
D = 1024
T = 256
KT = D // P
TT = T // P
HEADS = 4
DK = 128
DV = 256
CHUNK = 64
GNORM = 16.0
EMB, ORDER = 33, 64
E = 32
SLOTS = 64
MAXI = 64
EPS = 1e-6
LIMIT, ALPHA = 7.0, 1.702
MAGIC = 12582912.0
PI = 3.141592
TWO_PI_HI = 6.28125
TWO_PI_LO = 2 * np.pi - 6.28125

ROUNDS = ["ada0", "ada1", "qk", "v", "hv", "ada2", "hx1", "ada3", "hx0", "og", "ada4", "ma",
          "ada5", "mb", "gla", "hyo", "out"]
PROJ = [r for r in ROUNDS if not r.startswith("ada")]
FAR = 1000.0


def columns(parts):
    at, where = 0, {}
    for name, width in parts:
        where[name] = (at, width)
        at += width
    return where, at


VEC, NVEC = columns([("c", 8), ("cctx", 8), ("nm", 8), ("nf", 8), ("nfin", 8), ("bada", 48),
                     ("cw", 72), ("cb", 24), ("hb", 8), ("gn", 2), ("hmlp", 4)])
CON, NCON = columns([("ident", 128), ("ones", 128), ("mask", 512), ("rest", 256), ("after", 128),
                     ("before", 128), ("all16", 128), ("dft", 1024), ("idft", 1024),
                     ("slot", 128), ("tri", 96), ("eid", 1)])



def build_program(nc, vecs, cons, xt, zt, hw, hw4, window, wmix, wr, wgk, wrouter, brouter,
                  wup, bup, wdown, bdown, out):
    with ExitStack() as ctx:
        made = {}

        def sem(name):
            if name not in made:
                made[name] = ctx.enter_context(nc.semaphore(name))
            return made[name]

        def sb(name, shape, dt=F32):
            return ctx.enter_context(nc.sbuf_tensor(name, shape, dt))

        ring = sb("ring", [P, 8, KT, 256])
        arena = sb("arena", [P, 15, 2048])
        con = sb("con", [P, NCON])
        vec = sb("vec", [P, NVEC])
        kcx = sb("kcx", [P, TT, 512])
        mod = sb("mod", [P, 6, KT, 2])
        rstd = sb("rstd", [P, 512])
        csil = sb("csil", [P, KT, 32])
        adar = sb("adar", [P, 256])
        dec = sb("dec", [P, 2, HEADS, 4])
        eps = sb("eps", [P, 1])[:, :]
        bank = [ctx.enter_context(nc.psum_tensor(f"bank{i}", [P, 512], F32)) for i in range(8)]

        def C(name, a=0, b=None, p=P):
            at, width = CON[name]
            return con[0:p, at + a:at + (width if b is None else b)]

        def V(name, i, p=P):
            return vec[0:p, VEC[name][0] + i:VEC[name][0] + i + 1]

        def region(r, n=1):
            return arena[:, r:r + n, :].rearrange("p r n -> p (r n)")

        def half(b, h):
            return bank[b][:, h * 256:h * 256 + 256]

        ident, ones = C("ident"), C("ones")
        dft = C("dft").rearrange("p (a s f) -> p a s f", a=2, s=TT)
        idft = C("idft").rearrange("p (a s f) -> p a s f", a=2, s=TT)

        xT = region(0, 2).rearrange("p (k t) -> p k t", k=KT)
        xres, xctx = xT[:, :, 0:T], xT[:, :, T:2 * T]
        x1c = utok = act = xctx
        hx = region(2, 2).rearrange("p (k t) -> p k t", k=KT)
        hxx, hxc = hx[:, :, 0:T], hx[:, :, T:2 * T]
        uT = hxc
        spec = region(4, 2).rearrange("p (a f c) -> p a f c", a=2, f=TT)
        og = region(4).rearrange("p (m t) -> p m t", m=8)
        sma = region(5).rearrange("p (m t) -> p m t", m=8)
        qk = region(6).rearrange("p (m t) -> p m t", m=8)
        x0T = qk
        tok = region(6).rearrange("p (t c) -> p t c", t=TT)
        vx = region(7).rearrange("p (t c) -> p t c", t=TT)
        smb = region(7).rearrange("p (m t) -> p m t", m=8)
        vc = region(8).rearrange("p (t c) -> p t c", t=TT)
        sst = [region(r)[:, 0:1536].rearrange("p (d c v) -> p d c v", d=2, c=3) for r in (8, 10)]
        gc = region(9).rearrange("p (t d c) -> p t d c", t=TT, d=2)
        gx = region(10).rearrange("p (t d c) -> p t d c", t=TT, d=2)
        s0 = region(9).rearrange("p (h d v) -> p h d v", h=HEADS, d=2)
        win = region(11).rearrange("p (t c) -> p t c", t=TT)
        hsum = region(12).rearrange("p (t c) -> p t c", t=TT)
        hdif = region(13).rearrange("p (t c) -> p t c", t=TT)
        w4 = region(14)[0:64, :]
        kupc = region(11).rearrange("p (t d c) -> p t d c", t=TT, d=2)
        kupx = region(13).rearrange("p (t d c) -> p t d c", t=TT, d=2)
        qd = region(11).rearrange("p (d h t) -> p d h t", d=2, h=HEADS)
        ki = region(12).rearrange("p (d h t) -> p d h t", d=2, h=HEADS)
        sqo = region(12).rearrange("p (m t) -> p m t", m=8)
        rso = region(11)[:, 0:1024].rearrange("p (h t) -> p h t", h=HEADS)
        att = region(14).rearrange("p (h n) -> p h n", h=HEADS)
        tmp = region(14).rearrange("p (n c) -> p n c", n=4)
        zsb = region(7)[0:EMB, 0:256]
        hwsb = region(7)[0:64, 256:448]
        hact = region(7)[0:64, 512:1536].rearrange("p (n t) -> p n t", n=4)
        sq = region(8)[:, 0:1024].rearrange("p (n t) -> p n t", n=2)
        htmp = region(6)[:, 0:512]
        wrsb = region(12)[:, 0:256].rearrange("p (k n) -> p k n", k=KT)
        rT = region(12)[0:17, 256:1280].rearrange("p (d n) -> p d n", d=2)
        wgksb = region(13)[0:17, 0:1024].rearrange("p (d n) -> p d n", d=2)
        down = arena[:, 11:15, :].rearrange("p u (a n) -> p u a n", a=2)
        glu, sg, lin, am = (region(8)[:, a:a + 512] for a in (0, 512, 1024, 1536))
        aT = region(9)[:, 0:512].rearrange("p (b h s) -> p b h s", b=4, h=2)
        ysb = region(9)[:, 512:1024]
        xe = region(9)[:, 1024:1536].rearrange("p (k s) -> p k s", k=KT)
        pick = region(9)[:, 1536:1792].rearrange("p (t s) -> p t s", t=TT)
        spread = region(9)[:, 1792:2048].rearrange("p (t s) -> p t s", t=TT)
        back = region(10)[:, 0:256]
        posI = region(10)[:, 256:384].rearrange("p (t i) -> p t i", t=TT)
        gateI = region(10)[:, 384:512].rearrange("p (t i) -> p t i", t=TT)
        T3 = region(10)[0:96, 512:576]
        Q = region(10)[0:32, 576:640]
        eids = region(10)[0:1, 640:704].bitcast(I32)
        nitems = region(10)[0:1, 704:705].bitcast(I32)
        bsel = region(10)[0:96, 768:800].bitcast(BF16)
        bp = region(10)[0:96, 1024:2048].bitcast(BF16)
        bupsb = region(4)[0:96, :]
        R3 = region(5)
        wrt = R3[:, 0:256].rearrange("p (k e) -> p k e", k=KT)
        brt = R3[0:1, 256:288]
        logit = R3[:, 288:352].rearrange("p (t e) -> p t e", t=TT)
        m8 = R3[:, 352:368].rearrange("p (t e) -> p t e", t=TT)
        i8 = R3[:, 368:384].bitcast(U32).rearrange("p (t e) -> p t e", t=TT)
        if8 = R3[:, 384:400].rearrange("p (t e) -> p t e", t=TT)
        nm = R3[:, 400:402]
        ew = R3[:, 402:410].rearrange("p (t e) -> p t e", t=TT)
        es = R3[:, 410:412]
        gk = R3[:, 448:704].rearrange("p (t k e) -> p t k e", t=TT, k=4)
        sk = R3[:, 704:960].rearrange("p (t k e) -> p t k e", t=TT, k=4)
        sel = R3[:, 960:1152].rearrange("p (t e) -> p t e", t=TT)
        gate = R3[:, 1152:1216].rearrange("p (t e) -> p t e", t=TT)
        cnt = R3[0:96, 1216:1224]
        posm = R3[0:32, 1280:1536]
        selT = R3[0:32, 1536:1792]
        gateT = R3[0:32, 1792:2048]
        bdn = region(7)[0:32, 0:1024]
        zero = region(7)[0:32, 1024:1536]

        block = ctx.enter_context(nc.Block())

        @block.sync
        def _(sp):
            def unit(i, r, j, first):
                slot = 4 * r + j
                if not first:
                    sp.wait_ge(sem("unit_done"), 4 * i + 4 * r + j - 7)
                if isinstance(i, int):
                    src = wmix[i + r, j]
                else:
                    src = wmix[bass.ds(i + r, 1), j].rearrange("a p n -> (a p) n")
                sp.dma_start(ring[:, slot].rearrange("p k n -> p (k n)"),
                             src).then_inc(sem(f"ring_loaded{slot}"), 16)

            for r in range(2):
                for j in range(4):
                    unit(0, r, j, True)
            with sp.Fori(2, 16, 2) as i:
                for r in range(2):
                    for j in range(4):
                        unit(i, r, j, False)
            for j in range(4):
                unit(16, 0, j, False)

            def up_chunk(src, k):
                slot = (k + 4) % 8
                sp.dma_start(ring[:, slot].rearrange("p k n -> p (k n)"),
                             src).then_inc(sem(f"up_loaded{k}"), 16)

            def down_chunk(src, u):
                sp.dma_start(down[:, u], src).then_inc(sem(f"down_loaded{u}"), 16)

            for k in range(4):
                sp.wait_ge(sem("unit_done"), 4 * 15 + k + 1)
                up_chunk(wup[0, k], k)
            for k in range(4, 8):
                sp.wait_ge(sem("unit_done"), 4 * 16 + k - 3)
                up_chunk(wup[0, k], k)
            sp.wait_ge(sem("act_ready"), 1)
            for u in range(4):
                down_chunk(wdown[0, u].rearrange("a p n -> p a n"), u)
            sp.wait_ge(sem("list_ready"), 2)
            n = sp.value_load(nitems, min_val=E, max_val=48)
            with sp.Fori(1, n) as i:
                e = sp.value_load(eids[0:1, bass.ds(i, 1)], min_val=0, max_val=E - 1)
                for k in range(8):
                    sp.wait_ge(sem("up_used"), 8 * i + (k - 7))
                    up_chunk(wup[bass.ds(e, 1), k].rearrange("a p n -> (a p) n"), k)
                for u in range(4):
                    sp.wait_ge(sem("down_used"), 4 * i + (u - 3))
                    down_chunk(wdown[bass.ds(e, 1), u].rearrange("e a p n -> p (e a) n"), u)
            for k in range(KT):
                sp.wait_ge(sem("out_ready"), k + 1)
                sp.dma_start(out[k], hxx[:, k, :]).then_inc(sem("stored"), 16)
            sp.wait_ge(sem("stored"), 16 * KT)

        @block.tensor
        def _(pe):
            mm = pe.matmul

            def loaded(name, i, j):
                slot = 4 * (i % 2) + j
                pe.wait_ge(sem(f"ring_loaded{slot}"), 16 * (i // 2 + 1))
                return ring[:, slot]

            def projection(name, rhs, units=range(4), tokens=None):
                i = ROUNDS.index(name)
                before = PROJ[PROJ.index(name) - 1] if name != PROJ[0] else None
                for j in units:
                    w = loaded(name, i, j)
                    if before:
                        pe.wait_ge(sem(f"evac_{before}"), j + 1)
                    for m in range(2):
                        for k in range(KT):
                            last = mm(half(j, m), w[:, k, m * P:m * P + P], rhs[:, k, :],
                                      start=(k == 0), stop=(k == KT - 1))
                    if tokens and j >= 2:
                        last = by_token(w, hxc, 4 + j)
                    last.then_inc(sem("unit_done"), 1)

            def by_token(w, lhs, b):
                for t in range(TT):
                    for k in range(KT):
                        last = mm(half(b, t), lhs[:, k, t * P:t * P + P], w[:, k, :],
                                  start=(k == 0), stop=(k == KT - 1))
                return last

            def mean_square(base, b, n):
                for k in range(KT):
                    pe.wait_ge(sem("sq_ready"), base + k + 1)
                    mm(bank[b][:, 0:n], ones, sq[:, k % 2, 0:n], start=(k == 0),
                       stop=(k == KT - 1)).then_inc(sem("sq_used"), 1)

            def ada(s, bank_reads):
                i = ROUNDS.index(f"ada{s}")
                w = [loaded("ada", i, j) for j in range(4)]
                for name, n in bank_reads:
                    pe.wait_ge(sem(name), n)
                for k in range(KT):
                    for j in range(4):
                        last = mm(bank[4][32 * j:32 * j + 32, 0:256], csil[:, k, :], w[j][:, k, :],
                                  start=(k == 0), stop=(k == KT - 1))
                        if k == KT - 1:
                            last.then_inc(sem("unit_done"), 1)
                pe.wait_ge(sem("ada_rows"), s + 1)
                for j in range(2):
                    last = pe.transpose(bank[5][:, j * P:j * P + P], adar[:, j * P:j * P + P], ident)
                last.then_inc(sem("ada_turned"), 1)

            pe.wait_ge(sem("hw_loaded"), 32)
            pe.wait_ge(sem("con_loaded"), 16)
            mm(bank[4][0:64, 0:256], hwsb[0:EMB, 0:64], zsb, start=True,
               stop=True).then_inc(sem("mlp_mm"), 1)
            mean_square(0, 5, 512)
            for n in range(2):
                pe.wait_ge(sem("mlp_sin"), n + 1)
                mm(bank[4][0:64, 0:256], hwsb[:, 64 + 64 * n:128 + 64 * n], hact[:, 3, :], start=True,
                   stop=True).then_inc(sem("mlp_mm"), 1)
            pe.wait_ge(sem("mlp_sin"), 3)
            pe.wait_ge(sem("w4_loaded"), 16)
            pe.wait_ge(sem("rms"), 1)
            for n in range(8):
                t, c = n // 4, n % 4
                mm(bank[n][:, :], hact[:, 3, t * P:t * P + P], w4[:, c * 512:c * 512 + 512],
                   start=True, stop=True).then_inc(sem("taps_mm"), 1)
            pe.wait_ge(sem("taps_ready"), 4)
            for a, taps in ((0, hsum), (1, hdif)):
                for n in range(4):
                    f, c = n // 2, n % 2
                    for s in range(TT):
                        last = mm(bank[4 * a + n][:, :], dft[:, a, s, f * P:f * P + P],
                                  taps[:, s, c * 512:c * 512 + 512], start=(s == 0), stop=(s == TT - 1))
                    last.then_inc(sem("spec_mm"), 1)
            pe.wait_ge(sem("csil_ready"), 1)
            ada(0, [("spec_ready", 8)])
            ada(1, [("mod_ready", 1)])

            pe.wait_ge(sem("hx_ready"), 2 * KT)
            projection("qk", hxx, tokens=True)
            pe.wait_ge(sem("wr_loaded"), 16)
            pe.wait_ge(sem("mod_ready"), 2)
            for d in range(2):
                for k in range(KT):
                    last = mm(bank[4 + d][0:16, :], wrsb[:, k, 16 * d:16 * d + 16], hx[:, k, :],
                              start=(k == 0), stop=(k == KT - 1))
                last.then_inc(sem("low_mm"), 1)
            i = ROUNDS.index("v")
            for j in range(4):
                w = loaded("v", i, j)
                pe.wait_ge(sem("evac_qk"), j + 1)
                by_token(w, hxx, j)
                if j < 2:
                    pe.wait_ge(sem("low_ready"), j + 1)
                else:
                    pe.wait_ge(sem("kc_ready"), j - 1)
                by_token(w, hxc, 4 + j).then_inc(sem("unit_done"), 1)
            pe.wait_ge(sem("wgk_loaded"), 16)
            pe.wait_ge(sem("low_ready"), 2)
            for n in range(8):
                t, d = n // 2, n % 2
                if n == 0:
                    pe.wait_ge(sem("evac_vc"), 4)
                if n >= 4:
                    pe.wait_ge(sem("g_ready"), n - 3)
                mm(bank[(6, 7, 4, 5)[n % 4]][:, :], rT[:, d, t * P:t * P + P], wgksb[:, d, :],
                   start=True, stop=True).then_inc(sem("gate_mm"), 1)
            projection("hv", hxx)
            pe.wait_ge(sem("g_ready"), 8)
            after, earlier, every = C("after"), C("before"), C("all16")
            for n, terms in enumerate(([(after, 0), (every, 1)], [(earlier, 0)],
                                       [(after, 1)], [(every, 0), (earlier, 1)])):
                for m, (tri, s) in enumerate(terms):
                    last = mm(bank[4 + n][:, :], tri, gc[:, s, n % 2, :], start=(m == 0),
                              stop=(m == len(terms) - 1))
                last.then_inc(sem("crest_mm"), 1)
            ada(2, [("crest_read", 4)])
            projection("hx1", hxx)
            pe.wait_ge(sem("kupc_ready"), 4)
            pe.wait_ge(sem("mod_ready"), 3)
            for h in range(HEADS):
                for d in range(2):
                    for t in range(TT):
                        last = mm(half(4 + h, d), kupc[:, t, d, h * DK:h * DK + DK],
                                  vc[:, t, h * DV:h * DV + DV], start=(t == 0), stop=(t == TT - 1))
                last.then_inc(sem("s0_mm"), 1)
            for d in range(2):
                for h in range(HEADS):
                    n = d * HEADS + h
                    if n % 2 == 0:
                        pe.wait_ge(sem("s0_ready"), n // 2 + 1)
                    for t in range(TT):
                        last = mm(half(4 + n // 2, n % 2)[:, t * P:t * P + P],
                                  gx[:, t, d, h * DK:h * DK + DK],
                                  C("mask", d * P, d * P + P), start=True, stop=True)
                    if n % 2:
                        last.then_inc(sem("decay_mm"), 1)
            pe.wait_ge(sem("decay_read"), 4)
            for t in range(TT):
                for h in range(HEADS):
                    last = pe.transpose(bank[4 + t][:, h * P:h * P + P], qk[:, 4 + h, t * P:t * P + P],
                                        ident)
                last.then_inc(sem("k_turned"), 1)
            pe.wait_ge(sem("ktok_ready"), 2)
            ada(3, [])
            pe.wait_ge(sem("mod_ready"), 4)
            for n in range(4):
                t, d = n // 2, n % 2
                mm(bank[4 + n][:, :], C("rest", d * P, d * P + P), gx[:, t, d, :], start=True,
                   stop=True).then_inc(sem("rest_mm"), 1)
            projection("hx0", hxx)
            pe.wait_ge(sem("u_ready"), 1)
            pe.wait_ge(sem("rest_read"), 4)
            for b in range(4):
                for c in range(2 * b, 2 * b + 2):
                    for t in range(TT):
                        last = pe.transpose(bank[4 + b][:, (c % 2) * 256 + t * P:][:, 0:P],
                                            uT[:, c, t * P:t * P + P], ident)
                last.then_inc(sem("u_turned"), 1)
            pe.wait_ge(sem("utok_ready"), 4)
            for f in range(2):
                if f:
                    pe.wait_ge(sem("prod_ready"), 2)
                for c in range(2):
                    for a in range(2):
                        for s in range(TT):
                            last = mm(bank[4 + 2 * a + c][:, :], dft[:, a, s, f * P:f * P + P],
                                      utok[:, 4 * c:4 * c + 4, s * P:s * P + P],
                                      start=(s == 0), stop=(s == TT - 1))
                    last.then_inc(sem("u_spec"), 1)
            pe.wait_ge(sem("qdki_ready"), 4)
            pe.wait_ge(sem("prod_ready"), 4)
            for h in range(HEADS):
                for t in range(TT):
                    for d in range(2):
                        last = mm(bank[4 + h][:, (2 * t + d) * P:(2 * t + d) * P + P],
                                  ki[:, d, h, t * P:t * P + P], qd[:, d, h, t * P:t * P + P],
                                  start=True, stop=True)
                last.then_inc(sem("att_mm"), 1)
            for c in range(KT):
                if c % 2 == 0:
                    pe.wait_ge(sem("att_ready"), c // 2 + 1)
                for n in range(4):
                    a, f = n // 2, n % 2
                    last = mm(half(4 + c // 2, c % 2), spec[:, a, f, c * P:c * P + P], idft[:, a, f, :],
                              start=(n == 0), stop=(n == 3))
                last.then_inc(sem("z_mm"), 1)
            pe.wait_ge(sem("kupx_ready"), 4)
            pe.wait_ge(sem("z_read"), 8)
            for h in range(HEADS):
                if h:
                    pe.wait_ge(sem("state_ready"), 2 * h)
                    pe.wait_ge(sem("o_read"), 4 * h)
                for d, c, b, m in ((0, 0, 4, 0), (1, 3, 6, 1), (0, 1, 6, 0), (1, 2, 5, 0), (0, 2, 4, 1),
                                   (1, 1, 7, 0)):
                    t, r = c // 2, 64 * (c % 2)
                    last = mm(half(b, m), kupx[r:r + CHUNK, t, d, h * DK:h * DK + DK],
                              vx[r:r + CHUNK, t, h * DV:h * DV + DV], start=True, stop=True)
                    last.then_inc(sem("upd_mm"), 1)
                projection("og", hxx, units=[h])
                pe.wait_ge(sem("state_ready"), 2 * h + 2)
                for v in range(2):
                    dst = half(5 + 2 * v, 1)
                    vs = slice(v * P, v * P + P)
                    for t in range(TT):
                        for d in range(2):
                            mm(dst[:, t * P:t * P + P], vx[:, t, h * DV + v * P:h * DV + v * P + P],
                               att[:, h, (2 * t + d) * P:(2 * t + d) * P + P],
                               start=(t == 0 and d == 0), stop=False, skip_group_check=True)
                    for d in range(2):
                        for c in range(4):
                            if d == 0:
                                st = s0[:, h, 0, vs] if c == 0 else sst[h % 2][:, 0, c - 1, vs]
                            else:
                                st = s0[:, h, 1, vs] if c == 3 else sst[h % 2][:, 1, c, vs]
                            last = mm(dst[:, c * CHUNK:c * CHUNK + CHUNK], st,
                                      qd[:, d, h, c * CHUNK:c * CHUNK + CHUNK], start=False,
                                      stop=(d == 1 and c == 3), skip_group_check=True)
                    last.then_inc(sem("o_mm"), 1)
            ada(4, [("state_ready", 8), ("o_read", 16)])
            pe.wait_ge(sem("mod_ready"), 5)
            for h in range(HEADS):
                for v in range(2):
                    last = mm(half(4 + h // 2, h % 2), ones, sqo[:, 2 * h + v, :], start=(v == 0),
                              stop=(v == 1))
                if h % 2:
                    last.then_inc(sem("onorm_mm"), 1)
            projection("ma", hxx)
            ada(5, [("onorm_read", 2)])
            projection("mb", hxx)
            pe.wait_ge(sem("act_ready"), 1)
            projection("gla", act)
            pe.wait_ge(sem("z_ready"), 1)
            projection("hyo", uT)
            pe.wait_ge(sem("evac_hyo"), 4)
            projection("out", sma)
            pe.wait_ge(sem("mod_ready"), 6)
            mean_square(8, 4, T)
            pe.wait_ge(sem("wrt_loaded"), 32)
            pe.wait_ge(sem("hx2_ready"), KT)
            pe.wait_ge(sem("evac_out"), 4)
            for t in range(TT):
                dst = bank[5][:, t * E:t * E + E]
                mm(dst, ones[0:1, :], brt, start=True, stop=False)
                for k in range(KT):
                    last = mm(dst, hxx[:, k, t * P:t * P + P], wrt[:, k, :], start=False,
                              stop=(k == KT - 1))
            last.then_inc(sem("logit_mm"), 1)
            for t in range(TT):
                for k in range(KT):
                    last = pe.transpose(bank[2 * t + k // 4][:, (k % 4) * P:(k % 4) * P + P],
                                        hxx[:, k, t * P:t * P + P], ident)
                    if k % 4 == 3:
                        last.then_inc(sem("tok_turned"), 1)
            pe.wait_ge(sem("sel_ready"), 1)
            pe.wait_ge(sem("rms"), 2)
            cnt_ps, start_ps, n_ps, eid_ps = (bank[5][0:96, 64:65], bank[5][0:96, 66:67],
                                              bank[5][0:1, 68:69], bank[5][0:1, 128:192])
            for t in range(TT):
                last = mm(cnt_ps, sel[:, t, :], ones[:, 0:1], start=(t == 0), stop=(t == TT - 1))
            last.then_inc(sem("count_mm"), 1)
            for t in range(TT):
                pe.transpose(bank[6][0:32, t * P:t * P + P], sel[:, t, 0:E], ident)
                last = pe.transpose(bank[7][0:32, t * P:t * P + P], gate[:, t, :], ident)
            last.then_inc(sem("turned_sel"), 1)
            mm(bank[4][0:32, 0:P], sel[:, 0, 0:E], earlier, start=True, stop=True)
            mm(bank[4][0:32, P:T], sel[:, 0, 0:E], every, start=True, stop=False)
            mm(bank[4][0:32, P:T], sel[:, 1, 0:E], earlier, start=False,
               stop=True).then_inc(sem("place_mm"), 1)
            pe.wait_ge(sem("pass_ready"), 1)
            mm(start_ps, C("tri", p=E), cnt[0:E, 3:4], start=True, stop=True)
            mm(n_ps, cnt[0:E, 3:4], ones[0:E, 0:1], start=True, stop=True).then_inc(sem("start_mm"), 1)
            pe.wait_ge(sem("items_ready"), 1)
            mm(eid_ps, C("eid", p=E), T3[0:E, :], start=True, stop=True).then_inc(sem("eid_mm"), 1)
            for t in range(TT):
                mm(bank[4][:, 256 + t * MAXI:][:, 0:MAXI], posm[:, t * P:t * P + P], T3[0:E, :],
                   start=True, stop=False)
                mm(bank[4][:, 256 + t * MAXI:][:, 0:MAXI], ones[0:E, :], Q, start=False, stop=True)
                last = mm(bank[4][:, 384 + t * MAXI:][:, 0:MAXI], gateT[:, t * P:t * P + P], T3[0:E, :],
                          start=True, stop=True)
            last.then_inc(sem("itemcol_mm"), 1)
            pe.wait_ge(sem("itemcol_ready"), 1)
            pe.wait_ge(sem("bdn_loaded"), 16)
            for b in range(4):
                mm(bank[4 + b][:, :], zero[:, 0:P], zero, start=True, stop=False, skip_group_check=True)
                for m in range(2):
                    c = 2 * b + m
                    mm(half(4 + b, m), bdn[:, c * P:c * P + P], gateT, start=False, stop=False,
                       skip_group_check=True)

            def gather():
                for c in range(KT):
                    for t in range(TT):
                        last = mm(bank[3][:, c * SLOTS:c * SLOTS + SLOTS], tok[:, t, c * P:c * P + P],
                                  pick[:, t, 0:SLOTS], start=(t == 0), stop=(t == TT - 1))
                last.then_inc(sem("gathered"), 1)

            pe.wait_ge(sem("tok_ready"), 4)
            pe.wait_ge(sem("pick_ready"), 1)
            gather()
            pe.wait_ge(sem("bp_ready"), 1)
            pe.wait_ge(sem("list_ready"), 2)
            n = pe.value_load(nitems, min_val=E, max_val=48)
            with pe.Fori(0, n) as i:
                pe.wait_ge(sem("xe_ready"), i + 1)
                pe.wait_ge(sem("bsel_ready"), i + 1)
                pe.wait_ge(sem("aT_ready"), i + 1)
                pe.wait_ge(sem("back_ready"), i + 1)
                for b in range(2):
                    for gq in range(2):
                        mm(bank[b][64 * gq:64 * gq + 64, :], bsel,
                           bp[:, (2 * gq + b) * 512:(2 * gq + b) * 512 + 512], start=True, stop=False)
                for k in range(KT):
                    pe.wait_ge(sem(f"up_loaded{k}"), 16 * i + 16)
                    w = ring[:, (k + 4) % 8].rearrange("p k n -> p (k n)")
                    for b in range(2):
                        for gq in range(2):
                            last = mm(bank[b][64 * gq:64 * gq + 64, :], xe[:, k, :],
                                      w[:, (2 * gq + b) * 512:(2 * gq + b) * 512 + 512],
                                      start=False, stop=(k == KT - 1))
                    last.then_inc(sem("up_used"), 1)
                pe.wait_ge(sem("pick_ready"), i + 2)
                gather()
                pe.wait_ge(sem("a_ready"), i + 1)
                for b in range(4):
                    pe.transpose(bank[0][:, b * P:b * P + P], am[:, b * P:b * P + P], ident)
                pe.wait_ge(sem("spread_ready"), i + 1)
                for t in range(TT):
                    last = pe.transpose(bank[1][:, t * P:t * P + P], spread[:, t, :], ident)
                last.then_inc(sem("turned"), 1)
                pe.wait_ge(sem("aT_ready"), i + 2)
                for u in range(4):
                    pe.wait_ge(sem(f"down_loaded{u}"), 16 * i + 16)
                    for a in range(2):
                        kk = 2 * u + a
                        for gq in range(2):
                            last = mm(bank[2][64 * gq:64 * gq + 64, :], aT[:, kk % 4, kk // 4, :],
                                      down[:, u, a, gq * 512:gq * 512 + 512],
                                      start=(kk == 0), stop=(kk == 7))
                    last.then_inc(sem("down_used"), 1)
                pe.wait_ge(sem("y_ready"), i + 1)
                pe.wait_ge(sem("back_ready"), i + 2)
                for c in range(4):
                    for gq in range(2):
                        cc = 4 * gq + c
                        last = mm(half(4 + cc // 2, cc % 2), ysb[64 * gq:64 * gq + 64, c * P:c * P + P],
                                  back[64 * gq:64 * gq + 64, :], start=False, stop=False,
                                  skip_group_check=True)
                last.then_inc(sem("scattered"), 1)
            mean_square(16, 0, T)

        @block.scalar
        def _(ac):
            act_fn = ac.activation

            ac.dma_start(zsb, zt).then_inc(sem("hw_loaded"), 16)
            ac.dma_start(hwsb, hw).then_inc(sem("hw_loaded"), 16)
            ac.dma_start(vec[:, :], vecs).then_inc(sem("vec_loaded"), 16)
            for q in range(4):
                ac.dma_start(xT[:, 2 * q:2 * q + 2, :],
                             xt[2 * q:2 * q + 2].rearrange("k p t -> p k t")).then_inc(sem(f"x_loaded{q}"), 16)
            ac.dma_start(con[:, :], cons).then_inc(sem("con_loaded"), 16)
            ac.dma_start(w4, hw4).then_inc(sem("w4_loaded"), 16)
            ac.dma_start(win, window.rearrange("t p c -> p t c")).then_inc(sem("win_loaded"), 16)

            def squares(base, src, n):
                for k in range(KT):
                    if base == 0 and k % 2 == 0:
                        ac.wait_ge(sem(f"x_loaded{k // 2}"), 16)
                    if base + k >= 2:
                        ac.wait_ge(sem("sq_used"), base + k - 1)
                    act_fn(sq[:, k % 2, 0:n], src[:, k, :], ACT.Square).then_inc(sem("sq_ready"), 1)

            def root(base, b, n):
                ac.wait_ge(sem("sq_used"), base + KT)
                ac.wait_ge(sem("eps_ready"), 1)
                act_fn(rstd[:, 0:n], bank[b][:, 0:n], ACT.Sqrt, scale=1.0 / D,
                       bias=eps).then_inc(sem("rms"), 1)

            squares(0, xT, 512)
            ac.wait_ge(sem("mlp_arg"), 1)
            act_fn(hact[:, 3, :], hact[:, 2, :], ACT.Sin).then_inc(sem("mlp_sin"), 1)
            root(0, 5, 512)
            for n in range(1, 3):
                ac.wait_ge(sem("mlp_arg"), n + 1)
                act_fn(hact[:, 3, :], hact[:, 2, :], ACT.Sin).then_inc(sem("mlp_sin"), 1)
            ac.wait_ge(sem("vec_loaded"), 16)
            ac.wait_ge(sem("csil_zero"), 1)
            for r, name in enumerate(("c", "cctx")):
                at = VEC[name][0]
                act_fn(csil[:, :, 2 + r], vec[:, at:at + KT], ACT.Sigmoid).then_inc(sem("csig"), 1)
            for n in range(8):
                ac.wait_ge(sem("spec_mm"), n + 1)
                a, f, c = n // 4, (n % 4) // 2, n % 2
                act_fn(spec[:, a, f, c * 512:c * 512 + 512], bank[n][:, :],
                       ACT.Copy).then_inc(sem("spec_ready"), 1)

            def ada_rows(s):
                ac.wait_ge(sem("unit_done"), 4 * ROUNDS.index(f"ada{s}") + 4)
                act_fn(adar[:, :], half(4, 0), ACT.Copy).then_inc(sem("ada_rows"), 1)

            ada_rows(0)
            ada_rows(1)
            ac.dma_start(wrsb, wr).then_inc(sem("wr_loaded"), 16)
            ac.dma_start(wgksb, wgk).then_inc(sem("wgk_loaded"), 16)

            def unit_done(name, j):
                ac.wait_ge(sem("unit_done"), 4 * ROUNDS.index(name) + j + 1)

            for j in range(4):
                unit_done("qk", j)
                act_fn(qk[:, 2 * j:2 * j + 2, :].rearrange("p m t -> p (m t)"), bank[j][:, :], ACT.Copy,
                       scale=float(DK) ** -0.5 if j < 2 else 1.0).then_inc(sem("evac_qk"), 1)
            for j in range(4):
                unit_done("v", j)
                act_fn(vx[:, :, j * 256:j * 256 + 256], bank[j][:, :].rearrange("p (t c) -> p t c", t=TT),
                       ACT.Copy).then_inc(sem("evac_v"), 1)
            for n in range(8):
                ac.wait_ge(sem("gate_mm"), n + 1)
                if n >= 4:
                    ac.wait_ge(sem("g_ready"), n - 3)
                act_fn(tmp[:, n % 4, :], bank[(6, 7, 4, 5)[n % 4]][:, :],
                       ACT.Abs).then_inc(sem("gate_abs"), 1)
                ac.wait_ge(sem("gate_abs"), n + 1)
                act_fn(tmp[:, n % 4, :], tmp[:, n % 4, :], ACT.Exp, scale=-1.0).then_inc(sem("gate_exp"), 1)
                ac.wait_ge(sem("gate_exp"), n + 1)
                act_fn(tmp[:, n % 4, :], tmp[:, n % 4, :], ACT.Ln, bias=1.0).then_inc(sem("gate_ln"), 1)

            def conv_mid(name, base, dst):
                for j in range(4):
                    unit_done(name, j)
                    for m in range(2):
                        c = 2 * j + m
                        act_fn(dst[:, c, :], half(j, m), ACT.Identity, scale=V("cw", 24 + base + c),
                               bias=V("cb", base + c)).then_inc(sem("conv_mid"), 1)

            conv_mid("hv", 0, uT)
            ac.wait_ge(sem("spec_ready"), 8)
            for n in range(4):
                ac.wait_ge(sem("crest_mm"), n + 1)
                act_fn(kupc[:, n // 2, n % 2, :], bank[4 + n][:, :],
                       ACT.Exp).then_inc(sem("crest_read"), 1)
            ada_rows(2)
            conv_mid("hx1", 8, x1c)
            for h in range(HEADS):
                ac.wait_ge(sem("s0_mm"), h + 1)
                act_fn(s0[:, h].rearrange("p d v -> p (d v)"), bank[4 + h][:, :],
                       ACT.Copy).then_inc(sem("s0_ready"), 1)
            for n in range(4):
                ac.wait_ge(sem("decay_mm"), n + 1)
                d, h = n // 2, 2 * (n % 2)
                act_fn(qd[:, d, h:h + 2, :].rearrange("p h t -> p (h t)"), bank[4 + n][:, :],
                       ACT.Exp).then_inc(sem("exp_pos"), 1)
                act_fn(ki[:, d, h:h + 2, :].rearrange("p h t -> p (h t)"), bank[4 + n][:, :],
                       ACT.Exp, scale=-1.0).then_inc(sem("decay_read"), 1)
            ac.wait_ge(sem("kupc_ready"), 4)
            for t in range(TT):
                ac.wait_ge(sem("k_turned"), t + 1)
                act_fn(kcx[:, t, :], bank[4 + t][:, :], ACT.Copy).then_inc(sem("ktok_ready"), 1)
            ada_rows(3)
            for n in range(4):
                ac.wait_ge(sem("rest_mm"), n + 1)
                act_fn(kupx[:, n // 2, n % 2, :], bank[4 + n][:, :],
                       ACT.Exp).then_inc(sem("rest_read"), 1)
            ac.wait_ge(sem("qdki_ready"), 4)
            conv_mid("hx0", 16, x0T)
            ac.wait_ge(sem("u_ready"), 1)
            for b in range(4):
                ac.wait_ge(sem("u_turned"), b + 1)
                act_fn(utok[:, 2 * b:2 * b + 2, :], bank[4 + b][:, :].rearrange("p (c t) -> p c t", c=2),
                       ACT.Copy).then_inc(sem("utok_ready"), 1)
            ac.wait_ge(sem("z_mm"), 8)
            for h in range(HEADS):
                unit_done("og", h)
                act_fn(og[:, 2 * h:2 * h + 2, :].rearrange("p m t -> p (m t)"), bank[h][:, :],
                       ACT.Sigmoid).then_inc(sem("og_sig"), 1)
                for v in range(2):
                    ac.wait_ge(sem("o_mm"), 2 * h + v + 1)
                    act_fn(act[:, 2 * h + v, :], half(5 + 2 * v, 1), ACT.Copy).then_inc(sem("o_read"), 1)
                    act_fn(sqo[:, 2 * h + v, :], half(5 + 2 * v, 1), ACT.Square).then_inc(sem("o_read"), 1)
            ada_rows(4)
            for n in range(2):
                ac.wait_ge(sem("onorm_mm"), n + 1)
                act_fn(rso[:, 2 * n:2 * n + 2, :].rearrange("p h t -> p (h t)"), bank[4 + n][:, :],
                       ACT.Sqrt, scale=1.0 / DV, bias=eps).then_inc(sem("onorm_read"), 1)
            for name, dst in (("ma", sma), ("mb", smb)):
                if name == "mb":
                    ada_rows(5)
                for j in range(4):
                    unit_done(name, j)
                    act_fn(dst[:, 2 * j:2 * j + 2, :].rearrange("p m t -> p (m t)"), bank[j][:, :],
                           ACT.Sigmoid).then_inc(sem(f"evac_{name}"), 1)
            ac.wait_ge(sem("act_ready"), 1)
            for q in range(3):
                ac.dma_start(bupsb[32 * q:32 * q + 32, :], bup).then_inc(sem("bup_loaded"), 16)
            for k in range(KT):
                if k % 2 == 0:
                    ac.wait_ge(sem("evac_out"), k // 2 + 1)
                ac.wait_ge(sem("sq_used"), 8 + k - 1)
                act_fn(sq[:, k % 2, 0:T], xres[:, k, :], ACT.Square).then_inc(sem("sq_ready"), 1)
            ac.dma_start(wrt, wrouter).then_inc(sem("wrt_loaded"), 16)
            ac.dma_start(brt, brouter).then_inc(sem("wrt_loaded"), 16)
            ac.dma_start(bdn, bdown).then_inc(sem("bdn_loaded"), 16)
            root(8, 4, T)
            for b in range(4):
                ac.wait_ge(sem("tok_turned"), b + 1)
                act_fn(tok[:, b // 2, (b % 2) * 512:(b % 2) * 512 + 512], bank[b][:, :],
                       ACT.Copy).then_inc(sem("tok_ready"), 1)
            ac.wait_ge(sem("top_ready"), 2)
            for t in range(TT):
                act_fn(ew[:, t, :], m8[:, t, 0:4], ACT.Exp, bias=nm[:, t:t + 1],
                       accum_out=es[:, t:t + 1]).then_inc(sem("top_exp"), 1)
            ac.wait_ge(sem("list_ready"), 2)
            act_fn(back[:, 0:P], ident, ACT.Copy).then_inc(sem("back_ready"), 1)
            ac.wait_ge(sem("gathered"), 1)
            act_fn(xe.rearrange("p k s -> p (k s)"), bank[3][:, :], ACT.Copy).then_inc(sem("xe_ready"), 1)
            n = ac.value_load(nitems, min_val=E, max_val=48)
            with ac.Fori(0, n) as i:
                ac.wait_ge(sem("glu_ready"), i + 1)
                act_fn(sg, glu, ACT.Sigmoid, scale=ALPHA).then_inc(sem("sg_ready"), 1)
                ac.wait_ge(sem("gathered"), i + 2)
                act_fn(xe.rearrange("p k s -> p (k s)"), bank[3][:, :],
                       ACT.Copy).then_inc(sem("xe_ready"), 1)
                ac.wait_ge(sem("turned"), i + 1)
                act_fn(back, half(1, 0), ACT.Copy).then_inc(sem("back_ready"), 1)
                ac.wait_ge(sem("down_used"), 4 * i + 4)
                act_fn(ysb, bank[2][:, :], ACT.Copy).then_inc(sem("y_ready"), 1)
            for k in range(KT):
                ac.wait_ge(sem("x2_ready"), k + 1)
                ac.wait_ge(sem("sq_used"), 16 + k - 1)
                act_fn(sq[:, k % 2, 0:T], xres[:, k, :], ACT.Square).then_inc(sem("sq_ready"), 1)
            root(16, 0, T)

        @block.vector
        def _(ve):
            steps = [0]

            def link(ins):
                steps[0] += 1
                ins.then_inc(sem("vector_step"), 1)
                ve.wait_ge(sem("vector_step"), steps[0])

            def rows(ap):
                return ap.rearrange("p (r w) -> p r w", w=64)

            ve.memset(eps, EPS).then_inc(sem("eps_ready"), 1)
            ve.memset(csil[:, :, :], 0.0).then_inc(sem("csil_zero"), 1)
            ve.wait_ge(sem("vec_loaded"), 16)
            for n in range(3):
                ve.wait_ge(sem("mlp_mm"), n + 1)
                link(ve.tensor_scalar(hact[:, 0, :], bank[4][0:64, 0:256], V("hmlp", n, 64),
                                      V("hmlp", 3, 64), ALU.add, ALU.mult))
                link(ve.tensor_scalar(hact[:, 1, :], hact[:, 0, :], 1.0 / (2 * np.pi), MAGIC,
                                      ALU.mult, ALU.add))
                link(ve.tensor_scalar(hact[:, 1, :], hact[:, 1, :], MAGIC, None, ALU.subtract))
                link(ve.scalar_tensor_tensor(out=hact[:, 2, :], in0=hact[:, 1, :], scalar=-TWO_PI_HI,
                                             in1=hact[:, 0, :], op0=ALU.mult, op1=ALU.add))
                link(ve.scalar_tensor_tensor(out=hact[:, 2, :], in0=hact[:, 1, :], scalar=-TWO_PI_LO,
                                             in1=hact[:, 2, :], op0=ALU.mult, op1=ALU.add))
                ve.tensor_scalar(hact[:, 2, :], hact[:, 2, :], PI, -PI, ALU.min,
                                 ALU.max).then_inc(sem("mlp_arg"), 1)
                if n == 0:
                    ve.wait_ge(sem("rms"), 1)
                    ve.reciprocal(rstd[:, :], rstd[:, :]).then_inc(sem("rstd_ready"), 1)
            ve.wait_ge(sem("win_loaded"), 16)
            for t in range(TT):
                for c in range(2):
                    cs = slice(c * 512, c * 512 + 512)
                    ve.wait_ge(sem("taps_mm"), 4 * t + 2 + c + 1)
                    if 2 * t + c:
                        ve.wait_ge(sem("taps_ready"), 2 * t + c)
                    ve.tensor_tensor(hsum[:, t, cs], bank[4 * t + c][:, :], win[:, t, cs], ALU.mult)
                    link(ve.tensor_tensor(htmp, bank[4 * t + 2 + c][:, :], win[:, t, cs], ALU.mult))
                    if t == 0:
                        link(ve.memset(htmp[0:1, :], 0.0))
                    link(ve.tensor_tensor(hdif[:, t, cs], hsum[:, t, cs], htmp, ALU.subtract))
                    ve.tensor_tensor(hsum[:, t, cs], hsum[:, t, cs], htmp,
                                     ALU.add).then_inc(sem("taps_ready"), 1)
            ve.wait_ge(sem("csig"), 2)
            for r, name in enumerate(("c", "cctx")):
                at = VEC[name][0]
                link(ve.tensor_tensor(csil[:, :, r], csil[:, :, 2 + r], vec[:, at:at + KT], ALU.mult))
            ve.memset(csil[:, :, 2:4], 0.0).then_inc(sem("csil_ready"), 1)
            ve.wait_ge(sem("rstd_ready"), 1)
            for k in range(KT):
                ins = ve.scalar_tensor_tensor(out=hx[:, k, :], in0=xT[:, k, :], scalar=V("nm", k),
                                              in1=rstd[:, :], op0=ALU.mult, op1=ALU.mult)
            link(ins)

            def modulation(s):
                ve.wait_ge(sem("ada_turned"), s + 1)
                at = VEC["bada"][0] + s * KT
                bias = vec[:, at:at + KT].rearrange("p (g j) -> p j g", j=2)
                src = half(5, 0).rearrange("p (j g r) -> p j g r", j=2, g=4)
                for r in range(2):
                    dst = mod[:, s, :, r].rearrange("p (g j) -> p j g", j=2)
                    ins = ve.tensor_tensor(dst, src[:, :, :, r], bias, ALU.add)
                    if s in (1, 4):
                        link(ins)
                        ins = ve.tensor_scalar(mod[:, s, :, r], mod[:, s, :, r], 1.0, None, ALU.add)
                ins.then_inc(sem("mod_ready"), 1)

            modulation(0)
            modulation(1)
            ve.wait_ge(sem("mod_ready"), 2)
            for k in range(KT):
                for r, dst in enumerate((hxx, hxc)):
                    ve.tensor_scalar(dst[:, k, :], dst[:, k, :], mod[:, 1, k, r:r + 1],
                                     mod[:, 0, k, r:r + 1], ALU.mult, ALU.add).then_inc(sem("hx_ready"), 1)

            def unit_done(name, j):
                ve.wait_ge(sem("unit_done"), 4 * ROUNDS.index(name) + j + 1)

            for j in range(2, 4):
                unit_done("qk", j)
                ve.tensor_copy(kcx[:, :, (j - 2) * 256:(j - 2) * 256 + 256],
                               bank[4 + j][:, :].rearrange("p (t c) -> p t c", t=TT)).then_inc(sem("kc_ready"), 1)
            link(ve.memset(rT[:, :, :], 1.0))
            for d in range(2):
                ve.wait_ge(sem("low_mm"), d + 1)
                ve.tensor_copy(rT[0:16, d, :], bank[4 + d][0:16, :]).then_inc(sem("low_ready"), 1)
            for j in range(4):
                unit_done("v", j)
                ve.tensor_copy(vc[:, :, j * 256:j * 256 + 256],
                               bank[4 + j][:, :].rearrange("p (t c) -> p t c", t=TT)).then_inc(sem("evac_vc"), 1)

            def gate_end(n):
                t, d = n // 2, n % 2
                dst = (gx if t < 2 else gc)[:, t % 2, d, :]
                ve.wait_ge(sem("gate_ln"), n + 1)
                ve.scalar_tensor_tensor(out=dst, in0=bank[(6, 7, 4, 5)[n % 4]][:, :], scalar=0.0,
                                        in1=tmp[:, n % 4, :], op0=ALU.min,
                                        op1=ALU.subtract).then_inc(sem("g_ready"), 1)

            for n in range(8):
                gate_end(n)

            mids = [0]

            def conv_sides(name, base, dst):
                for j in range(4):
                    for tap, (a, b) in ((0, (1, 0)), (2, (0, 1))):
                        for m in range(2):
                            c = 2 * j + m
                            if tap == 0 and m == 0:
                                mids[0] += 2
                                ve.wait_ge(sem("conv_mid"), mids[0])
                            acc, src = rows(dst[:, c, :]), rows(half(j, m))
                            ins = ve.scalar_tensor_tensor(
                                out=acc[:, :, a:a + 63], in0=src[:, :, b:b + 63],
                                scalar=V("cw", 24 * tap + base + c), in1=acc[:, :, a:a + 63],
                                op0=ALU.mult, op1=ALU.add)
                        if tap == 0:
                            link(ins)
                    ins.then_inc(sem(f"evac_{name}"), 1)

            conv_sides("hv", 0, uT)
            for n in range(4):
                ve.wait_ge(sem("crest_read"), n + 1)
                ve.tensor_tensor(kupc[:, n // 2, n % 2, :], kupc[:, n // 2, n % 2, :], kcx[:, n // 2, :],
                                 ALU.mult).then_inc(sem("kupc_ready"), 1)
            modulation(2)
            conv_sides("hx1", 8, x1c)
            ve.wait_ge(sem("evac_hx1"), 4)
            ve.tensor_tensor(uT, uT, x1c, ALU.mult).then_inc(sem("u_ready"), 1)
            for n in range(4):
                ve.wait_ge(sem("exp_pos"), n + 1)
                ve.wait_ge(sem("decay_read"), n + 1)
                d, h = n // 2, 2 * (n % 2)
                at = 63 if d == 0 else 0
                link(ve.tensor_copy(
                    dec[:, d, h:h + 2, :],
                    qd[:, d, h:h + 2, :].rearrange("p h (c w) -> p h c w", w=CHUNK)[:, :, :, at]))
                ve.tensor_tensor(qd[:, d, h:h + 2, :], qd[:, d, h:h + 2, :], qk[:, h:h + 2, :], ALU.mult)
                ve.tensor_tensor(ki[:, d, h:h + 2, :], ki[:, d, h:h + 2, :], qk[:, 4 + h:6 + h, :],
                                 ALU.mult).then_inc(sem("qdki_ready"), 1)
            ve.wait_ge(sem("ktok_ready"), 2)
            modulation(3)
            for n in range(4):
                ve.wait_ge(sem("rest_read"), n + 1)
                ve.tensor_tensor(kupx[:, n // 2, n % 2, :], kupx[:, n // 2, n % 2, :], kcx[:, n // 2, :],
                                 ALU.mult).then_inc(sem("kupx_ready"), 1)
            conv_sides("hx0", 16, x0T)
            for f in range(2):
                for c in range(2):
                    cs = slice(c * 512, c * 512 + 512)
                    ve.wait_ge(sem("u_spec"), 2 * f + c + 1)
                    re, im = spec[:, 0, f, cs], spec[:, 1, f, cs]
                    ur, ui = bank[4 + c][:, :], bank[6 + c][:, :]
                    ve.tensor_tensor(tmp[:, 0, :], ur, re, ALU.mult)
                    ve.tensor_tensor(tmp[:, 1, :], ui, im, ALU.mult)
                    ve.tensor_tensor(tmp[:, 2, :], ui, re, ALU.mult)
                    link(ve.tensor_tensor(tmp[:, 3, :], ur, im, ALU.mult))
                    ve.tensor_tensor(re, tmp[:, 0, :], tmp[:, 1, :], ALU.subtract)
                    link(ve.tensor_tensor(im, tmp[:, 2, :], tmp[:, 3, :], ALU.add))
                    ve.engine_nop().then_inc(sem("prod_ready"), 1)
            link(ve.memset(region(14), 0.0))
            for h in range(HEADS):
                ve.wait_ge(sem("att_mm"), h + 1)
                ve.copy_predicated(att[:, h, :], C("mask").bitcast(U32),
                                   bank[4 + h][:, :]).then_inc(sem("att_ready"), 1)
            for c in range(KT):
                ve.wait_ge(sem("z_mm"), c - c % 2 + 2)
                ve.scalar_tensor_tensor(out=uT[:, c, :], in0=uT[:, c, :], scalar=V("hb", c),
                                        in1=half(4 + c // 2, c % 2), op0=ALU.mult,
                                        op1=ALU.add).then_inc(sem("z_read"), 1)
            ve.wait_ge(sem("z_read"), 8)
            ve.tensor_tensor(uT, uT, x0T, ALU.mult).then_inc(sem("z_ready"), 1)
            for h in range(HEADS):
                if h >= 2:
                    ve.wait_ge(sem("o_mm"), 2 * h - 2)
                st = sst[h % 2]
                upd = {(0, 0): half(4, 0), (1, 3): half(6, 1), (0, 1): half(6, 0), (1, 2): half(5, 0),
                       (0, 2): half(4, 1), (1, 1): half(7, 0)}
                for n in range(3):
                    ve.wait_ge(sem("upd_mm"), 6 * h + 6)
                    c = n
                    prev = s0[:, h, 0, :] if n == 0 else st[:, 0, n - 1, :]
                    a = ve.scalar_tensor_tensor(out=st[:, 0, n, :], in0=prev, scalar=dec[:, 0, h, c:c + 1],
                                                in1=upd[(0, c)], op0=ALU.mult, op1=ALU.add)
                    c = 3 - n
                    prev = s0[:, h, 1, :] if n == 0 else st[:, 1, c, :]
                    if n == 2:
                        a.then_inc(sem("state_ready"), 1)
                    b = ve.scalar_tensor_tensor(out=st[:, 1, c - 1, :], in0=prev,
                                                scalar=dec[:, 1, h, c:c + 1], in1=upd[(1, c)],
                                                op0=ALU.mult, op1=ALU.add)
                    if n == 2:
                        b.then_inc(sem("state_ready"), 1)
                    else:
                        link(b)
                ve.wait_ge(sem("og_sig"), h + 1)
                dst = og[:, 2 * h:2 * h + 2, :].rearrange("p m t -> p (m t)")
                ve.tensor_tensor(dst, dst, bank[h][:, :], ALU.mult).then_inc(sem("evac_og"), 1)
            modulation(4)
            for n in range(2):
                ve.wait_ge(sem("onorm_read"), n + 1)
                dst = rso[:, 2 * n:2 * n + 2, :]
                link(ve.reciprocal(dst, dst))
            for m in range(8):
                ins = ve.scalar_tensor_tensor(out=act[:, m, :], in0=act[:, m, :], scalar=V("gn", m % 2),
                                              in1=rso[:, m // 2, :], op0=ALU.mult, op1=ALU.mult)
            link(ins)
            ve.wait_ge(sem("evac_og"), 4)
            ve.tensor_tensor(act, act, og, ALU.mult).then_inc(sem("act_ready"), 1)
            modulation(5)
            for j in range(4):
                unit_done("gla", j)
                dst = sma[:, 2 * j:2 * j + 2, :].rearrange("p m t -> p (m t)")
                ve.tensor_tensor(dst, dst, bank[j][:, :], ALU.mult).then_inc(sem("evac_gla"), 1)
            for j in range(4):
                unit_done("hyo", j)
                dst = smb[:, 2 * j:2 * j + 2, :].rearrange("p m t -> p (m t)")
                link(ve.tensor_tensor(dst, dst, bank[j][:, :], ALU.mult))
                y = sma[:, 2 * j:2 * j + 2, :].rearrange("p m t -> p (m t)")
                ve.tensor_tensor(y, y, dst, ALU.add).then_inc(sem("evac_hyo"), 1)
            for j in range(4):
                unit_done("out", j)
                for m in range(2):
                    c = 2 * j + m
                    ins = ve.scalar_tensor_tensor(out=xres[:, c, :], in0=half(j, m),
                                                  scalar=mod[:, 2, c, 0:1], in1=xres[:, c, :],
                                                  op0=ALU.mult, op1=ALU.add)
                ins.then_inc(sem("evac_out"), 1)
            ve.wait_ge(sem("rms"), 2)
            link(ve.reciprocal(rstd[:, 0:T], rstd[:, 0:T]))
            for k in range(KT):
                ins = ve.scalar_tensor_tensor(out=hxx[:, k, :], in0=xres[:, k, :], scalar=V("nf", k),
                                              in1=rstd[:, 0:T], op0=ALU.mult, op1=ALU.mult)
            link(ins)
            for k in range(KT):
                ve.tensor_scalar(hxx[:, k, :], hxx[:, k, :], mod[:, 4, k, 0:1], mod[:, 3, k, 0:1],
                                 ALU.mult, ALU.add).then_inc(sem("hx2_ready"), 1)
            ve.wait_ge(sem("logit_mm"), 1)
            link(ve.tensor_copy(logit, bank[5][:, 0:TT * E].rearrange("p (t e) -> p t e", t=TT)))
            for t in range(TT):
                link(ve.max(m8[:, t, :], logit[:, t, :]))
                link(ve.max_index(i8[:, t, :], m8[:, t, :], logit[:, t, :]))
                ve.tensor_copy(if8[:, t, :], i8[:, t, :])
                ve.tensor_scalar(nm[:, t:t + 1], m8[:, t, 0:1], -1.0, None,
                                 ALU.mult).then_inc(sem("top_ready"), 1)
            ve.wait_ge(sem("top_exp"), 2)
            link(ve.reciprocal(es, es))
            experts = C("slot", 0, E)
            for t in range(TT):
                link(ve.tensor_scalar(ew[:, t, :], ew[:, t, :], es[:, t:t + 1], None, ALU.mult))
                for k in range(4):
                    ve.tensor_scalar(gk[:, t, k, :], experts, if8[:, t, k:k + 1], ew[:, t, k:k + 1],
                                     ALU.is_equal, ALU.mult)
                    ins = ve.tensor_scalar(sk[:, t, k, :], experts, if8[:, t, k:k + 1], None, ALU.is_equal)
                link(ins)
                ve.tensor_reduce(gate[:, t, :], gk[:, t].rearrange("p k e -> p e k"), AX_X, ALU.add)
                ve.tensor_reduce(sel[:, t, 0:E], sk[:, t].rearrange("p k e -> p e k"), AX_X, ALU.add)
                ve.tensor_reduce(sel[:, t, E:2 * E], sk[:, t].rearrange("p k e -> p e k"), AX_X, ALU.add)
                ins = ve.tensor_reduce(sel[:, t, 2 * E:3 * E], sk[:, t].rearrange("p k e -> p e k"),
                                       AX_X, ALU.add)
            ins.then_inc(sem("sel_ready"), 1)
            ve.wait_ge(sem("count_mm"), 1)
            link(ve.tensor_copy(cnt[:, 0:1], bank[5][0:96, 64:65]))
            link(ve.tensor_scalar(cnt[:, 1:2], cnt[:, 0:1], 1.0 * SLOTS, 1.0, ALU.is_gt, ALU.add))
            link(ve.scalar_tensor_tensor(out=cnt[:, 2:3], in0=cnt[:, 0:1], scalar=2.0 * SLOTS,
                                         in1=cnt[:, 1:2], op0=ALU.is_gt, op1=ALU.add))
            ve.scalar_tensor_tensor(out=cnt[:, 3:4], in0=cnt[:, 0:1], scalar=3.0 * SLOTS,
                                    in1=cnt[:, 2:3], op0=ALU.is_gt, op1=ALU.add).then_inc(sem("pass_ready"), 1)
            ve.wait_ge(sem("turned_sel"), 1)
            ve.tensor_copy(selT, bank[6][0:32, 0:T])
            ve.tensor_copy(gateT, bank[7][0:32, 0:T])
            ve.wait_ge(sem("place_mm"), 1)
            link(ve.tensor_scalar(posm, bank[4][0:32, 0:T], 16.0, FAR, ALU.mult, ALU.add))
            link(ve.tensor_tensor(posm, posm, selT, ALU.mult))
            link(ve.tensor_scalar(posm, posm, -FAR, None, ALU.add))
            ve.wait_ge(sem("start_mm"), 1)
            ve.tensor_copy(nitems, bank[5][0:1, 68:69]).then_inc(sem("list_ready"), 1)
            link(ve.tensor_copy(cnt[:, 4:5], bank[5][0:96, 66:67]))
            link(ve.tensor_tensor(cnt[:, 5:6], cnt[:, 4:5], cnt[:, 3:4], ALU.add))
            item = C("slot", 0, MAXI, p=96)
            link(ve.tensor_scalar(T3, item, cnt[:, 4:5], None, ALU.is_ge))
            link(ve.scalar_tensor_tensor(out=T3, in0=item, scalar=cnt[:, 5:6], in1=T3,
                                         op0=ALU.is_lt, op1=ALU.mult))
            link(ve.tensor_scalar(Q, item[0:E, :], cnt[0:E, 4:5], -1.0 * SLOTS, ALU.subtract, ALU.mult))
            ve.tensor_tensor(Q, Q, T3[0:E, :], ALU.mult).then_inc(sem("items_ready"), 1)
            ve.wait_ge(sem("eid_mm"), 1)
            ve.tensor_copy(eids, bank[5][0:1, 128:192]).then_inc(sem("list_ready"), 1)
            ve.memset(zero, 0.0)
            ve.wait_ge(sem("itemcol_mm"), 1)
            ve.tensor_copy(posI, bank[4][:, 256:384].rearrange("p (t i) -> p t i", t=TT))
            link(ve.tensor_copy(gateI, bank[4][:, 384:512].rearrange("p (t i) -> p t i", t=TT)))
            ve.engine_nop().then_inc(sem("itemcol_ready"), 1)

            slots = C("slot")

            def picks(i):
                for t in range(TT):
                    ins = ve.tensor_scalar(pick[:, t, :], slots, posI[:, t, bass.ds(i, 1)], None,
                                           ALU.is_equal)
                ins.then_inc(sem("pick_ready"), 1)

            def spreads(i):
                for t in range(TT):
                    ins = ve.tensor_scalar(spread[:, t, :], slots, posI[:, t, bass.ds(i, 1)],
                                           gateI[:, t, bass.ds(i, 1)], ALU.is_equal, ALU.mult)
                ins.then_inc(sem("spread_ready"), 1)

            def bias_select(i):
                ve.tensor_scalar(bsel, ones[0:96, 0:SLOTS], T3[:, bass.ds(i, 1)], None,
                                 ALU.mult).then_inc(sem("bsel_ready"), 1)

            picks(0)
            spreads(0)
            bias_select(0)
            ve.memset(aT, 0.0).then_inc(sem("aT_ready"), 1)
            ve.wait_ge(sem("list_ready"), 2)
            n = ve.value_load(nitems, min_val=E, max_val=48)
            with ve.Fori(0, n) as i:
                ve.wait_ge(sem("gathered"), i + 1)
                picks(i + 1)
                ve.wait_ge(sem("up_used"), 8 * i + 8)
                ve.tensor_scalar(glu, bank[0][:, :], LIMIT, None, ALU.min).then_inc(sem("glu_ready"), 1)
                ve.tensor_scalar(lin, bank[1][:, :], LIMIT, -LIMIT, ALU.min,
                                 ALU.max).then_inc(sem("lin_ready"), 1)
                bias_select(i + 1)
                ve.wait_ge(sem("glu_ready"), i + 1)
                ve.wait_ge(sem("lin_ready"), i + 1)
                ve.scalar_tensor_tensor(out=lin, in0=lin, scalar=1.0, in1=glu, op0=ALU.add,
                                        op1=ALU.mult).then_inc(sem("gated"), 1)
                ve.wait_ge(sem("gated"), i + 1)
                ve.wait_ge(sem("sg_ready"), i + 1)
                ve.tensor_tensor(am, lin, sg, ALU.mult).then_inc(sem("a_ready"), 1)
                ve.wait_ge(sem("turned"), i + 1)
                ve.tensor_copy(aT.rearrange("p b h s -> p (b h s)"), bank[0][:, :]).then_inc(sem("aT_ready"), 1)
                spreads(i + 1)
            ve.wait_ge(sem("scattered"), n)
            for c in range(KT):
                ve.scalar_tensor_tensor(out=xres[:, c, :], in0=half(4 + c // 2, c % 2),
                                        scalar=mod[:, 5, c, 0:1], in1=xres[:, c, :],
                                        op0=ALU.mult, op1=ALU.add).then_inc(sem("x2_ready"), 1)
            ve.wait_ge(sem("rms"), 3)
            link(ve.reciprocal(rstd[:, 0:T], rstd[:, 0:T]))
            for k in range(KT):
                ve.scalar_tensor_tensor(out=hxx[:, k, :], in0=xres[:, k, :], scalar=V("nfin", k),
                                        in1=rstd[:, 0:T], op0=ALU.mult,
                                        op1=ALU.mult).then_inc(sem("out_ready"), 1)

        @block.gpsimd
        def _(po):
            po.wait_ge(sem("bup_loaded"), 48)
            steps = 0
            for q in range(3):
                lo = slice(32 * q, 32 * q + 32)
                for r in range(q + 1):
                    steps += 1
                    po.tensor_copy(bp[lo, :], bupsb[lo, :]).then_inc(sem("pool_step"), 1)
                    po.wait_ge(sem("pool_step"), steps)
                    if r < q:
                        steps += 1
                        po.tensor_tensor(bupsb[lo, :], bupsb[lo, :], bp[lo, :],
                                         ALU.subtract).then_inc(sem("pool_step"), 1)
                        po.wait_ge(sem("pool_step"), steps)
            po.nop().then_inc(sem("bp_ready"), 1)


def shape_constants():
    c = np.zeros((P, NCON), np.float32)

    def put(name, a):
        at, width = CON[name]
        a = np.asarray(a, np.float64).reshape(len(a), width)
        c[:len(a), at:at + width] = a

    s, t = np.arange(P)[:, None], np.arange(P)[None]
    same = s // CHUNK == t // CHUNK
    put("ident", s == t)
    put("ones", np.ones((P, P)))
    upto, frm = (s <= t) & same, (s >= t) & same
    put("mask", np.concatenate([upto, frm, upto, frm], 1) / GNORM)
    put("rest", np.concatenate([(s > t) & same, (s < t) & same], 1) / GNORM)
    put("after", (s > t) / GNORM)
    put("before", (s < t) / GNORM)
    put("all16", np.ones((P, P)) / GNORM)
    n = np.arange(T)
    ang = np.pi * np.outer(n, 2 * n + 1) / (2 * T)
    fwd = np.stack([np.cos(ang), -np.sin(ang)])
    put("dft", fwd.reshape(2, TT, P, T).transpose(2, 0, 1, 3).reshape(P, -1))
    inv = np.stack([np.cos(ang).T, -np.sin(ang).T]) / T
    put("idft", inv.reshape(2, TT, P, T).transpose(2, 0, 1, 3).reshape(P, -1))
    put("slot", np.tile(np.arange(SLOTS), (P, 2)))
    put("tri", np.arange(E)[:, None] < np.arange(96)[None] % E)
    put("eid", np.arange(E)[:, None])
    pos = np.arange(T, dtype=np.float64)
    tn = (pos / (T - 1)).astype(np.float32)
    bands = (EMB - 1) // 2
    f = np.linspace(1e-4, bands - 1, bands).astype(np.float32)
    a = (np.float32(2 * np.pi / T) * pos.astype(np.float32)[:, None] * f[None]).astype(np.float32)
    z = np.concatenate([tn[:, None], np.cos(a, dtype=np.float64), -np.sin(a, dtype=np.float64)], 1)
    deltas = np.abs(np.linspace(np.log(1e-2) / 1.5, np.log(1e-2) / 0.3, D).astype(np.float32))
    w = np.exp(-tn[:, None].astype(np.float64) * deltas[None])
    return c, z.T.astype(np.float32), w.astype(np.float32).reshape(TT, P, D)


def kernel(**inputs):
    import concourse.bacc as bacc
    from concourse.bass_utils import run_bass_kernel_spmd

    a = {k: np.asarray(v) for k, v in inputs.items()}
    for k in a:
        if a[k].shape[0] == 1 and k not in ("x", "c", "ctx"):
            a[k] = a[k][0]
    con, z, window = shape_constants()
    vecs = np.zeros((P, NVEC), np.float32)

    def put(name, v, rows=P):
        at, width = VEC[name]
        vecs[:rows, at:at + width] = v

    def cols(v):
        return v.reshape(-1, P).T

    put("c", cols(a["c"][0]))
    put("cctx", cols(a["c_ctx"]))
    put("nm", cols(a["norm_mix"]))
    put("nf", cols(a["norm_ffn"]))
    put("nfin", cols(a["norm_final"]))
    put("bada", cols(a["b_ada"]))
    order = np.concatenate([np.arange(2 * D, 3 * D), np.arange(D, 2 * D), np.arange(D)])
    put("cw", np.concatenate([cols(a["hy_conv_w"][i][order]) for i in range(3)], 1))
    put("cb", cols(a["hy_conv_b"][order]))
    put("hb", cols(a["hy_bias"]))
    put("gn", cols(a["gla_norm"]))
    put("hmlp", np.stack([a["hy_f_b1"], a["hy_f_b2"], a["hy_f_b3"], a["hy_sin_freq"]], 1), ORDER)
    hw = np.zeros((ORDER, 192), np.float32)
    hw[:EMB, 0:64] = a["hy_f_w1"]
    hw[:, 64:128] = a["hy_f_w2"]
    hw[:, 128:192] = a["hy_f_w3"]
    w_in, w_ada = a["w_in"], a["w_ada"]
    blocks = {"qk": w_in[:, 0:1024], "v": w_in[:, 1024:2048], "og": w_in[:, 2048:3072],
              "hx0": w_in[:, 3104:4128], "hx1": w_in[:, 4128:5152], "hv": w_in[:, 5152:6176],
              "ma": w_in[:, 6176:7200], "mb": w_in[:, 7200:8224],
              "gla": a["w_gla_out"], "hyo": a["w_hy_out"], "out": a["w_out"]}
    for s in range(6):
        blocks[f"ada{s}"] = w_ada[:, s * D:s * D + D]
    wmix = np.stack([blocks[r].reshape(KT, P, 4, 256).transpose(2, 1, 0, 3).reshape(4, P, KT * 256)
                     for r in ROUNDS])
    xt = np.concatenate([a["x"][0], a["ctx"][0]], 0).T.reshape(KT, P, 2 * T)
    wgk = np.stack([np.concatenate([a["w_gk_f"], a["b_gk_f"][None]], 0),
                    np.concatenate([a["w_gk_b"], a["b_gk_b"][None]], 0)], 1)
    wup = a["w_up"].reshape(E, KT, P, 2, 512, 2).transpose(0, 1, 2, 3, 5, 4).reshape(E, KT, P, 2048)
    bup = a["b_up"].reshape(E, 2, 512, 2).transpose(0, 1, 3, 2).reshape(E, 2048)
    arrays = {
        "vecs": vecs, "cons": con, "xt": xt, "zt": z, "hw": hw, "hw4": a["hy_f_w4"], "window": window,
        "wmix": wmix, "wr": w_in[:, 3072:3104].reshape(KT, P, 32).transpose(1, 0, 2), "wgk": wgk,
        "wrouter": a["w_router"].reshape(KT, P, E).transpose(1, 0, 2), "brouter": a["b_router"][None],
        "wup": wup, "bup": bup, "wdown": a["w_down"].reshape(E, 4, 2, P, D), "bdown": a["b_down"],
    }
    nc = bacc.Bacc("TRN2", target_bir_lowering=False, num_devices=1)
    sent, args = {}, []
    for name, v in arrays.items():
        sent[f"in_{name}"] = np.ascontiguousarray(v)
        args.append(nc.dram_tensor(f"in_{name}", v.shape, F32, kind="ExternalInput").ap())
    args.append(nc.dram_tensor("out_t", (KT, P, T), F32, kind="ExternalOutput").ap())
    build_program(nc, *args)
    r = run_bass_kernel_spmd(nc, [sent], core_ids=[0])
    return np.ascontiguousarray(r.results[0]["out_t"].reshape(D, T).T)[None]
```

```python
from contextlib import ExitStack

import numpy as np

import concourse.bass as bass
from concourse import mybir

F32 = mybir.dt.float32
BF16 = mybir.dt.bfloat16
I32 = mybir.dt.int32
U32 = mybir.dt.uint32
ALU = mybir.AluOpType
ACT = mybir.ActivationFunctionType
AX_X = mybir.AxisListType.X

P = 128
D = 1024
T = 256
KT = D // P
TT = T // P
HEADS = 4
DK = 128
DV = 256
CHUNK = 64
GNORM = 16.0
EMB, ORDER = 33, 64
E = 32
SLOTS = 64
MAXI = 64
EPS = 1e-6
LIMIT, ALPHA = 7.0, 1.702
MAGIC = 12582912.0
PI = 3.141592
TWO_PI_HI = 6.28125
TWO_PI_LO = 2 * np.pi - 6.28125

ROUNDS = ["ada0", "ada1", "qk", "v", "hv", "ada2", "hx1", "ada3", "hx0", "ada4", "og", "ada5",
          "ma", "mb", "gla", "hyo", "out"]
MIDDLE = """
    gate0 gate1 hv0 gate2 gate3 hv1 gate4 gate5 hv2 gate6 gate7 hv3
    rows2 crest turn2 hx10 s0 hx11 decay hx12 kturn hx13 rows3 rest turn3
    hx00 uturn hx01 uspec0 hx02 uspec1 hx03 rows4 att turn4 inverse
    og0 update0 og1 output0 og2 update1 og3 rows5 output1 turn5
    ma0 update2 ma1 output2 ma2 update3 ma3 output3 mb0 onorm mb1 mb2 mb3
""".split()
PROJ = [r for r in ROUNDS if not r.startswith("ada")]
FAR = 1000.0


def columns(parts):
    at, where = 0, {}
    for name, width in parts:
        where[name] = (at, width)
        at += width
    return where, at


VEC, NVEC = columns([("c", 8), ("cctx", 8), ("nm", 8), ("nf", 8), ("nfin", 8), ("bada", 48),
                     ("cw", 72), ("cb", 24), ("hb", 8), ("gn", 2), ("hmlp", 4)])
CON, NCON = columns([("ident", 128), ("ones", 128), ("mask", 512), ("rest", 256), ("after", 128),
                     ("before", 128), ("all16", 128), ("slot", 128), ("tri", 96), ("eid", 1),
                     ("dft", 1024), ("idft", 1024)])
NCON1 = CON["dft"][0]



def build_program(nc, vecs, cons, xt, zt, hw, hw4, window, wmix, wr, wgk, wrouter, brouter,
                  wup, bup, wdown, bdown, out):
    with ExitStack() as ctx:
        made = {}

        def sem(name):
            if name not in made:
                made[name] = ctx.enter_context(nc.semaphore(name))
            return made[name]

        def sb(name, shape, dt=F32):
            return ctx.enter_context(nc.sbuf_tensor(name, shape, dt))

        ring = sb("ring", [P, 8, KT, 256])
        arena = sb("arena", [P, 15, 2048])
        con = sb("con", [P, NCON])
        vec = sb("vec", [P, NVEC])
        kcx = sb("kcx", [P, TT, 512])
        mod = sb("mod", [P, 6, KT, 2])
        rstd = sb("rstd", [P, 512])
        csil = sb("csil", [P, KT, 32])
        adar = sb("adar", [P, 256])
        dec = sb("dec", [P, 2, HEADS, 4])
        eps = sb("eps", [P, 1])[:, :]
        bank = [ctx.enter_context(nc.psum_tensor(f"bank{i}", [P, 512], F32)) for i in range(8)]

        def C(name, a=0, b=None, p=P):
            at, width = CON[name]
            return con[0:p, at + a:at + (width if b is None else b)]

        def V(name, i, p=P):
            return vec[0:p, VEC[name][0] + i:VEC[name][0] + i + 1]

        def region(r, n=1):
            return arena[:, r:r + n, :].rearrange("p r n -> p (r n)")

        def half(b, h):
            return bank[b][:, h * 256:h * 256 + 256]

        ident, ones = C("ident"), C("ones")
        dft = C("dft").rearrange("p (a s f) -> p a s f", a=2, s=TT)
        idft = C("idft").rearrange("p (a s f) -> p a s f", a=2, s=TT)

        xT = region(0, 2).rearrange("p (k t) -> p k t", k=KT)
        xres, xctx = xT[:, :, 0:T], xT[:, :, T:2 * T]
        x1c = utok = act = xctx
        hx = region(2, 2).rearrange("p (k t) -> p k t", k=KT)
        hxx, hxc = hx[:, :, 0:T], hx[:, :, T:2 * T]
        uT = hxc
        spec = region(4, 2).rearrange("p (a f c) -> p a f c", a=2, f=TT)
        og = region(4).rearrange("p (m t) -> p m t", m=8)
        sma = region(5).rearrange("p (m t) -> p m t", m=8)
        qk = region(6).rearrange("p (m t) -> p m t", m=8)
        x0T = qk
        tok = region(6).rearrange("p (t c) -> p t c", t=TT)
        vx = region(7).rearrange("p (t c) -> p t c", t=TT)
        smb = region(7).rearrange("p (m t) -> p m t", m=8)
        vc = region(8).rearrange("p (t c) -> p t c", t=TT)
        sst = [region(r)[:, 0:1536].rearrange("p (d c v) -> p d c v", d=2, c=3) for r in (8, 10)]
        gc = region(9).rearrange("p (t d c) -> p t d c", t=TT, d=2)
        gx = region(10).rearrange("p (t d c) -> p t d c", t=TT, d=2)
        s0 = region(9).rearrange("p (h d v) -> p h d v", h=HEADS, d=2)
        win = region(11).rearrange("p (t c) -> p t c", t=TT)
        hsum = region(12).rearrange("p (t c) -> p t c", t=TT)
        hdif = region(13).rearrange("p (t c) -> p t c", t=TT)
        w4 = region(14)[0:64, :]
        kupc = region(11).rearrange("p (t d c) -> p t d c", t=TT, d=2)
        kupx = region(13).rearrange("p (t d c) -> p t d c", t=TT, d=2)
        qd = region(11).rearrange("p (d h t) -> p d h t", d=2, h=HEADS)
        ki = region(12).rearrange("p (d h t) -> p d h t", d=2, h=HEADS)
        sqo = region(12).rearrange("p (m t) -> p m t", m=8)
        rso = region(11)[:, 0:1024].rearrange("p (h t) -> p h t", h=HEADS)
        att = region(14).rearrange("p (h n) -> p h n", h=HEADS)
        tmp = region(14).rearrange("p (n c) -> p n c", n=4)
        zsb = region(7)[0:EMB, 0:256]
        hwsb = region(7)[0:64, 256:448]
        hact = region(7)[0:64, 512:1536].rearrange("p (n t) -> p n t", n=4)
        sq = region(8)[:, 0:1024].rearrange("p (n t) -> p n t", n=2)
        htmp = region(6).rearrange("p (n a c) -> p n a c", n=2, a=2)
        wrsb = region(12)[:, 0:256].rearrange("p (k n) -> p k n", k=KT)
        rT = region(12)[0:33, 256:768]
        wgksb = region(13)[0:33, 0:1024].rearrange("p (d n) -> p d n", d=2)
        down = arena[:, 11:15, :].rearrange("p u (a n) -> p u a n", a=2)
        glu, sg, lin, am = (region(8)[:, a:a + 512] for a in (0, 512, 1024, 1536))
        aT = region(9)[:, 0:512].rearrange("p (b h s) -> p b h s", b=4, h=2)
        ysb = region(9)[:, 512:1024]
        xe = region(9)[:, 1024:1536].rearrange("p (k s) -> p k s", k=KT)
        pick = region(9)[:, 1536:1792].rearrange("p (t s) -> p t s", t=TT)
        spread = region(9)[:, 1792:2048].rearrange("p (t s) -> p t s", t=TT)
        back = region(10)[:, 0:256]
        posI = region(10)[:, 256:384].rearrange("p (t i) -> p t i", t=TT)
        gateI = region(10)[:, 384:512].rearrange("p (t i) -> p t i", t=TT)
        T3 = region(10)[0:96, 512:576]
        Q = region(10)[0:32, 576:640]
        eids = region(10)[0:1, 640:704].bitcast(I32)
        nitems = region(10)[0:1, 704:705].bitcast(I32)
        lasts = region(10)[0:1, 736:768].bitcast(I32)
        bsel = region(10)[0:96, 768:800].bitcast(BF16)
        bp = region(10)[0:96, 1024:2048].bitcast(BF16)
        bupsb = region(4)[0:96, :]
        R3 = region(5)
        wrt = R3[:, 0:256].rearrange("p (k e) -> p k e", k=KT)
        brt = R3[0:1, 256:288]
        logit = R3[:, 288:352].rearrange("p (t e) -> p t e", t=TT)
        m8 = R3[:, 352:368].rearrange("p (t e) -> p t e", t=TT)
        i8 = R3[:, 368:384].bitcast(U32).rearrange("p (t e) -> p t e", t=TT)
        if8 = R3[:, 384:400].rearrange("p (t e) -> p t e", t=TT)
        nm = R3[:, 400:402]
        ew = R3[:, 402:410].rearrange("p (t e) -> p t e", t=TT)
        es = R3[:, 410:412]
        gk = R3[:, 448:704].rearrange("p (t k e) -> p t k e", t=TT, k=4)
        sk = R3[:, 704:960].rearrange("p (t k e) -> p t k e", t=TT, k=4)
        sel = R3[:, 960:1152].rearrange("p (t e) -> p t e", t=TT)
        gate_ = R3[:, 1152:1216].rearrange("p (t e) -> p t e", t=TT)
        cnt = R3[0:96, 1216:1224]
        posm = R3[0:32, 1280:1536]
        selT = R3[0:32, 1536:1792]
        gateT = R3[0:32, 1792:2048]
        bdn = region(7)[0:32, 0:1024]
        zero = region(7)[0:32, 1024:1280].bitcast(BF16)

        block = ctx.enter_context(nc.Block())

        def run_middle(steps, unit):
            for step in MIDDLE:
                if step[:-1] in PROJ:
                    unit(step[:-1], int(step[-1]))
                elif step in steps:
                    steps[step]()
                elif step[:-1] in steps:
                    steps[step[:-1]](int(step[-1]))


        @block.sync
        def _(sp):
            def unit(i, r, j, first):
                slot = 4 * r + j
                if not first:
                    sp.wait_ge(sem("unit_done"), 4 * i + 4 * r + j - 7)
                if isinstance(i, int):
                    src = wmix[i + r, j]
                else:
                    src = wmix[bass.ds(i + r, 1), j].rearrange("a p n -> (a p) n")
                sp.dma_start(ring[:, slot].rearrange("p k n -> p (k n)"),
                             src).then_inc(sem(f"ring_loaded{slot}"), 16)

            sp.dma_start(zsb, zt).then_inc(sem("z_loaded"), 16)
            sp.dma_start(hwsb, hw).then_inc(sem("hw_loaded"), 16)
            sp.dma_start(vec[:, :], vecs).then_inc(sem("vec_loaded"), 16)
            sp.dma_start(con[:, 0:NCON1], cons[:, 0:NCON1]).then_inc(sem("con_loaded"), 16)
            for q in range(4):
                sp.dma_start(xT[:, 2 * q:2 * q + 2, :],
                             xt[2 * q:2 * q + 2].rearrange("k p t -> p k t")).then_inc(sem(f"x_loaded{q}"), 16)
            sp.dma_start(w4, hw4).then_inc(sem("w4_loaded"), 16)
            sp.dma_start(win, window.rearrange("t p c -> p t c")).then_inc(sem("win_loaded"), 16)
            sp.dma_start(con[:, NCON1:], cons[:, NCON1:]).then_inc(sem("dft_loaded"), 16)
            for r in range(2):
                for j in range(4):
                    unit(0, r, j, True)
            with sp.Fori(2, 16, 2) as i:
                for r in range(2):
                    for j in range(4):
                        unit(i, r, j, False)
            for j in range(4):
                unit(16, 0, j, False)

            def up_chunk(src, k):
                slot = (k + 4) % 8
                sp.dma_start(ring[:, slot].rearrange("p k n -> p (k n)"),
                             src).then_inc(sem(f"up_loaded{k}"), 16)

            def down_chunk(src, u):
                sp.dma_start(down[:, u], src).then_inc(sem(f"down_loaded{u}"), 16)

            for k in range(4):
                sp.wait_ge(sem("unit_done"), 4 * 15 + k + 1)
                up_chunk(wup[0, k], k)
            for k in range(4, 8):
                sp.wait_ge(sem("unit_done"), 4 * 16 + k - 3)
                up_chunk(wup[0, k], k)
            sp.wait_ge(sem("act_ready"), 1)
            for u in range(4):
                down_chunk(wdown[0, u].rearrange("a p n -> p a n"), u)
            sp.wait_ge(sem("list_ready"), 3)
            with sp.Fori(1, E) as e:
                last = sp.value_load(lasts[0:1, bass.ds(e - 1, 1)], min_val=0, max_val=47)
                for k in range(8):
                    sp.wait_ge(sem("up_used"), 8 * last + (k + 1))
                    up_chunk(wup[bass.ds(e, 1), k].rearrange("a p n -> (a p) n"), k)
                for u in range(4):
                    sp.wait_ge(sem("down_used"), 4 * last + (u + 1))
                    down_chunk(wdown[bass.ds(e, 1), u].rearrange("e a p n -> p (e a) n"), u)
            for k in range(KT):
                sp.wait_ge(sem("out_ready"), k + 1)
                sp.dma_start(out[k], hxx[:, k, :]).then_inc(sem("stored"), 16)
            sp.wait_ge(sem("stored"), 16 * KT)

        @block.tensor
        def _(pe):
            mm = pe.matmul

            def loaded(i, j):
                slot = 4 * (i % 2) + j
                pe.wait_ge(sem(f"ring_loaded{slot}"), 16 * (i // 2 + 1))
                return ring[:, slot]

            def projection(name, rhs, units=range(4), tokens=None):
                i = ROUNDS.index(name)
                before = PROJ[PROJ.index(name) - 1] if name != PROJ[0] else None
                for j in units:
                    w = loaded(i, j)
                    if ROUNDS[i - 1].startswith("ada") and j < 2:
                        pe.wait_ge(sem(("ada_rows", "mod_ready")[j]), int(ROUNDS[i - 1][3:]) + 1)
                    if before:
                        pe.wait_ge(sem(f"evac_{before}"), j + 1)
                    for m in range(2):
                        for k in range(KT):
                            last = mm(half(j, m), w[:, k, m * P:m * P + P], rhs[:, k, :],
                                      start=(k == 0), stop=(k == KT - 1))
                    if tokens and j >= 2:
                        pe.wait_ge(sem("hx_ready"), 2 * KT)
                        last = by_token(w, hxc, 4 + j)
                    last.then_inc(sem("unit_done"), 1)

            def by_token(w, lhs, b):
                for t in range(TT):
                    for k in range(KT):
                        last = mm(half(b, t), lhs[:, k, t * P:t * P + P], w[:, k, :],
                                  start=(k == 0), stop=(k == KT - 1))
                return last

            def mean_square(base, b, n):
                for k in range(KT):
                    pe.wait_ge(sem("sq_ready"), base + k + 1)
                    mm(bank[b][:, 0:n], ones, sq[:, k % 2, 0:n], start=(k == 0),
                       stop=(k == KT - 1)).then_inc(sem("sq_used"), 1)

            def rows(s):
                i = ROUNDS.index(f"ada{s}")
                w = [loaded(i, j) for j in range(4)]
                if s >= 2:
                    pe.wait_ge(sem(f"evac_{ROUNDS[i - 1]}"), 1)
                for k in range(KT):
                    for j in range(4):
                        last = mm(bank[0][32 * j:32 * j + 32, 0:256], csil[:, k, :], w[j][:, k, :],
                                  start=(k == 0), stop=(k == KT - 1))
                        if k == KT - 1:
                            last.then_inc(sem("unit_done"), 1)

            def turn(s):
                if s >= 2:
                    pe.wait_ge(sem(f"evac_{ROUNDS[ROUNDS.index(f'ada{s}') - 1]}"), 2)
                pe.wait_ge(sem("ada_rows"), s + 1)
                for j in range(2):
                    last = pe.transpose(bank[1][:, j * P:j * P + P], adar[:, j * P:j * P + P], ident)
                last.then_inc(sem("ada_turned"), 1)

            pe.wait_ge(sem("z_loaded"), 16)
            pe.wait_ge(sem("hw_loaded"), 16)
            mm(bank[4][0:64, 0:256], hwsb[0:EMB, 0:64], zsb, start=True,
               stop=True).then_inc(sem("mlp_mm"), 1)
            pe.wait_ge(sem("con_loaded"), 16)
            for n in range(2):
                pe.wait_ge(sem("mlp_sin"), n + 1)
                mm(bank[4][0:64, 0:256], hwsb[:, 64 + 64 * n:128 + 64 * n], hact[:, 3, :], start=True,
                   stop=True).then_inc(sem("mlp_mm"), 1)
                if n == 0:
                    mean_square(0, 5, 512)
            pe.wait_ge(sem("mlp_sin"), 3)
            pe.wait_ge(sem("w4_loaded"), 16)
            pe.wait_ge(sem("rms"), 1)
            for n in range(8):
                t, c = n // 4, (n % 4) // 2 + 2 * (n % 2)
                mm(bank[4 * t + c][:, :], hact[:, 3, t * P:t * P + P], w4[:, c * 512:c * 512 + 512],
                   start=True, stop=True).then_inc(sem("taps_mm"), 1)
            pe.wait_ge(sem("dft_loaded"), 16)
            for a, taps in ((0, hsum), (1, hdif)):
                pe.wait_ge(sem(("taps_sum", "taps_dif")[a]), 4)
                for n in range(4):
                    f, c = n // 2, n % 2
                    for s in range(TT):
                        last = mm(bank[4 * a + n][:, :], dft[:, a, s, f * P:f * P + P],
                                  taps[:, s, c * 512:c * 512 + 512], start=(s == 0), stop=(s == TT - 1))
                    last.then_inc(sem("spec_mm"), 1)
            pe.wait_ge(sem("csil_ready"), 1)
            pe.wait_ge(sem("spec_ready"), 2)
            rows(0)
            turn(0)
            pe.wait_ge(sem("mod_ready"), 1)
            rows(1)
            turn(1)

            pe.wait_ge(sem("spec_ready"), 8)
            pe.wait_ge(sem("hx_ready"), KT)
            projection("qk", hxx, tokens=True)
            pe.wait_ge(sem("wr_loaded"), 16)
            for k in range(KT):
                last = mm(bank[4][0:32, :], wrsb[:, k, :], hx[:, k, :], start=(k == 0),
                          stop=(k == KT - 1))
            last.then_inc(sem("low_mm"), 1)
            i = ROUNDS.index("v")
            for j in range(4):
                w = loaded(i, j)
                pe.wait_ge(sem("evac_qk"), j + 1)
                by_token(w, hxx, j)
                if j == 0:
                    pe.wait_ge(sem("low_ready"), 2)
                elif j >= 2:
                    pe.wait_ge(sem("kc_ready"), j - 1)
                by_token(w, hxc, 4 + j).then_inc(sem("unit_done"), 1)
            after, earlier, every = C("after"), C("before"), C("all16")

            def gate(n):
                t, d = n // 2, n % 2
                if n == 0:
                    pe.wait_ge(sem("wgk_loaded"), 16)
                pe.wait_ge(sem("evac_vc" if n < 4 else "g_ready"), n % 4 + 1)
                mm(bank[4 + n % 4][:, :], rT[:, t * P:t * P + P], wgksb[:, d, :], start=True,
                   stop=True).then_inc(sem("gate_mm"), 1)

            def crest():
                pe.wait_ge(sem("g_ready"), 8)
                for n, terms in enumerate(([(after, 0), (every, 1)], [(earlier, 0)],
                                           [(after, 1)], [(every, 0), (earlier, 1)])):
                    for m, (tri, s) in enumerate(terms):
                        last = mm(bank[4 + n][:, :], tri, gc[:, s, n % 2, :], start=(m == 0),
                                  stop=(m == len(terms) - 1))
                    last.then_inc(sem("crest_mm"), 1)

            def initial():
                pe.wait_ge(sem("kupc_ready"), 4)
                for h in range(HEADS):
                    for d in range(2):
                        for t in range(TT):
                            last = mm(half(4 + h, d), kupc[:, t, d, h * DK:h * DK + DK],
                                      vc[:, t, h * DV:h * DV + DV], start=(t == 0), stop=(t == TT - 1))
                    last.then_inc(sem("s0_mm"), 1)

            def decay():
                for d in range(2):
                    for h in range(HEADS):
                        n = d * HEADS + h
                        if n % 2 == 0:
                            pe.wait_ge(sem("s0_ready"), n // 2 + 1)
                        for t in range(TT):
                            last = mm(half(4 + n // 2, n % 2)[:, t * P:t * P + P],
                                      gx[:, t, d, h * DK:h * DK + DK],
                                      C("mask", d * P, d * P + P), start=True, stop=True)
                        if n % 2:
                            last.then_inc(sem("decay_mm"), 1)

            def kturn():
                for t in range(TT):
                    pe.wait_ge(sem("decay_read"), t + 1)
                    for h in range(HEADS):
                        last = pe.transpose(bank[4 + t][:, h * P:h * P + P],
                                            qk[:, 4 + h, t * P:t * P + P], ident)
                    last.then_inc(sem("k_turned"), 1)

            def rest():
                for n in (2, 3, 0, 1):
                    t, d = n // 2, n % 2
                    if n < 2:
                        pe.wait_ge(sem("ktok_ready"), n + 1)
                    else:
                        pe.wait_ge(sem("decay_read"), n + 1)
                    mm(bank[4 + n][:, :], C("rest", d * P, d * P + P), gx[:, t, d, :], start=True,
                       stop=True).then_inc(sem("rest_mm"), 1)

            def uturn():
                pe.wait_ge(sem("u_ready"), 1)
                pe.wait_ge(sem("rest_read"), 4)
                for b in range(4):
                    for c in range(2 * b, 2 * b + 2):
                        for t in range(TT):
                            last = pe.transpose(bank[4 + b][:, (c % 2) * 256 + t * P:][:, 0:P],
                                                uT[:, c, t * P:t * P + P], ident)
                    last.then_inc(sem("u_turned"), 1)

            def uspec(f):
                pe.wait_ge(sem("utok_ready"), 4)
                for c in range(2):
                    if f:
                        pe.wait_ge(sem("prod_ready"), 2 * c + 2)
                    for a in range(2):
                        for s in range(TT):
                            last = mm(bank[4 + 2 * a + c][:, :], dft[:, a, s, f * P:f * P + P],
                                      utok[:, 4 * c:4 * c + 4, s * P:s * P + P],
                                      start=(s == 0), stop=(s == TT - 1))
                    last.then_inc(sem("u_spec"), 1)

            def scores():
                pe.wait_ge(sem("qdki_ready"), 4)
                pe.wait_ge(sem("prod_ready"), 8)
                for h in range(HEADS):
                    for t in range(TT):
                        for d in range(2):
                            last = mm(bank[4 + h][:, (2 * t + d) * P:(2 * t + d) * P + P],
                                      ki[:, d, h, t * P:t * P + P], qd[:, d, h, t * P:t * P + P],
                                      start=True, stop=True)
                    last.then_inc(sem("att_mm"), 1)

            def inverse():
                for c in range(KT):
                    if c % 2 == 0:
                        pe.wait_ge(sem("att_ready"), c // 2 + 1)
                    for n in range(4):
                        a, f = n // 2, n % 2
                        last = mm(half(4 + c // 2, c % 2), spec[:, a, f, c * P:c * P + P],
                                  idft[:, a, f, :], start=(n == 0), stop=(n == 3))
                    last.then_inc(sem("z_mm"), 1)

            def update(h):
                if h:
                    pe.wait_ge(sem("state_ready"), 2 * h)
                    pe.wait_ge(sem("o_read"), 4 * h)
                else:
                    pe.wait_ge(sem("kupx_ready"), 4)
                    pe.wait_ge(sem("z_read"), 8)
                for d, c, b, m in ((0, 0, 4, 0), (1, 3, 6, 1), (0, 1, 6, 0), (1, 2, 5, 0),
                                   (0, 2, 4, 1), (1, 1, 7, 0)):
                    t, r = c // 2, 64 * (c % 2)
                    mm(half(b, m), kupx[r:r + CHUNK, t, d, h * DK:h * DK + DK],
                       vx[r:r + CHUNK, t, h * DV:h * DV + DV], start=True,
                       stop=True).then_inc(sem("upd_mm"), 1)

            def output(h):
                pe.wait_ge(sem("state_ready"), 2 * h + 2)
                for v in range(2):
                    dst = half(5 + 2 * v, 1)
                    vs = slice(v * P, v * P + P)
                    for t in range(TT):
                        for d in range(2):
                            mm(dst[:, t * P:t * P + P], vx[:, t, h * DV + v * P:h * DV + v * P + P],
                               att[:, h, (2 * t + d) * P:(2 * t + d) * P + P],
                               start=(t == 0 and d == 0), stop=False, skip_group_check=True)
                    for d in range(2):
                        for c in range(4):
                            if d == 0:
                                st = s0[:, h, 0, vs] if c == 0 else sst[h % 2][:, 0, c - 1, vs]
                            else:
                                st = s0[:, h, 1, vs] if c == 3 else sst[h % 2][:, 1, c, vs]
                            last = mm(dst[:, c * CHUNK:c * CHUNK + CHUNK], st,
                                      qd[:, d, h, c * CHUNK:c * CHUNK + CHUNK], start=False,
                                      stop=(d == 1 and c == 3), skip_group_check=True)
                    last.then_inc(sem("o_mm"), 1)

            def onorm():
                pe.wait_ge(sem("o_read"), 16)
                for h in range(HEADS):
                    for v in range(2):
                        last = mm(half(4 + h // 2, h % 2), ones, sqo[:, 2 * h + v, :], start=(v == 0),
                                  stop=(v == 1))
                    if h % 2:
                        last.then_inc(sem("onorm_mm"), 1)

            run_middle(dict(gate=gate, crest=crest, s0=initial, decay=decay, kturn=kturn, rest=rest,
                            uturn=uturn, uspec=uspec, att=scores, inverse=inverse, update=update,
                            output=output, onorm=onorm, rows=rows, turn=turn),
                       lambda name, j: projection(name, hxx, units=[j]))
            pe.wait_ge(sem("act_ready"), 1)
            projection("gla", act)
            pe.wait_ge(sem("z_ready"), 1)
            projection("hyo", uT)
            pe.wait_ge(sem("evac_hyo"), 4)
            projection("out", sma)
            pe.wait_ge(sem("evac_out"), 1)
            mean_square(8, 0, T)
            pe.wait_ge(sem("wrt_loaded"), 16)
            pe.wait_ge(sem("brt_loaded"), 16)
            pe.wait_ge(sem("evac_out"), 4)
            for t in range(TT):
                dst = bank[1][:, t * E:t * E + E]
                mm(dst, ones[0:1, :], brt, start=True, stop=False)
                for k in range(KT):
                    pe.wait_ge(sem("hx2_ready"), k + 1)
                    last = mm(dst, hxx[:, k, t * P:t * P + P], wrt[:, k, :], start=False,
                              stop=(k == KT - 1))
            last.then_inc(sem("logit_mm"), 1)
            pe.wait_ge(sem("onorm_read"), 2)
            for t in range(TT):
                for k in range(KT):
                    last = pe.transpose(bank[4 + 2 * t + k // 4][:, (k % 4) * P:(k % 4) * P + P],
                                        hxx[:, k, t * P:t * P + P], ident)
                    if k % 4 == 3:
                        last.then_inc(sem("tok_turned"), 1)
            pe.wait_ge(sem("zero_ready"), 1)
            for b in range(4):
                pe.wait_ge(sem("tok_ready"), b + 1)
                mm(bank[4 + b][:, :], zero[:, 0:P], zero, start=True, stop=False, skip_group_check=True)
            pe.wait_ge(sem("sel_ready"), 1)
            cnt_ps, start_ps, n_ps, ends_ps, eid_ps = (
                bank[1][0:96, 64:65], bank[1][0:96, 66:67], bank[1][0:1, 68:69], bank[1][0:1, 96:128],
                bank[1][0:1, 128:192])
            for t in range(TT):
                last = mm(cnt_ps, sel[:, t, :], ones[:, 0:1], start=(t == 0), stop=(t == TT - 1))
            last.then_inc(sem("count_mm"), 1)
            for t in range(TT):
                last = pe.transpose(bank[2][0:32, t * P:t * P + P], sel[:, t, 0:E], ident)
            last.then_inc(sem("turned_sel"), 1)
            pe.wait_ge(sem("rms"), 2)
            mm(bank[0][0:32, 0:P], sel[:, 0, 0:E], earlier, start=True, stop=True)
            mm(bank[0][0:32, P:T], sel[:, 0, 0:E], every, start=True, stop=False)
            mm(bank[0][0:32, P:T], sel[:, 1, 0:E], earlier, start=False,
               stop=True).then_inc(sem("place_mm"), 1)
            pe.wait_ge(sem("pass_ready"), 1)
            mm(start_ps, C("tri", p=E), cnt[0:E, 3:4], start=True, stop=True)
            mm(n_ps, cnt[0:E, 3:4], ones[0:E, 0:1], start=True, stop=True).then_inc(sem("start_mm"), 1)
            pe.wait_ge(sem("gate_ready"), 1)
            for t in range(TT):
                last = pe.transpose(bank[3][0:32, t * P:t * P + P], gate_[:, t, :], ident)
            last.then_inc(sem("turned_gate"), 1)
            pe.wait_ge(sem("items_ready"), 1)
            mm(ends_ps, cnt[0:E, 5:6], ident[0:E, 0:E], start=True, stop=True)
            mm(eid_ps, C("eid", p=E), T3[0:E, :], start=True, stop=True).then_inc(sem("eid_mm"), 1)
            for t in range(TT):
                mm(bank[0][:, 256 + t * MAXI:][:, 0:MAXI], posm[:, t * P:t * P + P], T3[0:E, :],
                   start=True, stop=False)
                mm(bank[0][:, 256 + t * MAXI:][:, 0:MAXI], ones[0:E, :], Q, start=False, stop=True)
            for t in range(TT):
                last = mm(bank[0][:, 384 + t * MAXI:][:, 0:MAXI], gateT[:, t * P:t * P + P], T3[0:E, :],
                          start=True, stop=True)
            last.then_inc(sem("itemcol_mm"), 1)
            pe.wait_ge(sem("bdn_loaded"), 16)
            for c in range(KT):
                mm(half(4 + c // 2, c % 2), bdn[:, c * P:c * P + P], gateT, start=False, stop=False,
                   skip_group_check=True)

            def gather():
                for c in range(KT):
                    for t in range(TT):
                        last = mm(bank[3][:, c * SLOTS:c * SLOTS + SLOTS], tok[:, t, c * P:c * P + P],
                                  pick[:, t, 0:SLOTS], start=(t == 0), stop=(t == TT - 1))
                last.then_inc(sem("gathered"), 1)

            pe.wait_ge(sem("tok_ready"), 4)
            pe.wait_ge(sem("pick_ready"), 1)
            gather()
            pe.wait_ge(sem("bp_ready"), 1)
            pe.wait_ge(sem("list_ready"), 3)
            n = pe.value_load(nitems, min_val=E, max_val=48)
            with pe.Fori(0, n) as i:
                e = pe.value_load(eids[0:1, bass.ds(i, 1)], min_val=0, max_val=E - 1)
                pe.wait_ge(sem("xe_ready"), i + 1)
                pe.wait_ge(sem("bsel_ready"), i + 1)
                pe.wait_ge(sem("aT_ready"), i + 1)
                pe.wait_ge(sem("back_ready"), i + 1)
                for b in range(2):
                    for gq in range(2):
                        mm(bank[b][64 * gq:64 * gq + 64, :], bsel,
                           bp[:, (2 * gq + b) * 512:(2 * gq + b) * 512 + 512], start=True, stop=False)
                for k in range(KT):
                    pe.wait_ge(sem(f"up_loaded{k}"), 16 * e + 16)
                    w = ring[:, (k + 4) % 8].rearrange("p k n -> p (k n)")
                    for b in range(2):
                        for gq in range(2):
                            last = mm(bank[b][64 * gq:64 * gq + 64, :], xe[:, k, :],
                                      w[:, (2 * gq + b) * 512:(2 * gq + b) * 512 + 512],
                                      start=False, stop=(k == KT - 1))
                    last.then_inc(sem("up_used"), 1)
                pe.wait_ge(sem("pick_ready"), i + 2)
                gather()
                pe.wait_ge(sem("a_ready"), i + 1)
                for b in range(4):
                    pe.transpose(bank[0][:, b * P:b * P + P], am[:, b * P:b * P + P], ident)
                pe.wait_ge(sem("spread_ready"), i + 1)
                for t in range(TT):
                    last = pe.transpose(bank[1][:, t * P:t * P + P], spread[:, t, :], ident)
                last.then_inc(sem("turned"), 1)
                pe.wait_ge(sem("aT_ready"), i + 2)
                for u in range(4):
                    pe.wait_ge(sem(f"down_loaded{u}"), 16 * e + 16)
                    for a in range(2):
                        kk = 2 * u + a
                        for gq in range(2):
                            last = mm(bank[2][64 * gq:64 * gq + 64, :], aT[:, kk % 4, kk // 4, :],
                                      down[:, u, a, gq * 512:gq * 512 + 512],
                                      start=(kk == 0), stop=(kk == 7))
                    last.then_inc(sem("down_used"), 1)
                pe.wait_ge(sem("y_ready"), i + 1)
                pe.wait_ge(sem("back_ready"), i + 2)
                for c in range(4):
                    for gq in range(2):
                        cc = 4 * gq + c
                        last = mm(half(4 + cc // 2, cc % 2), ysb[64 * gq:64 * gq + 64, c * P:c * P + P],
                                  back[64 * gq:64 * gq + 64, :], start=False, stop=False,
                                  skip_group_check=True)
                last.then_inc(sem("scattered"), 1)
            mean_square(16, 0, T)

        @block.scalar
        def _(ac):
            act_fn = ac.activation

            def squares(base, src, n):
                for k in range(KT):
                    if base == 0 and k % 2 == 0:
                        ac.wait_ge(sem(f"x_loaded{k // 2}"), 16)
                    if base + k >= 2:
                        ac.wait_ge(sem("sq_used"), base + k - 1)
                    act_fn(sq[:, k % 2, 0:n], src[:, k, :], ACT.Square).then_inc(sem("sq_ready"), 1)

            def root(base, b, n):
                ac.wait_ge(sem("sq_used"), base + KT)
                ac.wait_ge(sem("eps_ready"), 1)
                act_fn(rstd[:, 0:n], bank[b][:, 0:n], ACT.Sqrt, scale=1.0 / D,
                       bias=eps).then_inc(sem("rms"), 1)

            ac.wait_ge(sem("vec_loaded"), 16)
            ac.wait_ge(sem("csil_zero"), 1)
            for r, name in enumerate(("c", "cctx")):
                at = VEC[name][0]
                act_fn(csil[:, :, 2 + r], vec[:, at:at + KT], ACT.Sigmoid).then_inc(sem("csig"), 1)

            def sine(n):
                ac.wait_ge(sem("mlp_arg"), n + 1)
                act_fn(hact[:, 3, :], hact[:, 2, :], ACT.Sin).then_inc(sem("mlp_sin"), 1)

            sine(0)
            squares(0, xT, 512)
            root(0, 5, 512)
            sine(1)
            sine(2)
            for n in range(8):
                ac.wait_ge(sem("spec_mm"), n + 1)
                a, f, c = n // 4, (n % 4) // 2, n % 2
                act_fn(spec[:, a, f, c * 512:c * 512 + 512], bank[n][:, :],
                       ACT.Copy).then_inc(sem("spec_ready"), 1)

            def rows(s):
                ac.wait_ge(sem("unit_done"), 4 * ROUNDS.index(f"ada{s}") + 4)
                if s:
                    ac.wait_ge(sem("ada_turned"), s)
                act_fn(adar[:, :], half(0, 0), ACT.Copy).then_inc(sem("ada_rows"), 1)

            rows(0)
            rows(1)
            ac.dma_start(wrsb, wr).then_inc(sem("wr_loaded"), 16)
            ac.dma_start(wgksb, wgk).then_inc(sem("wgk_loaded"), 16)

            def unit_done(name, j):
                ac.wait_ge(sem("unit_done"), 4 * ROUNDS.index(name) + j + 1)

            for j in range(4):
                unit_done("qk", j)
                act_fn(qk[:, 2 * j:2 * j + 2, :].rearrange("p m t -> p (m t)"), bank[j][:, :], ACT.Copy,
                       scale=float(DK) ** -0.5 if j < 2 else 1.0).then_inc(sem("evac_qk"), 1)
            for j in range(4):
                unit_done("v", j)
                act_fn(vx[:, :, j * 256:j * 256 + 256], bank[j][:, :].rearrange("p (t c) -> p t c", t=TT),
                       ACT.Copy).then_inc(sem("evac_v"), 1)

            def gate(n):
                buf = tmp[:, n % 4, :]
                ac.wait_ge(sem("gate_mm"), n + 1)
                if n >= 4:
                    ac.wait_ge(sem("g_ready"), n - 3)
                act_fn(buf, bank[4 + n % 4][:, :], ACT.Abs).then_inc(sem("gate_abs"), 1)
                ac.wait_ge(sem("gate_abs"), n + 1)
                act_fn(buf, buf, ACT.Exp, scale=-1.0).then_inc(sem("gate_exp"), 1)
                ac.wait_ge(sem("gate_exp"), n + 1)
                act_fn(buf, buf, ACT.Ln, bias=1.0).then_inc(sem("gate_ln"), 1)

            def crest():
                for n in range(4):
                    ac.wait_ge(sem("crest_mm"), n + 1)
                    act_fn(kupc[:, n // 2, n % 2, :], bank[4 + n][:, :],
                           ACT.Exp).then_inc(sem("crest_read"), 1)

            def initial():
                for h in range(HEADS):
                    ac.wait_ge(sem("s0_mm"), h + 1)
                    act_fn(s0[:, h].rearrange("p d v -> p (d v)"), bank[4 + h][:, :],
                           ACT.Copy).then_inc(sem("s0_ready"), 1)

            def decay():
                for n in range(4):
                    ac.wait_ge(sem("decay_mm"), n + 1)
                    d, h = n // 2, 2 * (n % 2)
                    act_fn(qd[:, d, h:h + 2, :].rearrange("p h t -> p (h t)"), bank[4 + n][:, :],
                           ACT.Exp).then_inc(sem("exp_pos"), 1)
                    act_fn(ki[:, d, h:h + 2, :].rearrange("p h t -> p (h t)"), bank[4 + n][:, :],
                           ACT.Exp, scale=-1.0).then_inc(sem("decay_read"), 1)

            def kturn():
                ac.wait_ge(sem("kupc_ready"), 4)
                for t in range(TT):
                    ac.wait_ge(sem("k_turned"), t + 1)
                    act_fn(kcx[:, t, :], bank[4 + t][:, :], ACT.Copy).then_inc(sem("ktok_ready"), 1)

            def rest():
                for m, n in enumerate((2, 3, 0, 1)):
                    ac.wait_ge(sem("rest_mm"), m + 1)
                    act_fn(kupx[:, n // 2, n % 2, :], bank[4 + n][:, :],
                           ACT.Exp).then_inc(sem("rest_read"), 1)

            def uturn():
                for b in range(4):
                    ac.wait_ge(sem("u_turned"), b + 1)
                    act_fn(utok[:, 2 * b:2 * b + 2, :],
                           bank[4 + b][:, :].rearrange("p (c t) -> p c t", c=2),
                           ACT.Copy).then_inc(sem("utok_ready"), 1)

            def output(h):
                for v in range(2):
                    ac.wait_ge(sem("o_mm"), 2 * h + v + 1)
                    act_fn(act[:, 2 * h + v, :], half(5 + 2 * v, 1), ACT.Copy).then_inc(sem("o_read"), 1)
                    act_fn(sqo[:, 2 * h + v, :], half(5 + 2 * v, 1), ACT.Square).then_inc(sem("o_read"), 1)

            def onorm():
                for n in range(2):
                    ac.wait_ge(sem("onorm_mm"), n + 1)
                    act_fn(rso[:, 2 * n:2 * n + 2, :].rearrange("p h t -> p (h t)"), bank[4 + n][:, :],
                           ACT.Sqrt, scale=1.0 / DV, bias=eps).then_inc(sem("onorm_read"), 1)

            convs = {"hv": (0, uT), "hx1": (8, x1c), "hx0": (16, x0T)}

            def unit(name, j):
                unit_done(name, j)
                if name in convs:
                    base, dst = convs[name]
                    if name == "hx0":
                        ac.wait_ge(sem("qdki_ready"), 4)
                    for m in range(2):
                        c = 2 * j + m
                        act_fn(dst[:, c, :], half(j, m), ACT.Identity, scale=V("cw", 24 + base + c),
                               bias=V("cb", base + c)).then_inc(sem("conv_mid"), 1)
                else:
                    if name == "og":
                        ac.wait_ge(sem("z_mm"), 8)
                    dst = {"og": og, "ma": sma, "mb": smb}[name]
                    act_fn(dst[:, 2 * j:2 * j + 2, :].rearrange("p m t -> p (m t)"), bank[j][:, :],
                           ACT.Sigmoid).then_inc(sem("og_sig" if name == "og" else f"evac_{name}"), 1)

            run_middle(dict(gate=gate, crest=crest, s0=initial, decay=decay, kturn=kturn, rest=rest,
                            uturn=uturn, output=output, onorm=onorm, rows=rows), unit)
            ac.wait_ge(sem("act_ready"), 1)
            for q in range(3):
                ac.dma_start(bupsb[32 * q:32 * q + 32, :], bup).then_inc(sem(f"bup_loaded{q}"), 16)
            for k in range(KT):
                if k % 2 == 0:
                    ac.wait_ge(sem("evac_out"), k // 2 + 1)
                ac.wait_ge(sem("sq_used"), 8 + k - 1)
                act_fn(sq[:, k % 2, 0:T], xres[:, k, :], ACT.Square).then_inc(sem("sq_ready"), 1)
            root(8, 0, T)
            for k in range(KT):
                ac.wait_ge(sem("hx2_scaled"), k + 1)
                act_fn(hxx[:, k, :], hxx[:, k, :], ACT.Identity,
                       bias=mod[:, 3, k, 0:1]).then_inc(sem("hx2_ready"), 1)
            for b in range(4):
                ac.wait_ge(sem("tok_turned"), b + 1)
                act_fn(tok[:, b // 2, (b % 2) * 512:(b % 2) * 512 + 512], bank[4 + b][:, :],
                       ACT.Copy).then_inc(sem("tok_ready"), 1)
            ac.wait_ge(sem("top_ready"), 1)
            for t in range(TT):
                act_fn(ew[:, t, :], m8[:, t, 0:4], ACT.Exp, bias=nm[:, t:t + 1],
                       accum_out=es[:, t:t + 1]).then_inc(sem("top_exp"), 1)
            ac.wait_ge(sem("list_ready"), 3)
            act_fn(back[:, 0:P], ident, ACT.Copy).then_inc(sem("back_ready"), 1)
            ac.wait_ge(sem("gathered"), 1)
            act_fn(xe.rearrange("p k s -> p (k s)"), bank[3][:, :], ACT.Copy).then_inc(sem("xe_ready"), 1)
            n = ac.value_load(nitems, min_val=E, max_val=48)
            with ac.Fori(0, n) as i:
                ac.wait_ge(sem("glu_ready"), i + 1)
                act_fn(sg, glu, ACT.Sigmoid, scale=ALPHA).then_inc(sem("sg_ready"), 1)
                ac.wait_ge(sem("gathered"), i + 2)
                act_fn(xe.rearrange("p k s -> p (k s)"), bank[3][:, :],
                       ACT.Copy).then_inc(sem("xe_ready"), 1)
                ac.wait_ge(sem("turned"), i + 1)
                act_fn(back, half(1, 0), ACT.Copy).then_inc(sem("back_ready"), 1)
                ac.wait_ge(sem("down_used"), 4 * i + 4)
                act_fn(ysb, bank[2][:, :], ACT.Copy).then_inc(sem("y_ready"), 1)
            for k in range(KT):
                ac.wait_ge(sem("x2_ready"), k + 1)
                ac.wait_ge(sem("sq_used"), 16 + k - 1)
                act_fn(sq[:, k % 2, 0:T], xres[:, k, :], ACT.Square).then_inc(sem("sq_ready"), 1)
            root(16, 0, T)

        @block.vector
        def _(ve):
            steps = [0]

            def link(ins):
                steps[0] += 1
                ins.then_inc(sem("vector_step"), 1)
                ve.wait_ge(sem("vector_step"), steps[0])

            def grid(ap):
                return ap.rearrange("p (r w) -> p r w", w=64)

            ve.memset(eps, EPS).then_inc(sem("eps_ready"), 1)
            ve.memset(csil[:, :, :], 0.0).then_inc(sem("csil_zero"), 1)
            ve.wait_ge(sem("vec_loaded"), 16)
            for n in range(3):
                ve.wait_ge(sem("mlp_mm"), n + 1)
                link(ve.tensor_scalar(hact[:, 0, :], bank[4][0:64, 0:256], V("hmlp", n, 64),
                                      V("hmlp", 3, 64), ALU.add, ALU.mult))
                link(ve.tensor_scalar(hact[:, 1, :], hact[:, 0, :], 1.0 / (2 * np.pi), MAGIC,
                                      ALU.mult, ALU.add))
                link(ve.tensor_scalar(hact[:, 1, :], hact[:, 1, :], MAGIC, None, ALU.subtract))
                link(ve.scalar_tensor_tensor(out=hact[:, 2, :], in0=hact[:, 1, :], scalar=-TWO_PI_HI,
                                             in1=hact[:, 0, :], op0=ALU.mult, op1=ALU.add))
                link(ve.scalar_tensor_tensor(out=hact[:, 2, :], in0=hact[:, 1, :], scalar=-TWO_PI_LO,
                                             in1=hact[:, 2, :], op0=ALU.mult, op1=ALU.add))
                ve.tensor_scalar(hact[:, 2, :], hact[:, 2, :], PI, -PI, ALU.min,
                                 ALU.max).then_inc(sem("mlp_arg"), 1)
                if n == 1:
                    ve.wait_ge(sem("csig"), 2)
                    for r, name in enumerate(("c", "cctx")):
                        at = VEC[name][0]
                        ins = ve.tensor_tensor(csil[:, :, r], csil[:, :, 2 + r], vec[:, at:at + KT],
                                               ALU.mult)
                    link(ins)
                    ve.memset(csil[:, :, 2:4], 0.0).then_inc(sem("csil_ready"), 1)
            ve.wait_ge(sem("rms"), 1)
            ve.reciprocal(rstd[:, :], rstd[:, :]).then_inc(sem("rstd_ready"), 1)
            ve.wait_ge(sem("win_loaded"), 16)
            for n in range(4):
                t, c = n // 2, n % 2
                cs = slice(c * 512, c * 512 + 512)
                ve.wait_ge(sem("taps_mm"), 2 * n + 2)
                if n >= 2:
                    ve.wait_ge(sem("taps_sum"), n - 1)
                    ve.wait_ge(sem("taps_dif"), n - 1)
                fwd, bwd = htmp[:, n % 2, 0, :], htmp[:, n % 2, 1, :]
                ve.tensor_tensor(fwd, bank[4 * t + c][:, :], win[:, t, cs], ALU.mult)
                ins = ve.tensor_tensor(bwd, bank[4 * t + 2 + c][:, :], win[:, t, cs], ALU.mult)
                if t == 0:
                    link(ins)
                    ins = ve.memset(bwd[0:1, :], 0.0)
                ins.then_inc(sem("taps_win"), 1)
                ve.wait_ge(sem("taps_win"), n + 1)
                ve.tensor_tensor(hsum[:, t, cs], fwd, bwd, ALU.add).then_inc(sem("taps_sum"), 1)
            ve.wait_ge(sem("rstd_ready"), 1)
            for k in range(KT):
                ins = ve.scalar_tensor_tensor(out=hx[:, k, :], in0=xT[:, k, :], scalar=V("nm", k),
                                              in1=rstd[:, :], op0=ALU.mult, op1=ALU.mult)
            link(ins)

            def turn(s):
                ve.wait_ge(sem("ada_turned"), s + 1)
                at = VEC["bada"][0] + s * KT
                bias = vec[:, at:at + KT].rearrange("p (g j) -> p j g", j=2)
                src = half(1, 0).rearrange("p (j g r) -> p j g r", j=2, g=4)
                for r in range(2):
                    dst = mod[:, s, :, r].rearrange("p (g j) -> p j g", j=2)
                    ins = ve.tensor_tensor(dst, src[:, :, :, r], bias, ALU.add)
                if s in (1, 4):
                    link(ins)
                    ins = ve.tensor_scalar(mod[:, s, :, :], mod[:, s, :, :], 1.0, None, ALU.add)
                if s == 4:
                    link(ins)
                    at = VEC["nf"][0]
                    ins = ve.tensor_tensor(mod[:, s, :, 1], mod[:, s, :, 0], vec[:, at:at + KT], ALU.mult)
                ins.then_inc(sem("mod_ready"), 1)

            turn(0)
            turn(1)
            ve.wait_ge(sem("mod_ready"), 2)
            for r, dst in enumerate((hxx, hxc)):
                for k in range(KT):
                    ve.tensor_scalar(dst[:, k, :], dst[:, k, :], mod[:, 1, k, r:r + 1],
                                     mod[:, 0, k, r:r + 1], ALU.mult, ALU.add).then_inc(sem("hx_ready"), 1)

            def unit_done(name, j):
                ve.wait_ge(sem("unit_done"), 4 * ROUNDS.index(name) + j + 1)

            for j in range(2, 4):
                unit_done("qk", j)
                ve.tensor_copy(kcx[:, :, (j - 2) * 256:(j - 2) * 256 + 256],
                               bank[4 + j][:, :].rearrange("p (t c) -> p t c", t=TT)).then_inc(sem("kc_ready"), 1)
            ve.wait_ge(sem("wr_loaded"), 16)
            ve.memset(rT[32:33, :], 1.0).then_inc(sem("low_ready"), 1)
            ve.wait_ge(sem("low_mm"), 1)
            ve.tensor_copy(rT[0:32, :], bank[4][0:32, :]).then_inc(sem("low_ready"), 1)
            for j in range(4):
                unit_done("v", j)
                ve.tensor_copy(vc[:, :, j * 256:j * 256 + 256],
                               bank[4 + j][:, :].rearrange("p (t c) -> p t c", t=TT)).then_inc(sem("evac_vc"), 1)

            def gate(n):
                dst = (gx if n < 4 else gc)[:, (n // 2) % 2, n % 2, :]
                ve.wait_ge(sem("gate_ln"), n + 1)
                ve.scalar_tensor_tensor(out=dst, in0=bank[4 + n % 4][:, :], scalar=0.0,
                                        in1=tmp[:, n % 4, :], op0=ALU.min,
                                        op1=ALU.subtract).then_inc(sem("g_ready"), 1)

            convs = {"hv": (0, uT), "hx1": (8, x1c), "hx0": (16, x0T)}

            def unit(name, j):
                if name in convs:
                    base, dst = convs[name]
                    mids[0] += 2
                    ve.wait_ge(sem("conv_mid"), mids[0])
                    for tap, a, b in ((0, 1, 0), (2, 0, 1)):
                        for m in range(2):
                            c = 2 * j + m
                            acc, src = grid(dst[:, c, :]), grid(half(j, m))
                            ins = ve.scalar_tensor_tensor(
                                out=acc[:, :, a:a + 63], in0=src[:, :, b:b + 63],
                                scalar=V("cw", 24 * tap + base + c), in1=acc[:, :, a:a + 63],
                                op0=ALU.mult, op1=ALU.add)
                        if tap == 0:
                            link(ins)
                    ins.then_inc(sem(f"evac_{name}"), 1)
                    if name == "hx1" and j == 3:
                        ve.wait_ge(sem("evac_hx1"), 4)
                        ve.tensor_tensor(uT, uT, x1c, ALU.mult).then_inc(sem("u_ready"), 1)
                elif name == "og":
                    ve.wait_ge(sem("og_sig"), j + 1)
                    dst = og[:, 2 * j:2 * j + 2, :].rearrange("p m t -> p (m t)")
                    ve.tensor_tensor(dst, dst, bank[j][:, :], ALU.mult).then_inc(sem("evac_og"), 1)

            def crest():
                for n in range(4):
                    ve.wait_ge(sem("crest_read"), n + 1)
                    ve.tensor_tensor(kupc[:, n // 2, n % 2, :], kupc[:, n // 2, n % 2, :],
                                     kcx[:, n // 2, :], ALU.mult).then_inc(sem("kupc_ready"), 1)

            def decay():
                for n in range(4):
                    ve.wait_ge(sem("exp_pos"), n + 1)
                    ve.wait_ge(sem("decay_read"), n + 1)
                    d, h = n // 2, 2 * (n % 2)
                    at = 63 if d == 0 else 0
                    link(ve.tensor_copy(
                        dec[:, d, h:h + 2, :],
                        qd[:, d, h:h + 2, :].rearrange("p h (c w) -> p h c w", w=CHUNK)[:, :, :, at]))
                    ve.tensor_tensor(qd[:, d, h:h + 2, :], qd[:, d, h:h + 2, :], qk[:, h:h + 2, :],
                                     ALU.mult)
                    ve.tensor_tensor(ki[:, d, h:h + 2, :], ki[:, d, h:h + 2, :], qk[:, 4 + h:6 + h, :],
                                     ALU.mult).then_inc(sem("qdki_ready"), 1)

            def rest():
                ve.wait_ge(sem("ktok_ready"), 2)
                for m, n in enumerate((2, 3, 0, 1)):
                    ve.wait_ge(sem("rest_read"), m + 1)
                    ve.tensor_tensor(kupx[:, n // 2, n % 2, :], kupx[:, n // 2, n % 2, :],
                                     kcx[:, n // 2, :], ALU.mult).then_inc(sem("kupx_ready"), 1)

            def uspec(f):
                for c in range(2):
                    n = 2 * f + c
                    cs = slice(c * 512, c * 512 + 512)
                    ve.wait_ge(sem("u_spec"), n + 1)
                    if n:
                        ve.wait_ge(sem("prod_ready"), 2 * n)
                    re, im = spec[:, 0, f, cs], spec[:, 1, f, cs]
                    ur, ui = bank[4 + c][:, :], bank[6 + c][:, :]
                    ve.tensor_tensor(tmp[:, 0, :], ur, re, ALU.mult)
                    ve.tensor_tensor(tmp[:, 1, :], ui, im, ALU.mult)
                    ve.tensor_tensor(tmp[:, 2, :], ui, re, ALU.mult)
                    link(ve.tensor_tensor(tmp[:, 3, :], ur, im, ALU.mult))
                    ve.tensor_tensor(re, tmp[:, 0, :], tmp[:, 1, :],
                                     ALU.subtract).then_inc(sem("prod_ready"), 1)
                    ve.tensor_tensor(im, tmp[:, 2, :], tmp[:, 3, :],
                                     ALU.add).then_inc(sem("prod_ready"), 1)

            def scores():
                ve.wait_ge(sem("prod_ready"), 8)
                link(ve.memset(region(14), 0.0))
                for h in range(HEADS):
                    ve.wait_ge(sem("att_mm"), h + 1)
                    ve.copy_predicated(att[:, h, :], C("mask").bitcast(U32),
                                       bank[4 + h][:, :]).then_inc(sem("att_ready"), 1)

            def inverse():
                for c in range(KT):
                    ve.wait_ge(sem("z_mm"), c - c % 2 + 2)
                    ve.scalar_tensor_tensor(out=uT[:, c, :], in0=uT[:, c, :], scalar=V("hb", c),
                                            in1=half(4 + c // 2, c % 2), op0=ALU.mult,
                                            op1=ALU.add).then_inc(sem("z_read"), 1)
                ve.wait_ge(sem("z_read"), 8)
                ve.wait_ge(sem("evac_hx0"), 4)
                ve.tensor_tensor(uT, uT, x0T, ALU.mult).then_inc(sem("z_ready"), 1)

            def update(h):
                if h >= 2:
                    ve.wait_ge(sem("o_mm"), 2 * h - 2)
                st = sst[h % 2]
                upd = {(0, 0): half(4, 0), (1, 3): half(6, 1), (0, 1): half(6, 0), (1, 2): half(5, 0),
                       (0, 2): half(4, 1), (1, 1): half(7, 0)}
                ve.wait_ge(sem("upd_mm"), 6 * h + 6)
                for n in range(3):
                    for d, c, to in ((0, n, n), (1, 3 - n, 2 - n)):
                        prev = s0[:, h, d, :] if n == 0 else st[:, d, n - 1 if d == 0 else c, :]
                        ins = ve.scalar_tensor_tensor(out=st[:, d, to, :], in0=prev,
                                                      scalar=dec[:, d, h, c:c + 1], in1=upd[(d, c)],
                                                      op0=ALU.mult, op1=ALU.add)
                        if n == 2:
                            ins.then_inc(sem("state_ready"), 1)
                    if n < 2:
                        link(ins)

            def onorm():
                for n in range(2):
                    ve.wait_ge(sem("onorm_read"), n + 1)
                    dst = rso[:, 2 * n:2 * n + 2, :]
                    ins = ve.reciprocal(dst, dst)
                link(ins)
                for m in range(8):
                    ins = ve.scalar_tensor_tensor(out=act[:, m, :], in0=act[:, m, :],
                                                  scalar=V("gn", m % 2), in1=rso[:, m // 2, :],
                                                  op0=ALU.mult, op1=ALU.mult)
                link(ins)
                ve.wait_ge(sem("evac_og"), 4)
                ve.tensor_tensor(act, act, og, ALU.mult).then_inc(sem("act_ready"), 1)

            mids = [0]
            run_middle(dict(gate=gate, crest=crest, decay=decay, rest=rest, uspec=uspec, att=scores,
                            inverse=inverse, update=update, onorm=onorm, turn=turn), unit)
            for j in range(4):
                unit_done("gla", j)
                dst = sma[:, 2 * j:2 * j + 2, :].rearrange("p m t -> p (m t)")
                ve.tensor_tensor(dst, dst, bank[j][:, :], ALU.mult).then_inc(sem("evac_gla"), 1)
            for j in range(4):
                unit_done("hyo", j)
                dst = smb[:, 2 * j:2 * j + 2, :].rearrange("p m t -> p (m t)")
                link(ve.tensor_tensor(dst, dst, bank[j][:, :], ALU.mult))
                y = sma[:, 2 * j:2 * j + 2, :].rearrange("p m t -> p (m t)")
                ve.tensor_tensor(y, y, dst, ALU.add).then_inc(sem("evac_hyo"), 1)
            for j in range(4):
                unit_done("out", j)
                for m in range(2):
                    c = 2 * j + m
                    ins = ve.scalar_tensor_tensor(out=xres[:, c, :], in0=half(j, m),
                                                  scalar=mod[:, 2, c, 0:1], in1=xres[:, c, :],
                                                  op0=ALU.mult, op1=ALU.add)
                ins.then_inc(sem("evac_out"), 1)
            ve.memset(zero, 0.0).then_inc(sem("zero_ready"), 1)
            ve.wait_ge(sem("rms"), 2)
            link(ve.reciprocal(rstd[:, 0:T], rstd[:, 0:T]))
            for k in range(KT):
                ve.scalar_tensor_tensor(out=hxx[:, k, :], in0=xres[:, k, :], scalar=mod[:, 4, k, 1:2],
                                        in1=rstd[:, 0:T], op0=ALU.mult,
                                        op1=ALU.mult).then_inc(sem("hx2_scaled"), 1)
            ve.wait_ge(sem("logit_mm"), 1)
            link(ve.tensor_copy(logit, bank[1][:, 0:TT * E].rearrange("p (t e) -> p t e", t=TT)))
            for t in range(TT):
                ins = ve.max(m8[:, t, :], logit[:, t, :])
            link(ins)
            ve.tensor_scalar(nm, m8[:, :, 0], -1.0, None, ALU.mult).then_inc(sem("top_ready"), 1)
            for t in range(TT):
                ins = ve.max_index(i8[:, t, :], m8[:, t, :], logit[:, t, :])
            link(ins)
            link(ve.tensor_copy(if8, i8))
            experts = C("slot", 0, E)
            for t in range(TT):
                for k in range(4):
                    ins = ve.tensor_scalar(sk[:, t, k, :], experts, if8[:, t, k:k + 1], None, ALU.is_equal)
            link(ins)
            for t in range(TT):
                for q in range(3):
                    ins = ve.tensor_reduce(sel[:, t, q * E:q * E + E], sk[:, t].rearrange("p k e -> p e k"),
                                           AX_X, ALU.add)
            ins.then_inc(sem("sel_ready"), 1)
            ve.wait_ge(sem("top_exp"), 2)
            link(ve.reciprocal(es, es))
            for t in range(TT):
                ins = ve.tensor_scalar(ew[:, t, :], ew[:, t, :], es[:, t:t + 1], None, ALU.mult)
            link(ins)
            ve.wait_ge(sem("count_mm"), 1)
            link(ve.tensor_copy(cnt[:, 0:1], bank[1][0:96, 64:65]))
            link(ve.tensor_scalar(cnt[:, 1:2], cnt[:, 0:1], 1.0 * SLOTS, 1.0, ALU.is_gt, ALU.add))
            link(ve.scalar_tensor_tensor(out=cnt[:, 2:3], in0=cnt[:, 0:1], scalar=2.0 * SLOTS,
                                         in1=cnt[:, 1:2], op0=ALU.is_gt, op1=ALU.add))
            ve.scalar_tensor_tensor(out=cnt[:, 3:4], in0=cnt[:, 0:1], scalar=3.0 * SLOTS,
                                    in1=cnt[:, 2:3], op0=ALU.is_gt, op1=ALU.add).then_inc(sem("pass_ready"), 1)
            for t in range(TT):
                for k in range(4):
                    ins = ve.tensor_scalar(gk[:, t, k, :], experts, if8[:, t, k:k + 1], ew[:, t, k:k + 1],
                                           ALU.is_equal, ALU.mult)
            link(ins)
            for t in range(TT):
                ins = ve.tensor_reduce(gate_[:, t, :], gk[:, t].rearrange("p k e -> p e k"), AX_X, ALU.add)
            ins.then_inc(sem("gate_ready"), 1)
            ve.wait_ge(sem("start_mm"), 1)
            ve.tensor_copy(nitems, bank[1][0:1, 68:69]).then_inc(sem("list_ready"), 1)
            link(ve.tensor_copy(cnt[:, 4:5], bank[1][0:96, 66:67]))
            link(ve.tensor_tensor(cnt[:, 5:6], cnt[:, 4:5], cnt[:, 3:4], ALU.add))
            item = C("slot", 0, MAXI, p=96)
            ve.tensor_scalar(Q, item[0:E, :], cnt[0:E, 4:5], -1.0 * SLOTS, ALU.subtract, ALU.mult)
            link(ve.tensor_scalar(T3, item, cnt[:, 4:5], None, ALU.is_ge))
            link(ve.scalar_tensor_tensor(out=T3, in0=item, scalar=cnt[:, 5:6], in1=T3,
                                         op0=ALU.is_lt, op1=ALU.mult))
            ve.tensor_tensor(Q, Q, T3[0:E, :], ALU.mult)
            ve.wait_ge(sem("turned_sel"), 1)
            link(ve.tensor_copy(selT, bank[2][0:32, 0:T]))
            ve.wait_ge(sem("place_mm"), 1)
            link(ve.tensor_scalar(posm, bank[0][0:32, 0:T], 16.0, FAR, ALU.mult, ALU.add))
            link(ve.tensor_tensor(posm, posm, selT, ALU.mult))
            link(ve.tensor_scalar(posm, posm, -FAR, None, ALU.add))
            ve.wait_ge(sem("turned_gate"), 1)
            ve.tensor_copy(gateT, bank[3][0:32, 0:T]).then_inc(sem("items_ready"), 1)
            ve.wait_ge(sem("eid_mm"), 1)
            ve.tensor_scalar(lasts, bank[1][0:1, 96:128], -1.0, None, ALU.add).then_inc(sem("list_ready"), 1)
            ve.tensor_copy(eids, bank[1][0:1, 128:192]).then_inc(sem("list_ready"), 1)
            ve.wait_ge(sem("itemcol_mm"), 1)
            ve.tensor_copy(posI, bank[0][:, 256:384].rearrange("p (t i) -> p t i", t=TT))
            link(ve.tensor_copy(gateI, bank[0][:, 384:512].rearrange("p (t i) -> p t i", t=TT)))

            slots = C("slot")

            def picks(i):
                for t in range(TT):
                    ins = ve.tensor_scalar(pick[:, t, :], slots, posI[:, t, bass.ds(i, 1)], None,
                                           ALU.is_equal)
                ins.then_inc(sem("pick_ready"), 1)

            def spreads(i):
                for t in range(TT):
                    ins = ve.tensor_scalar(spread[:, t, :], slots, posI[:, t, bass.ds(i, 1)],
                                           gateI[:, t, bass.ds(i, 1)], ALU.is_equal, ALU.mult)
                ins.then_inc(sem("spread_ready"), 1)

            def bias_select(i):
                ve.tensor_scalar(bsel, ones[0:96, 0:SLOTS], T3[:, bass.ds(i, 1)], None,
                                 ALU.mult).then_inc(sem("bsel_ready"), 1)

            picks(0)
            spreads(0)
            bias_select(0)
            ve.memset(aT, 0.0).then_inc(sem("aT_ready"), 1)
            ve.wait_ge(sem("list_ready"), 3)
            n = ve.value_load(nitems, min_val=E, max_val=48)
            with ve.Fori(0, n) as i:
                ve.wait_ge(sem("gathered"), i + 1)
                picks(i + 1)
                ve.wait_ge(sem("up_used"), 8 * i + 8)
                ve.tensor_scalar(glu, bank[0][:, :], LIMIT, None, ALU.min).then_inc(sem("glu_ready"), 1)
                ve.tensor_scalar(lin, bank[1][:, :], LIMIT, -LIMIT, ALU.min,
                                 ALU.max).then_inc(sem("lin_ready"), 1)
                bias_select(i + 1)
                ve.wait_ge(sem("glu_ready"), i + 1)
                ve.wait_ge(sem("lin_ready"), i + 1)
                ve.scalar_tensor_tensor(out=lin, in0=lin, scalar=1.0, in1=glu, op0=ALU.add,
                                        op1=ALU.mult).then_inc(sem("gated"), 1)
                ve.wait_ge(sem("gated"), i + 1)
                ve.wait_ge(sem("sg_ready"), i + 1)
                ve.tensor_tensor(am, lin, sg, ALU.mult).then_inc(sem("a_ready"), 1)
                ve.wait_ge(sem("turned"), i + 1)
                ve.tensor_copy(aT.rearrange("p b h s -> p (b h s)"), bank[0][:, :]).then_inc(sem("aT_ready"), 1)
                spreads(i + 1)
            ve.wait_ge(sem("scattered"), n)
            for c in range(KT):
                ve.scalar_tensor_tensor(out=xres[:, c, :], in0=half(4 + c // 2, c % 2),
                                        scalar=mod[:, 5, c, 0:1], in1=xres[:, c, :],
                                        op0=ALU.mult, op1=ALU.add).then_inc(sem("x2_ready"), 1)
            ve.wait_ge(sem("rms"), 3)
            link(ve.reciprocal(rstd[:, 0:T], rstd[:, 0:T]))
            for k in range(KT):
                ve.scalar_tensor_tensor(out=hxx[:, k, :], in0=xres[:, k, :], scalar=V("nfin", k),
                                        in1=rstd[:, 0:T], op0=ALU.mult,
                                        op1=ALU.mult).then_inc(sem("out_ready"), 1)

        @block.gpsimd
        def _(po):
            for n in range(4):
                t, c = n // 2, n % 2
                po.wait_ge(sem("taps_win"), n + 1)
                po.tensor_tensor(hdif[:, t, c * 512:c * 512 + 512], htmp[:, n % 2, 0, :],
                                 htmp[:, n % 2, 1, :], ALU.subtract).then_inc(sem("taps_dif"), 1)
            po.wait_ge(sem("evac_hyo"), 4)
            po.dma_start(bdn, bdown).then_inc(sem("bdn_loaded"), 16)
            po.wait_ge(sem("unit_done"), 4 * len(ROUNDS))
            po.dma_start(wrt, wrouter).then_inc(sem("wrt_loaded"), 16)
            po.dma_start(brt, brouter).then_inc(sem("brt_loaded"), 16)
            for q in range(3):
                po.wait_ge(sem(f"bup_loaded{q}"), 16)
            steps = 0
            for q in range(3):
                lo = slice(32 * q, 32 * q + 32)
                for r in range(q + 1):
                    steps += 1
                    po.tensor_copy(bp[lo, :], bupsb[lo, :]).then_inc(sem("pool_step"), 1)
                    po.wait_ge(sem("pool_step"), steps)
                    if r < q:
                        steps += 1
                        po.tensor_tensor(bupsb[lo, :], bupsb[lo, :], bp[lo, :],
                                         ALU.subtract).then_inc(sem("pool_step"), 1)
                        po.wait_ge(sem("pool_step"), steps)
            po.nop().then_inc(sem("bp_ready"), 1)


def shape_constants():
    c = np.zeros((P, NCON), np.float32)

    def put(name, a):
        at, width = CON[name]
        a = np.asarray(a, np.float64).reshape(len(a), width)
        c[:len(a), at:at + width] = a

    s, t = np.arange(P)[:, None], np.arange(P)[None]
    same = s // CHUNK == t // CHUNK
    put("ident", s == t)
    put("ones", np.ones((P, P)))
    upto, frm = (s <= t) & same, (s >= t) & same
    put("mask", np.concatenate([upto, frm, upto, frm], 1) / GNORM)
    put("rest", np.concatenate([(s > t) & same, (s < t) & same], 1) / GNORM)
    put("after", (s > t) / GNORM)
    put("before", (s < t) / GNORM)
    put("all16", np.ones((P, P)) / GNORM)
    n = np.arange(T)
    ang = np.pi * np.outer(n, 2 * n + 1) / (2 * T)
    fwd = np.stack([np.cos(ang), -np.sin(ang)])
    put("dft", fwd.reshape(2, TT, P, T).transpose(2, 0, 1, 3).reshape(P, -1))
    inv = np.stack([np.cos(ang).T, -np.sin(ang).T]) / T
    put("idft", inv.reshape(2, TT, P, T).transpose(2, 0, 1, 3).reshape(P, -1))
    put("slot", np.tile(np.arange(SLOTS), (P, 2)))
    put("tri", np.arange(E)[:, None] < np.arange(96)[None] % E)
    put("eid", np.arange(E)[:, None])
    pos = np.arange(T, dtype=np.float64)
    tn = (pos / (T - 1)).astype(np.float32)
    bands = (EMB - 1) // 2
    f = np.linspace(1e-4, bands - 1, bands).astype(np.float32)
    a = (np.float32(2 * np.pi / T) * pos.astype(np.float32)[:, None] * f[None]).astype(np.float32)
    z = np.concatenate([tn[:, None], np.cos(a, dtype=np.float64), -np.sin(a, dtype=np.float64)], 1)
    deltas = np.abs(np.linspace(np.log(1e-2) / 1.5, np.log(1e-2) / 0.3, D).astype(np.float32))
    w = np.exp(-tn[:, None].astype(np.float64) * deltas[None])
    return c, z.T.astype(np.float32), w.astype(np.float32).reshape(TT, P, D)


def kernel(**inputs):
    import concourse.bacc as bacc
    from concourse.bass_utils import run_bass_kernel_spmd

    a = {k: np.asarray(v) for k, v in inputs.items()}
    for k in a:
        if a[k].shape[0] == 1 and k not in ("x", "c", "ctx"):
            a[k] = a[k][0]
    con, z, window = shape_constants()
    vecs = np.zeros((P, NVEC), np.float32)

    def put(name, v, rows=P):
        at, width = VEC[name]
        vecs[:rows, at:at + width] = v

    def cols(v):
        return v.reshape(-1, P).T

    put("c", cols(a["c"][0]))
    put("cctx", cols(a["c_ctx"]))
    put("nm", cols(a["norm_mix"]))
    put("nf", cols(a["norm_ffn"]))
    put("nfin", cols(a["norm_final"]))
    put("bada", cols(a["b_ada"]))
    order = np.concatenate([np.arange(2 * D, 3 * D), np.arange(D, 2 * D), np.arange(D)])
    put("cw", np.concatenate([cols(a["hy_conv_w"][i][order]) for i in range(3)], 1))
    put("cb", cols(a["hy_conv_b"][order]))
    put("hb", cols(a["hy_bias"]))
    put("gn", cols(a["gla_norm"]))
    put("hmlp", np.stack([a["hy_f_b1"], a["hy_f_b2"], a["hy_f_b3"], a["hy_sin_freq"]], 1), ORDER)
    hw = np.zeros((ORDER, 192), np.float32)
    hw[:EMB, 0:64] = a["hy_f_w1"]
    hw[:, 64:128] = a["hy_f_w2"]
    hw[:, 128:192] = a["hy_f_w3"]
    w_in, w_ada = a["w_in"], a["w_ada"]
    blocks = {"qk": w_in[:, 0:1024], "v": w_in[:, 1024:2048], "og": w_in[:, 2048:3072],
              "hx0": w_in[:, 3104:4128], "hx1": w_in[:, 4128:5152], "hv": w_in[:, 5152:6176],
              "ma": w_in[:, 6176:7200], "mb": w_in[:, 7200:8224],
              "gla": a["w_gla_out"], "hyo": a["w_hy_out"], "out": a["w_out"]}
    for s in range(6):
        blocks[f"ada{s}"] = w_ada[:, s * D:s * D + D]
    wmix = np.stack([blocks[r].reshape(KT, P, 4, 256).transpose(2, 1, 0, 3).reshape(4, P, KT * 256)
                     for r in ROUNDS])
    xt = np.concatenate([a["x"][0], a["ctx"][0]], 0).T.reshape(KT, P, 2 * T)
    wgk = np.zeros((33, 2, 512), np.float32)
    wgk[0:16, 0], wgk[16:32, 1] = a["w_gk_f"], a["w_gk_b"]
    wgk[32, 0], wgk[32, 1] = a["b_gk_f"], a["b_gk_b"]
    wup = a["w_up"].reshape(E, KT, P, 2, 512, 2).transpose(0, 1, 2, 3, 5, 4).reshape(E, KT, P, 2048)
    bup = a["b_up"].reshape(E, 2, 512, 2).transpose(0, 1, 3, 2).reshape(E, 2048)
    arrays = {
        "vecs": vecs, "cons": con, "xt": xt, "zt": z, "hw": hw, "hw4": a["hy_f_w4"], "window": window,
        "wmix": wmix, "wr": w_in[:, 3072:3104].reshape(KT, P, 32).transpose(1, 0, 2), "wgk": wgk,
        "wrouter": a["w_router"].reshape(KT, P, E).transpose(1, 0, 2), "brouter": a["b_router"][None],
        "wup": wup, "bup": bup, "wdown": a["w_down"].reshape(E, 4, 2, P, D), "bdown": a["b_down"],
    }
    nc = bacc.Bacc("TRN2", target_bir_lowering=False, num_devices=1)
    sent, args = {}, []
    for name, v in arrays.items():
        sent[f"in_{name}"] = np.ascontiguousarray(v)
        args.append(nc.dram_tensor(f"in_{name}", v.shape, F32, kind="ExternalInput").ap())
    args.append(nc.dram_tensor("out_t", (KT, P, T), F32, kind="ExternalOutput").ap())
    build_program(nc, *args)
    r = run_bass_kernel_spmd(nc, [sent], core_ids=[0])
    return np.ascontiguousarray(r.results[0]["out_t"].reshape(D, T).T)[None]
```

```python
from contextlib import ExitStack

import numpy as np

import concourse.bass as bass
from concourse import mybir

F32 = mybir.dt.float32
BF16 = mybir.dt.bfloat16
I32 = mybir.dt.int32
U32 = mybir.dt.uint32
ALU = mybir.AluOpType
ACT = mybir.ActivationFunctionType
AX_X = mybir.AxisListType.X

P = 128
D = 1024
T = 256
KT = D // P
TT = T // P
HEADS = 4
DK = 128
DV = 256
CHUNK = 64
GNORM = 16.0
EMB, ORDER = 33, 64
E = 32
SLOTS = 64
MAXI = 64
EPS = 1e-6
LIMIT, ALPHA = 7.0, 1.702
MAGIC = 12582912.0
PI = 3.141592
TWO_PI_HI = 6.28125
TWO_PI_LO = 2 * np.pi - 6.28125

ROUNDS = ["ada0", "ada1", "qk", "v", "hv", "ada2", "hx1", "ada3", "hx0", "ada4", "og", "ada5",
          "ma", "mb", "gla", "hyo", "out"]
MIDDLE = """
    gate0 gate1 hv0 gate2 gate3 hv1 gate4 gate5 hv2 gate6 gate7 hv3
    rows2 crest turn2 hx10 s0 hx11 decay hx12 kturn hx13 rows3 rest turn3
    uturn hx00 uspec0 hx01 uspec1 hx02 hx03 rows4 turn4 att inverse
    og0 update0 og1 output0 og2 update1 og3 rows5 output1 turn5
    ma0 update2 ma1 output2 ma2 update3 ma3 output3 mb0 onorm mb1 mb2 mb3
""".split()
PROJ = [r for r in ROUNDS if not r.startswith("ada")]
FAR = 1000.0
SPECTRUM = [2, 0, 3, 4, 6, 1, 5, 7]
PARTS = [(0, 0), (1, 0), (0, 1), (1, 1)]
PLACE = [0, 1, 6, 8, 9, 10, 7, 2, 3, 4, 5, 11, 12, 13, 14]
REGIONS = len(PLACE)
RING, GROUP, CHUNKS = 18, 6, 12


def place(e, c):
    return GROUP * ((2 * e + 1 + c // GROUP) % 3) + c % GROUP


def turn_of(e, c):
    return (2 * e + 1 + c // GROUP + 2) // 3


def columns(parts):
    at, where = 0, {}
    for name, width in parts:
        where[name] = (at, width)
        at += width
    return where, at


VEC, NVEC = columns([("c", 8), ("cctx", 8), ("nm", 8), ("nf", 8), ("nfin", 8), ("bada", 48),
                     ("cw", 72), ("cb", 24), ("hb", 8), ("gn", 2), ("hmlp", 4)])
CON, NCON = columns([("dft", 512), ("idft", 512), ("room", 1024), ("ident", 128), ("ones", 128),
                     ("mask", 512), ("rest", 256), ("after", 128), ("before", 128), ("all16", 128),
                     ("slot", 128), ("tri", 96), ("stack", E)])



def build_program(nc, vecs, cons, xt, zt, hw, hw4, window, wmix, wr, wgk, wrouter, brouter,
                  wexp, bup, bdown, out):
    with ExitStack() as ctx:
        made = {}

        def sem(name):
            if name not in made:
                made[name] = ctx.enter_context(nc.semaphore(name))
            return made[name]

        def sb(name, shape, dt=F32):
            return ctx.enter_context(nc.sbuf_tensor(name, shape, dt))

        mem = sb("mem", [P, (REGIONS + 8) * 2048 + NCON])
        regions = mem[:, 0:(REGIONS + 8) * 2048].rearrange("p (r n) -> p r n", n=2048)
        con = mem[:, (REGIONS + 8) * 2048:]
        chunks = mem[:, (REGIONS + 9 - RING) * 2048:(REGIONS + 9) * 2048]
        vec = sb("vec", [P, NVEC])
        kcx = sb("kcx", [P, TT, 512])
        mod = sb("mod", [P, 6, KT, 2])
        rstd = sb("rstd", [P, 512])
        csil = sb("csil", [P, KT, 32])
        adar = sb("adar", [P, 256])
        dec = sb("dec", [P, 2, HEADS, 4])
        eps = sb("eps", [P, 1])[:, :]
        bank = [ctx.enter_context(nc.psum_tensor(f"bank{i}", [P, 512], F32)) for i in range(8)]

        def C(name, a=0, b=None, p=P):
            at, width = CON[name]
            return con[0:p, at + a:at + (width if b is None else b)]

        def V(name, i, p=P):
            return vec[0:p, VEC[name][0] + i:VEC[name][0] + i + 1]

        ring = regions[:, REGIONS:, :].rearrange("p r (k n) -> p r k n", k=KT)

        def region(r, n=1):
            at = PLACE.index(r)
            assert PLACE[at:at + n] == list(range(r, r + n))
            return regions[:, at:at + n, :].rearrange("p r n -> p (r n)")

        def place_loaded(s):
            j = s - 9
            if 0 <= j < 8:
                return sem(f"ring_loaded{j}"), 8 + (j < 4)
            return sem(f"chunk_loaded{s}"), 0

        def half(b, h):
            return bank[b][:, h * 256:h * 256 + 256]

        def by_parity(ap):
            return ap.rearrange("p (q o) -> p o q", o=2)

        def two(ap):
            return ap.rearrange("p (k t) -> p k t", k=2)

        def u_odd(c, a):
            return utok[:, 4 * c + 2 * a:4 * c + 2 * a + 2, :]

        ident, ones = C("ident"), C("ones")
        dft = C("dft").rearrange("p (a s f) -> p a s f", a=2, s=2)
        idft = C("idft").rearrange("p (a s n) -> p a s n", a=2, s=2)

        xT = region(0, 2).rearrange("p (k t) -> p k t", k=KT)
        xres, xctx = xT[:, :, 0:T], xT[:, :, T:2 * T]
        x1c = utok = act = xctx
        hx = region(2, 2).rearrange("p (k t) -> p k t", k=KT)
        hxx, hxc = hx[:, :, 0:T], hx[:, :, T:2 * T]
        uT = hxc
        spec = region(4, 2).rearrange("p (a f c) -> p a f c", a=2, f=TT)
        og = region(4).rearrange("p (m t) -> p m t", m=8)
        sma = region(5).rearrange("p (m t) -> p m t", m=8)
        qk = region(6).rearrange("p (m t) -> p m t", m=8)
        x0T = qk
        tok = region(6).rearrange("p (t c) -> p t c", t=TT)
        vx = region(7).rearrange("p (t c) -> p t c", t=TT)
        smb = region(7).rearrange("p (m t) -> p m t", m=8)
        vc = region(8).rearrange("p (t c) -> p t c", t=TT)
        sst = [region(r)[:, 0:1536].rearrange("p (d c v) -> p d c v", d=2, c=3) for r in (8, 10)]
        gc = region(9).rearrange("p (t d c) -> p t d c", t=TT, d=2)
        gx = region(10).rearrange("p (t d c) -> p t d c", t=TT, d=2)
        s0 = region(9).rearrange("p (h d v) -> p h d v", h=HEADS, d=2)
        win = region(11).rearrange("p (t c) -> p t c", t=TT)
        hsum = region(12).rearrange("p (t c) -> p t c", t=TT)
        hdif = region(13).rearrange("p (t c) -> p t c", t=TT)
        w4 = region(14)[0:64, :]
        kupc = region(11).rearrange("p (t d c) -> p t d c", t=TT, d=2)
        kupx = region(13).rearrange("p (t d c) -> p t d c", t=TT, d=2)
        qd = region(11).rearrange("p (d h t) -> p d h t", d=2, h=HEADS)
        ki = region(12).rearrange("p (d h t) -> p d h t", d=2, h=HEADS)
        sqo = region(12).rearrange("p (m t) -> p m t", m=8)
        rso = region(11)[:, 0:1024].rearrange("p (h t) -> p h t", h=HEADS)
        att = region(14).rearrange("p (h n) -> p h n", h=HEADS)
        tmp = region(14).rearrange("p (n c) -> p n c", n=4)
        zsb = region(7)[0:EMB, 0:256]
        hwsb = region(7)[0:64, 256:448]
        hact = region(7)[0:64, 512:1536].rearrange("p (n t) -> p n t", n=4)
        sq = region(8)[:, 0:1024].rearrange("p (n t) -> p n t", n=2)
        sq8 = region(8).rearrange("p (k t) -> p k t", k=KT)
        htmp = region(6).rearrange("p (n a c) -> p n a c", n=2, a=2)
        wrsb = region(12)[:, 0:256].rearrange("p (k n) -> p k n", k=KT)
        rT = region(12)[0:97, 256:768]
        wgksb = region(13)[0:97, 0:1024].rearrange("p (d n) -> p d n", d=2)
        glu, sg, lin, am = (region(8)[:, a:a + 512] for a in (0, 512, 1024, 1536))
        aT = region(9)[:, 0:512].rearrange("p (b h s) -> p b h s", b=4, h=2)
        ysb = region(9)[:, 512:1024]
        xe = region(9)[:, 1024:1536].rearrange("p (b h s) -> p b h s", b=4, h=2)
        xrow = kcx[:, 0, :]
        pick = region(9)[:, 1536:1792].rearrange("p (t s) -> p t s", t=TT)
        spread = region(9)[:, 1792:2048].rearrange("p (t s) -> p t s", t=TT)
        back = region(10)[:, 0:256]
        posI = region(10)[:, 256:384].rearrange("p (t i) -> p t i", t=TT)
        gateI = region(10)[:, 384:512].rearrange("p (t i) -> p t i", t=TT)
        T3 = region(10)[0:96, 512:576]
        Q = region(10)[0:32, 576:640]
        nitems = region(10)[0:1, 640:641].bitcast(I32)
        lasts = region(10)[0:1, 672:704].bitcast(I32)
        bounds = region(10)[0:1, 704:704 + E + 1].bitcast(I32)
        bsel = region(10)[0:96, 768:800].bitcast(BF16)
        bp = region(10)[0:96, 1024:2048].bitcast(BF16)
        bupsb = region(4)[0:96, :]
        R3 = region(5)
        wrt = R3[:, 0:256].rearrange("p (k e) -> p k e", k=KT)
        brt = R3[0:1, 256:288]
        logit = R3[:, 288:352].rearrange("p (t e) -> p t e", t=TT)
        m8 = R3[:, 352:368].rearrange("p (t e) -> p t e", t=TT)
        i8 = R3[:, 368:384].bitcast(U32).rearrange("p (t e) -> p t e", t=TT)
        if8 = R3[:, 384:400].rearrange("p (t e) -> p t e", t=TT)
        nm = R3[:, 400:402]
        ew = R3[:, 402:410].rearrange("p (t e) -> p t e", t=TT)
        es = R3[:, 410:412]
        gk = R3[:, 448:704].rearrange("p (t k e) -> p t k e", t=TT, k=4)
        sk = R3[:, 704:960].rearrange("p (t k e) -> p t k e", t=TT, k=4)
        sel = R3[:, 960:1152].rearrange("p (t e) -> p t e", t=TT)
        parts = R3[:, 1792:2048]
        gate_ = R3[:, 1152:1216].rearrange("p (t e) -> p t e", t=TT)
        cnt = R3[0:96, 1216:1224]
        posm = R3[0:32, 1280:1536]
        selT = R3[0:32, 1536:1792]
        gateT = kcx[0:32, 1, 0:T]
        bdn = xctx[0:32, 0:4, :]
        zero = region(7)[0:32, 0:256].bitcast(BF16)

        def squared(base, k):
            return sq8[:, k, :] if base else sq[:, k % 2, :]

        block = ctx.enter_context(nc.Block())

        def run_middle(steps, unit):
            for step in MIDDLE:
                if step[:-1] in PROJ:
                    unit(step[:-1], int(step[-1]))
                elif step in steps:
                    steps[step]()
                elif step[:-1] in steps:
                    steps[step[:-1]](int(step[-1]))


        @block.sync
        def _(sp):
            def unit(i, r, j, first):
                slot = 4 * r + j
                if not first:
                    sp.wait_ge(sem("unit_done"), 4 * i + 4 * r + j - 7)
                if isinstance(i, int):
                    src = wmix[i + r, j]
                else:
                    src = wmix[bass.ds(i + r, 1), j].rearrange("a p n -> (a p) n")
                sp.dma_start(ring[:, slot].rearrange("p k n -> p (k n)"),
                             src).then_inc(sem(f"ring_loaded{slot}"), 16)

            sp.dma_start(zsb, zt).then_inc(sem("z_loaded"), 16)
            sp.dma_start(hwsb, hw).then_inc(sem("hw_loaded"), 16)
            sp.dma_start(vec[:, :], vecs).then_inc(sem("vec_loaded"), 16)
            sp.dma_start(con[:, 2048:], cons[:, 2048:]).then_inc(sem("con_loaded"), 16)
            for q in range(4):
                sp.dma_start(xT[:, 2 * q:2 * q + 2, :],
                             xt[2 * q:2 * q + 2].rearrange("k p t -> p k t")).then_inc(sem(f"x_loaded{q}"), 16)
            sp.dma_start(w4, hw4).then_inc(sem("w4_loaded"), 16)
            sp.dma_start(win, window.rearrange("t p c -> p t c")).then_inc(sem("win_loaded"), 16)
            for j in range(4):
                unit(0, 0, j, True)
            sp.dma_start(con[:, 0:1024], cons[:, 0:1024]).then_inc(sem("dft_loaded"), 16)
            for j in range(4):
                unit(0, 1, j, True)
            with sp.Fori(2, 16, 2) as i:
                for r in range(2):
                    for j in range(4):
                        unit(i, r, j, False)
            for j in range(4):
                unit(16, 0, j, False)

            def chunk(e, c, where):
                src = wexp[e, c] if isinstance(e, int) else wexp[bass.ds(e, 1), c].rearrange(
                    "a p n -> (a p) n")
                sp.dma_start(chunks[:, where * 2048:where * 2048 + 2048],
                             src).then_inc(place_loaded(where)[0], 16)

            sp.wait_ge(sem("z_mm"), KT)
            chunk(0, 11, place(0, 11))
            for c in range(7, 11):
                sp.wait_ge(sem("unit_done"), 4 * 15 + c - 6)
                chunk(0, c, place(0, c))
            sp.wait_ge(sem("act_ready"), 1)
            for c in range(3):
                chunk(0, c, place(0, c))
            chunk(1, 5, place(1, 5))
            for c in range(3, 7):
                if c == 6:
                    sp.wait_ge(sem("bup_split"), 5)
                    chunk(1, 3, place(1, 3))
                sp.wait_ge(sem("unit_done"), 4 * 16 + c - 2)
                chunk(0, c, place(0, c))
            sp.wait_ge(sem("tok_turned"), 4)
            for c in (1, 2):
                chunk(1, c, place(1, c))
            sp.wait_ge(sem("itemcol_mm"), 1)
            for c in (4, 0):
                chunk(1, c, place(1, c))
            sp.wait_ge(sem("list_ready"), 3)

            def group(e, g, owner, place_e):
                last = sp.value_load(lasts[0:1, owner:owner + 1] if isinstance(owner, int) else
                                     lasts[0:1, bass.ds(owner, 1)], min_val=0, max_val=47)
                for n in range(GROUP):
                    c = GROUP * g + n
                    sp.wait_ge(sem("chunk_used"), CHUNKS * last + (CHUNKS - GROUP * (g + 1) + n + 1))
                    chunk(e, c, place(place_e, c))

            group(1, 1, 0, 1)
            with sp.Fori(0, E - 4, 3) as m:
                for s in range(2, 5):
                    group(m + s, 0, m + (s - 2), s)
                    group(m + s, 1, m + (s - 1), s)
            for k in range(KT):
                sp.wait_ge(sem("out_ready"), k + 1)
                sp.dma_start(out[k], hxx[:, k, :]).then_inc(sem("stored"), 16)
            sp.wait_ge(sem("stored"), 16 * KT)

        @block.tensor
        def _(pe):
            mm = pe.matmul

            def loaded(i, j):
                slot = 4 * (i % 2) + j
                pe.wait_ge(sem(f"ring_loaded{slot}"), 16 * (i // 2 + 1))
                return ring[:, slot]

            def projection(name, rhs, units=range(4), tokens=None, arriving=None):
                i = ROUNDS.index(name)
                before = PROJ[PROJ.index(name) - 1] if name != PROJ[0] else None
                for j in units:
                    w = loaded(i, j)
                    if ROUNDS[i - 1].startswith("ada") and j < 2:
                        pe.wait_ge(sem(("ada_rows", "mod_ready")[j]), int(ROUNDS[i - 1][3:]) + 1)
                    if before:
                        pe.wait_ge(sem(f"evac_{before}"), j + 1)
                    for m in range(2):
                        for k in range(KT):
                            if arriving and j == m == 0:
                                pe.wait_ge(*arriving(k))
                            last = mm(half(j, m), w[:, k, m * P:m * P + P], rhs[:, k, :],
                                      start=(k == 0), stop=(k == KT - 1))
                    if tokens and j >= 2:
                        pe.wait_ge(sem("hx_ready"), 2 * KT)
                        last = by_token(w, hxc, 4 + j)
                    last.then_inc(sem("unit_done"), 1)

            def by_token(w, lhs, b):
                for t in range(TT):
                    for k in range(KT):
                        last = mm(half(b, t), lhs[:, k, t * P:t * P + P], w[:, k, :],
                                  start=(k == 0), stop=(k == KT - 1))
                return last

            def mean_square(base, b, n, part=range(KT)):
                for k in part:
                    pe.wait_ge(sem("sq_ready"), base + k + 1)
                    mm(bank[b][:, 0:n], ones, squared(base, k), start=(k == 0),
                       stop=(k == KT - 1)).then_inc(sem("sq_used"), 1)

            def rows(s):
                i = ROUNDS.index(f"ada{s}")
                w = [loaded(i, j) for j in range(4)]
                if s >= 2:
                    pe.wait_ge(sem(f"evac_{ROUNDS[i - 1]}"), 1)
                for k in range(KT):
                    for j in range(4):
                        last = mm(bank[0][32 * j:32 * j + 32, 0:256], csil[:, k, :], w[j][:, k, :],
                                  start=(k == 0), stop=(k == KT - 1))
                        if k == KT - 1:
                            last.then_inc(sem("unit_done"), 1)

            def turn(s):
                if s >= 2:
                    pe.wait_ge(sem(f"evac_{ROUNDS[ROUNDS.index(f'ada{s}') - 1]}"), 2)
                pe.wait_ge(sem("ada_rows"), s + 1)
                for j in range(2):
                    last = pe.transpose(bank[1][:, j * P:j * P + P], adar[:, j * P:j * P + P], ident)
                last.then_inc(sem("ada_turned"), 1)

            pe.wait_ge(sem("z_loaded"), 16)
            pe.wait_ge(sem("hw_loaded"), 16)
            mm(bank[4][0:64, 0:256], hwsb[0:EMB, 0:64], zsb, start=True,
               stop=True).then_inc(sem("mlp_mm"), 1)
            pe.wait_ge(sem("con_loaded"), 16)
            for n in range(2):
                pe.wait_ge(sem("mlp_sin"), n + 1)
                mm(bank[4][0:64, 0:256], hwsb[:, 64 + 64 * n:128 + 64 * n], hact[:, 3, :], start=True,
                   stop=True).then_inc(sem("mlp_mm"), 1)
                mean_square(0, 5, 512, range(4 * n, 4 * n + 4))
            pe.wait_ge(sem("mlp_sin"), 3)
            pe.wait_ge(sem("w4_loaded"), 16)
            for n in range(8):
                t, c = n // 4, (n % 4) // 2 + 2 * (n % 2)
                if n == 6:
                    pe.wait_ge(sem("rms"), 1)
                mm(bank[4 * t + c][:, :], hact[:, 3, t * P:t * P + P], w4[:, c * 512:c * 512 + 512],
                   start=True, stop=True).then_inc(sem("taps_mm"), 1)

            def spectrum(b):
                a, o, c = b // 4, b % 4 // 2, b % 2
                pe.wait_ge(sem(("taps_sum", "pool_step")[a]), 4)
                mm(bank[b][:, :], dft[:, a, o, :], (hsum, hdif)[a][:, o, c * 512:c * 512 + 512],
                   start=True, stop=True).then_inc(sem("spec_mm"), 1)

            pe.wait_ge(sem("csil_ready"), 1)
            pe.wait_ge(sem("taps_win"), 3)
            rows(0)
            pe.wait_ge(sem("dft_loaded"), 16)
            spectrum(SPECTRUM[0])
            turn(0)
            for b in SPECTRUM[1:]:
                if b == 1:
                    pe.wait_ge(sem("mod_ready"), 1)
                spectrum(b)
            pe.wait_ge(sem("spec_ready"), 2 * PARTS.index((0, 0)) + 2)
            rows(1)
            pe.wait_ge(sem("spec_ready"), 2 * PARTS.index((0, 1)) + 2)
            turn(1)

            pe.wait_ge(sem("spec_ready"), 8)
            projection("qk", hxx, tokens=True, arriving=lambda k: (sem("hx_ready"), k + 1))
            pe.wait_ge(sem("wr_loaded"), 16)
            for k in range(KT):
                g = k % 3
                last = mm(bank[4][32 * g:32 * g + 32, :], wrsb[:, k, :], hx[:, k, :], start=(k < 3),
                          stop=(k >= KT - 3))
            last.then_inc(sem("low_mm"), 1)
            i = ROUNDS.index("v")
            for j in range(4):
                w = loaded(i, j)
                pe.wait_ge(sem("evac_qk"), j + 1)
                by_token(w, hxx, j)
                if j == 0:
                    pe.wait_ge(sem("low_ready"), 2)
                elif j >= 2:
                    pe.wait_ge(sem("kc_ready"), j - 1)
                by_token(w, hxc, 4 + j).then_inc(sem("unit_done"), 1)
            after, earlier, every = C("after"), C("before"), C("all16")

            def gate(n):
                t, d = n // 2, n % 2
                if n == 0:
                    pe.wait_ge(sem("wgk_loaded"), 16)
                pe.wait_ge(sem("evac_vc" if n < 4 else "g_ready"), n % 4 + 1)
                mm(bank[4 + n % 4][:, :], rT[:, t * P:t * P + P], wgksb[:, d, :], start=True,
                   stop=True).then_inc(sem("gate_mm"), 1)

            def crest():
                pe.wait_ge(sem("g_ready"), 8)
                for n, terms in enumerate(([(after, 0), (every, 1)], [(earlier, 0)],
                                           [(after, 1)], [(every, 0), (earlier, 1)])):
                    for m, (tri, s) in enumerate(terms):
                        last = mm(bank[4 + n][:, :], tri, gc[:, s, n % 2, :], start=(m == 0),
                                  stop=(m == len(terms) - 1))
                    last.then_inc(sem("crest_mm"), 1)

            def initial():
                pe.wait_ge(sem("kupc_ready"), 4)
                for h in range(HEADS):
                    for d in range(2):
                        for t in range(TT):
                            last = mm(half(4 + h, d), kupc[:, t, d, h * DK:h * DK + DK],
                                      vc[:, t, h * DV:h * DV + DV], start=(t == 0), stop=(t == TT - 1))
                    last.then_inc(sem("s0_mm"), 1)

            def decay():
                for d in range(2):
                    for h in range(HEADS):
                        n = d * HEADS + h
                        if n % 2 == 0:
                            pe.wait_ge(sem("s0_ready"), n // 2 + 1)
                        for t in range(TT):
                            last = mm(half(4 + n // 2, n % 2)[:, t * P:t * P + P],
                                      gx[:, t, d, h * DK:h * DK + DK],
                                      C("mask", d * P, d * P + P), start=True, stop=True)
                        if n % 2:
                            last.then_inc(sem("decay_mm"), 1)

            def kturn():
                for t in range(TT):
                    pe.wait_ge(sem("decay_read"), t + 1)
                    for h in range(HEADS):
                        last = pe.transpose(bank[4 + t][:, h * P:h * P + P],
                                            qk[:, 4 + h, t * P:t * P + P], ident)
                    last.then_inc(sem("k_turned"), 1)

            def rest():
                for n in (2, 3, 0, 1):
                    t, d = n // 2, n % 2
                    if n < 2:
                        pe.wait_ge(sem("ktok_ready"), n + 1)
                    else:
                        pe.wait_ge(sem("decay_read"), n + 1)
                    mm(bank[4 + n][:, :], C("rest", d * P, d * P + P), gx[:, t, d, :], start=True,
                       stop=True).then_inc(sem("rest_mm"), 1)

            def uturn():
                pe.wait_ge(sem("u_ready"), 1)
                pe.wait_ge(sem("rest_read"), 4)
                for b in range(4):
                    for c in range(2 * b, 2 * b + 2):
                        for o in range(2):
                            last = pe.transpose(bank[4 + b][:, (c % 2) * 256 + o * P:][:, 0:P],
                                                by_parity(uT[:, c, :])[:, o, :], ident)
                    last.then_inc(sem("u_turned"), 1)

            def uspec(c):
                pe.wait_ge(sem("utok_ready"), 4)
                if c:
                    pe.wait_ge(sem("u_read"), c)
                for a in range(2):
                    for o in range(2):
                        last = mm(bank[4 + 2 * a + o][:, :], dft[:, a, o, :],
                                  utok[:, 4 * c:4 * c + 4, o * P:o * P + P], start=True, stop=True)
                last.then_inc(sem("u_spec"), 1)

            def scores():
                pe.wait_ge(sem("qdki_ready"), 4)
                pe.wait_ge(sem("prod_ready"), 2)
                for h in range(HEADS):
                    for t in range(TT):
                        for d in range(2):
                            last = mm(bank[4 + h][:, (2 * t + d) * P:(2 * t + d) * P + P],
                                      ki[:, d, h, t * P:t * P + P], qd[:, d, h, t * P:t * P + P],
                                      start=True, stop=True)
                    last.then_inc(sem("att_mm"), 1)

            def inverse():
                for c in range(KT):
                    if c % 2 == 0:
                        pe.wait_ge(sem("att_ready"), c // 2 + 1)
                    for o in range(2):
                        for a in range(2):
                            last = mm(half(4 + c // 2, c % 2)[:, o * P:o * P + P],
                                      spec[:, a, o, c * P:c * P + P], idft[:, a, o, :],
                                      start=(a == 0), stop=(a == 1))
                    last.then_inc(sem("z_mm"), 1)

            def update(h):
                if h:
                    pe.wait_ge(sem("state_ready"), 2 * h)
                    pe.wait_ge(sem("o_read"), 4 * h)
                else:
                    pe.wait_ge(sem("kupx_ready"), 4)
                    pe.wait_ge(sem("z_read"), 8)
                for d, c, b, m in ((0, 0, 4, 0), (1, 3, 6, 1), (0, 1, 6, 0), (1, 2, 5, 0),
                                   (0, 2, 4, 1), (1, 1, 7, 0)):
                    t, r = c // 2, 64 * (c % 2)
                    mm(half(b, m), kupx[r:r + CHUNK, t, d, h * DK:h * DK + DK],
                       vx[r:r + CHUNK, t, h * DV:h * DV + DV], start=True,
                       stop=True).then_inc(sem("upd_mm"), 1)

            def output(h):
                pe.wait_ge(sem("state_ready"), 2 * h + 2)
                for v in range(2):
                    dst = half(5 + 2 * v, 1)
                    vs = slice(v * P, v * P + P)
                    for t in range(TT):
                        for d in range(2):
                            mm(dst[:, t * P:t * P + P], vx[:, t, h * DV + v * P:h * DV + v * P + P],
                               att[:, h, (2 * t + d) * P:(2 * t + d) * P + P],
                               start=(t == 0 and d == 0), stop=False, skip_group_check=True)
                    for d in range(2):
                        for c in range(4):
                            if d == 0:
                                st = s0[:, h, 0, vs] if c == 0 else sst[h % 2][:, 0, c - 1, vs]
                            else:
                                st = s0[:, h, 1, vs] if c == 3 else sst[h % 2][:, 1, c, vs]
                            last = mm(dst[:, c * CHUNK:c * CHUNK + CHUNK], st,
                                      qd[:, d, h, c * CHUNK:c * CHUNK + CHUNK], start=False,
                                      stop=(d == 1 and c == 3), skip_group_check=True)
                    last.then_inc(sem("o_mm"), 1)

            def onorm():
                pe.wait_ge(sem("o_read"), 16)
                for h in range(HEADS):
                    for v in range(2):
                        last = mm(half(4 + h // 2, h % 2), ones, sqo[:, 2 * h + v, :], start=(v == 0),
                                  stop=(v == 1))
                    if h % 2:
                        last.then_inc(sem("onorm_mm"), 1)

            run_middle(dict(gate=gate, crest=crest, s0=initial, decay=decay, kturn=kturn, rest=rest,
                            uturn=uturn, uspec=uspec, att=scores, inverse=inverse, update=update,
                            output=output, onorm=onorm, rows=rows, turn=turn),
                       lambda name, j: projection(name, hxx, units=[j]))
            pe.wait_ge(sem("act_ready"), 1)
            projection("gla", act)
            pe.wait_ge(sem("z_ready"), 1)
            projection("hyo", uT)
            projection("out", sma, units=range(3), arriving=lambda k: (sem("evac_hyo"), k // 2 + 1))
            pe.wait_ge(sem("evac_out"), 1)
            mean_square(8, 0, T, range(4))
            projection("out", sma, units=[3])
            mean_square(8, 0, T, range(4, 8))
            pe.wait_ge(sem("wrt_loaded"), 16)
            pe.wait_ge(sem("brt_loaded"), 16)
            pe.wait_ge(sem("evac_out"), 4)
            for k in range(KT):
                pe.wait_ge(sem("hx2_ready"), k + 1)
                g = k % 4
                last = mm(bank[1][32 * g:32 * g + 32, 0:T], wrt[:, k, :], hxx[:, k, :], start=(k < 4),
                          stop=(k >= 4))
            last.then_inc(sem("parts_mm"), 1)
            pe.wait_ge(sem("onorm_read"), 2)

            def turn_tokens(t):
                for k in range(KT):
                    last = pe.transpose(bank[4 + 2 * t + k // 4][:, (k % 4) * P:(k % 4) * P + P],
                                        hxx[:, k, t * P:t * P + P], ident)
                    if k % 4 == 3:
                        last.then_inc(sem("tok_turned"), 1)

            turn_tokens(0)
            pe.wait_ge(sem("parts_ready"), 1)
            for t in range(TT):
                dst = bank[1][:, t * E:t * E + E]
                mm(dst, ones[0:1, :], brt, start=True, stop=False)
                last = mm(dst, parts[:, t * P:t * P + P], C("stack"), start=False, stop=True)
            last.then_inc(sem("logit_mm"), 1)
            turn_tokens(1)
            pe.wait_ge(sem("sel_ready"), 1)
            cnt_ps, start_ps, n_ps, ends_ps = (
                bank[1][0:96, 64:65], bank[1][0:96, 66:67], bank[1][0:1, 68:69], bank[1][0:1, 96:128])
            for t in range(TT):
                last = mm(cnt_ps, sel[:, t, :], ones[:, 0:1], start=(t == 0), stop=(t == TT - 1))
            last.then_inc(sem("count_mm"), 1)
            for t in range(TT):
                last = pe.transpose(bank[2][0:32, t * P:t * P + P], sel[:, t, 0:E], ident)
            last.then_inc(sem("turned_sel"), 1)
            pe.wait_ge(sem("rms"), 2)
            mm(bank[0][0:32, 0:P], sel[:, 0, 0:E], earlier, start=True, stop=True)
            mm(bank[0][0:32, P:T], sel[:, 0, 0:E], every, start=True, stop=False)
            mm(bank[0][0:32, P:T], sel[:, 1, 0:E], earlier, start=False,
               stop=True).then_inc(sem("place_mm"), 1)
            pe.wait_ge(sem("pass_ready"), 1)
            mm(start_ps, C("tri", p=E), cnt[0:E, 3:4], start=True, stop=True)
            mm(n_ps, cnt[0:E, 3:4], ones[0:E, 0:1], start=True, stop=True).then_inc(sem("start_mm"), 1)
            pe.wait_ge(sem("gate_ready"), 1)
            for t in range(TT):
                last = pe.transpose(bank[3][0:32, t * P:t * P + P], gate_[:, t, :], ident)
            last.then_inc(sem("turned_gate"), 1)
            pe.wait_ge(sem("zero_ready"), 1)
            for b in range(4):
                pe.wait_ge(sem("tok_ready"), b + 1)
                mm(bank[4 + b][:, :], zero[:, 0:P], zero, start=True, stop=False, skip_group_check=True)
            pe.wait_ge(sem("items_ready"), 1)
            mm(ends_ps, cnt[0:E, 5:6], ident[0:E, 0:E], start=True, stop=True).then_inc(sem("ends_mm"), 1)
            for t in range(TT):
                mm(bank[0][:, 256 + t * MAXI:][:, 0:MAXI], posm[:, t * P:t * P + P], T3[0:E, :],
                   start=True, stop=False)
                mm(bank[0][:, 256 + t * MAXI:][:, 0:MAXI], ones[0:E, :], Q, start=False, stop=True)
            for t in range(TT):
                last = mm(bank[0][:, 384 + t * MAXI:][:, 0:MAXI], gateT[:, t * P:t * P + P], T3[0:E, :],
                          start=True, stop=True)
            last.then_inc(sem("itemcol_mm"), 1)
            def rows():
                for t in range(TT):
                    for g in range(2):
                        last = mm(bank[3][64 * g:64 * g + 64, :], pick[:, t, 0:SLOTS],
                                  tok[:, t, g * 512:g * 512 + 512], start=(t == 0), stop=(t == TT - 1))
                last.then_inc(sem("gathered"), 1)

            def turn_rows():
                for b in range(4):
                    last = pe.transpose(bank[3][:, b * P:b * P + P], xrow[:, b * P:b * P + P], ident)
                last.then_inc(sem("rows_turned"), 1)

            def scatter(blocks):
                for c in blocks:
                    g, at = c // 4, c % 4 * P
                    last = mm(half(4 + c // 2, c % 2), ysb[64 * g:64 * g + 64, at:at + P],
                              back[64 * g:64 * g + 64, :], start=False, stop=False,
                              skip_group_check=True)
                last.then_inc(sem("scattered"), 1)

            pe.wait_ge(sem("tok_ready"), 4)
            pe.wait_ge(sem("pick_ready"), 1)
            rows()
            pe.wait_ge(sem("xrow_ready"), 1)
            turn_rows()
            pe.wait_ge(sem("bup_split"), 5)
            pe.wait_ge(sem("list_ready"), 3)

            def item(i, m, s):

                def weights(c):
                    loaded_sem, before = place_loaded(place(s, c))
                    pe.wait_ge(loaded_sem, 32 * m + 16 * (before + turn_of(s, c)))
                    return chunks[:, place(s, c) * 2048:place(s, c) * 2048 + 2048]

                pe.wait_ge(sem("xe_ready"), i + 1)
                pe.wait_ge(sem("bsel_ready"), i + 1)
                pe.wait_ge(sem("aT_ready"), i + 1)
                pe.wait_ge(sem("back_ready"), i + 1)
                for b in range(2):
                    for g in range(2):
                        mm(bank[b][64 * g:64 * g + 64, :], bsel,
                           bp[:, (2 * g + b) * 512:(2 * g + b) * 512 + 512], start=True, stop=False)
                for k in range(KT):
                    w = weights(k)
                    for b in range(2):
                        for g in range(2):
                            last = mm(bank[b][64 * g:64 * g + 64, :], xe[:, k % 4, k // 4, :],
                                      w[:, (2 * g + b) * 512:(2 * g + b) * 512 + 512],
                                      start=False, stop=(k == KT - 1))
                    last.then_inc(sem("chunk_used"), 1)
                pe.wait_ge(sem("y_ready"), i + 1)
                scatter(range(KT))
                pe.wait_ge(sem("a_ready"), i + 1)
                for b in range(4):
                    last = pe.transpose(bank[0][:, b * P:b * P + P], am[:, b * P:b * P + P], ident)
                last.then_inc(sem("turned"), 1)
                pe.wait_ge(sem("pick_ready"), i + 2)
                rows()
                pe.wait_ge(sem("spread_ready"), i + 1)
                for t in range(TT):
                    last = pe.transpose(bank[1][:, t * P:t * P + P], spread[:, t, :], ident)
                last.then_inc(sem("spread_turned"), 1)
                pe.wait_ge(sem("aT_ready"), i + 2)
                for u in range(4):
                    w = weights(8 + u)
                    for a in range(2):
                        kk = 2 * u + a
                        for g in range(2):
                            last = mm(bank[2][64 * g:64 * g + 64, :], aT[:, kk % 4, kk // 4, :],
                                      w[:, a * D + g * 512:a * D + g * 512 + 512],
                                      start=(kk == 0), stop=(kk == 7))
                    last.then_inc(sem("chunk_used"), 1)
                    if u == 1:
                        pe.wait_ge(sem("xrow_ready"), i + 2)
                        turn_rows()

            def expert(m, s):
                first, end = (pe.value_load(bounds[0:1, bass.ds(3 * m + (s + n), 1)], min_val=n,
                                            max_val=48) for n in range(2))
                with pe.Fori(first, end) as i:
                    item(i, m, s)

            for part in ((0, 6), (6, E // 3)):
                with pe.Fori(*part) as m:
                    for s in range(3):
                        expert(m, s)
                if part[0] == 0:
                    pe.wait_ge(sem("bdn_loaded"), 16)
                    for c in range(KT):
                        mm(half(4 + c // 2, c % 2), bdn[:, c // 2, c % 2 * P:c % 2 * P + P], gateT,
                           start=False, stop=False, skip_group_check=True)
            for s in range(E % 3):
                expert(E // 3, s)
            n = pe.value_load(nitems, min_val=E, max_val=48)
            pe.wait_ge(sem("y_ready"), n + 1)
            pe.wait_ge(sem("back_ready"), n + 1)
            for c in range(0, KT, 2):
                scatter((c, c + 1))
            mean_square(16, 0, T)

        @block.scalar
        def _(ac):
            act_fn = ac.activation

            def squares(base, src, n, part):
                for k in part:
                    if base == 0 and k % 2 == 0:
                        ac.wait_ge(sem(f"x_loaded{k // 2}"), 16)
                    if base + k >= 2:
                        ac.wait_ge(sem("sq_used"), base + k - 1)
                    act_fn(squared(base, k), src[:, k, :], ACT.Square).then_inc(sem("sq_ready"), 1)

            def root(base, b, n):
                ac.wait_ge(sem("sq_used"), base + KT)
                ac.wait_ge(sem("eps_ready"), 1)
                act_fn(rstd[:, 0:n], bank[b][:, 0:n], ACT.Sqrt, scale=1.0 / D,
                       bias=eps).then_inc(sem("rms"), 1)

            ac.wait_ge(sem("vec_loaded"), 16)
            ac.wait_ge(sem("csil_zero"), 1)
            for r, name in enumerate(("c", "cctx")):
                at = VEC[name][0]
                act_fn(csil[:, :, 2 + r], vec[:, at:at + KT], ACT.Sigmoid).then_inc(sem("csig"), 1)

            def sine(n):
                ac.wait_ge(sem("mlp_arg"), n + 1)
                act_fn(hact[:, 3, :], hact[:, 2, :], ACT.Sin).then_inc(sem("mlp_sin"), 1)

            sine(0)
            squares(0, xT, 512, range(4))
            sine(1)
            squares(0, xT, 512, range(4, 6))
            sine(2)
            squares(0, xT, 512, range(6, 8))
            root(0, 5, 512)

            def rows(s):
                ac.wait_ge(sem("unit_done"), 4 * ROUNDS.index(f"ada{s}") + 4)
                if s:
                    ac.wait_ge(sem("ada_turned"), s)
                act_fn(adar[:, :], half(0, 0), ACT.Copy).then_inc(sem("ada_rows"), 1)

            rows(0)
            for a, c in PARTS:
                b = 4 * a + 2 + c
                ac.wait_ge(sem("spec_mm"), SPECTRUM.index(b) + 1)
                act_fn(spec[:, a, 1, c * 512:c * 512 + 512], bank[b][:, :],
                       ACT.Copy).then_inc(sem("odd_ready"), 1)
            rows(1)
            ac.dma_start(wrsb, wr).then_inc(sem("wr_loaded"), 16)
            ac.dma_start(wgksb, wgk).then_inc(sem("wgk_loaded"), 16)

            def unit_done(name, j):
                ac.wait_ge(sem("unit_done"), 4 * ROUNDS.index(name) + j + 1)

            for j in range(4):
                unit_done("qk", j)
                act_fn(qk[:, 2 * j:2 * j + 2, :].rearrange("p m t -> p (m t)"), bank[j][:, :], ACT.Copy,
                       scale=float(DK) ** -0.5 if j < 2 else 1.0).then_inc(sem("evac_qk"), 1)
            for j in range(4):
                unit_done("v", j)
                act_fn(vx[:, :, j * 256:j * 256 + 256], bank[j][:, :].rearrange("p (t c) -> p t c", t=TT),
                       ACT.Copy).then_inc(sem("evac_v"), 1)

            def gate(n):
                buf = tmp[:, n % 4, :]
                ac.wait_ge(sem("gate_mm"), n + 1)
                if n >= 4:
                    ac.wait_ge(sem("g_ready"), n - 3)
                act_fn(buf, bank[4 + n % 4][:, :], ACT.Abs).then_inc(sem("gate_abs"), 1)
                ac.wait_ge(sem("gate_abs"), n + 1)
                act_fn(buf, buf, ACT.Exp, scale=-1.0).then_inc(sem("gate_exp"), 1)
                ac.wait_ge(sem("gate_exp"), n + 1)
                act_fn(buf, buf, ACT.Ln, bias=1.0).then_inc(sem("gate_ln"), 1)

            def crest():
                for n in range(4):
                    ac.wait_ge(sem("crest_mm"), n + 1)
                    act_fn(kupc[:, n // 2, n % 2, :], bank[4 + n][:, :],
                           ACT.Exp).then_inc(sem("crest_read"), 1)

            def initial():
                for h in range(HEADS):
                    ac.wait_ge(sem("s0_mm"), h + 1)
                    act_fn(s0[:, h].rearrange("p d v -> p (d v)"), bank[4 + h][:, :],
                           ACT.Copy).then_inc(sem("s0_ready"), 1)

            def decay():
                for n in range(4):
                    ac.wait_ge(sem("decay_mm"), n + 1)
                    d, h = n // 2, 2 * (n % 2)
                    act_fn(qd[:, d, h:h + 2, :].rearrange("p h t -> p (h t)"), bank[4 + n][:, :],
                           ACT.Exp).then_inc(sem("exp_pos"), 1)
                    act_fn(ki[:, d, h:h + 2, :].rearrange("p h t -> p (h t)"), bank[4 + n][:, :],
                           ACT.Exp, scale=-1.0).then_inc(sem("decay_read"), 1)

            def kturn():
                ac.wait_ge(sem("kupc_ready"), 4)
                for t in range(TT):
                    ac.wait_ge(sem("k_turned"), t + 1)
                    act_fn(kcx[:, t, :], bank[4 + t][:, :], ACT.Copy).then_inc(sem("ktok_ready"), 1)

            def rest():
                for m, n in enumerate((2, 3, 0, 1)):
                    ac.wait_ge(sem("rest_mm"), m + 1)
                    act_fn(kupx[:, n // 2, n % 2, :], bank[4 + n][:, :],
                           ACT.Exp).then_inc(sem("rest_read"), 1)

            def uturn():
                for b in range(4):
                    ac.wait_ge(sem("u_turned"), b + 1)
                    act_fn(utok[:, 2 * b:2 * b + 2, :],
                           bank[4 + b][:, :].rearrange("p (c t) -> p c t", c=2),
                           ACT.Copy).then_inc(sem("utok_ready"), 1)

            def uspec(c):
                ac.wait_ge(sem("u_spec"), c + 1)
                for a in range(2):
                    act_fn(u_odd(c, a), two(bank[5 + 2 * a][:, :]), ACT.Copy).then_inc(sem("odd_ready"), 1)

            def output(h):
                for v in range(2):
                    ac.wait_ge(sem("o_mm"), 2 * h + v + 1)
                    act_fn(act[:, 2 * h + v, :], half(5 + 2 * v, 1), ACT.Copy).then_inc(sem("o_read"), 1)
                    act_fn(sqo[:, 2 * h + v, :], half(5 + 2 * v, 1), ACT.Square).then_inc(sem("o_read"), 1)

            def onorm():
                for n in range(2):
                    ac.wait_ge(sem("onorm_mm"), n + 1)
                    act_fn(rso[:, 2 * n:2 * n + 2, :].rearrange("p h t -> p (h t)"), bank[4 + n][:, :],
                           ACT.Sqrt, scale=1.0 / DV, bias=eps).then_inc(sem("onorm_read"), 1)

            convs = {"hv": (0, uT), "hx1": (8, x1c), "hx0": (16, x0T)}

            def unit(name, j):
                unit_done(name, j)
                if name in convs:
                    base, dst = convs[name]
                    if name == "hx0":
                        ac.wait_ge(sem("qdki_ready"), 4)
                    for m in range(2):
                        c = 2 * j + m
                        act_fn(dst[:, c, :], half(j, m), ACT.Identity, scale=V("cw", 24 + base + c),
                               bias=V("cb", base + c)).then_inc(sem("conv_mid"), 1)
                else:
                    if name == "og":
                        ac.wait_ge(sem("z_mm"), 8)
                    dst = {"og": og, "ma": sma, "mb": smb}[name]
                    act_fn(dst[:, 2 * j:2 * j + 2, :].rearrange("p m t -> p (m t)"), bank[j][:, :],
                           ACT.Sigmoid).then_inc(sem("og_sig" if name == "og" else f"evac_{name}"), 1)

            run_middle(dict(gate=gate, crest=crest, s0=initial, decay=decay, kturn=kturn, rest=rest,
                            uturn=uturn, uspec=uspec, output=output, onorm=onorm, rows=rows), unit)
            ac.wait_ge(sem("act_ready"), 1)
            for q in range(3):
                ac.dma_start(bupsb[32 * q:32 * q + 32, :], bup).then_inc(sem("bup_loaded"), 16)
            act_fn(csil[:, 0, 0:1], eps, ACT.Sqrt)
            for k in range(KT):
                if k % 2 == 0:
                    ac.wait_ge(sem("evac_out"), k // 2 + 1)
                act_fn(squared(8, k), xres[:, k, :], ACT.Square).then_inc(sem("sq_ready"), 1)
            root(8, 0, T)
            for k in range(KT):
                ac.wait_ge(sem("hx2_scaled"), k + 1)
                act_fn(hxx[:, k, :], hxx[:, k, :], ACT.Identity,
                       bias=mod[:, 3, k, 0:1]).then_inc(sem("hx2_ready"), 1)
            ac.wait_ge(sem("parts_mm"), 1)
            act_fn(parts, half(1, 0), ACT.Copy).then_inc(sem("parts_ready"), 1)
            act_fn(csil[:, 1, 0:1], eps, ACT.Exp)
            for b in range(4):
                ac.wait_ge(sem("tok_turned"), b + 1)
                act_fn(tok[:, b // 2, (b % 2) * 512:(b % 2) * 512 + 512], bank[4 + b][:, :],
                       ACT.Copy).then_inc(sem("tok_ready"), 1)
            ac.wait_ge(sem("top_ready"), 1)
            for t in range(TT):
                act_fn(ew[:, t, :], m8[:, t, 0:4], ACT.Exp, bias=nm[:, t:t + 1],
                       accum_out=es[:, t:t + 1]).then_inc(sem("top_exp"), 1)
            ac.wait_ge(sem("list_ready"), 3)
            act_fn(back, C("mask", 0, T), ACT.Copy, scale=0.0).then_inc(sem("back_ready"), 1)
            act_fn(ysb, C("mask"), ACT.Copy, scale=0.0).then_inc(sem("y_ready"), 1)

            def rows():
                act_fn(xrow, bank[3][:, :], ACT.Copy).then_inc(sem("xrow_ready"), 1)

            def turned_rows():
                act_fn(xe.rearrange("p b h s -> p (b h s)"), bank[3][:, :],
                       ACT.Copy).then_inc(sem("xe_ready"), 1)

            ac.wait_ge(sem("gathered"), 1)
            rows()
            ac.wait_ge(sem("rows_turned"), 1)
            turned_rows()
            n = ac.value_load(nitems, min_val=E, max_val=48)
            with ac.Fori(0, n) as i:
                ac.wait_ge(sem("glu_ready"), i + 1)
                act_fn(sg, glu, ACT.Sigmoid, scale=ALPHA).then_inc(sem("sg_ready"), 1)
                ac.wait_ge(sem("gathered"), i + 2)
                rows()
                ac.wait_ge(sem("spread_turned"), i + 1)
                act_fn(back, half(1, 0), ACT.Copy).then_inc(sem("back_ready"), 1)
                ac.wait_ge(sem("rows_turned"), i + 2)
                turned_rows()
                ac.wait_ge(sem("chunk_used"), CHUNKS * i + CHUNKS)
                act_fn(ysb, bank[2][:, :], ACT.Copy).then_inc(sem("y_ready"), 1)
            act_fn(csil[:, 2, 0:1], eps, ACT.Sqrt)
            for k in range(KT):
                ac.wait_ge(sem("x2_ready"), k + 1)
                act_fn(squared(16, k), xres[:, k, :], ACT.Square).then_inc(sem("sq_ready"), 1)
            root(16, 0, T)

        @block.vector
        def _(ve):
            steps = [0]

            def link(ins):
                steps[0] += 1
                ins.then_inc(sem("vector_step"), 1)
                ve.wait_ge(sem("vector_step"), steps[0])

            def grid(ap):
                return ap.rearrange("p (r w) -> p r w", w=64)

            ve.memset(eps, EPS).then_inc(sem("eps_ready"), 1)
            ve.memset(csil[:, :, :], 0.0).then_inc(sem("csil_zero"), 1)
            ve.wait_ge(sem("vec_loaded"), 16)
            for n in range(3):
                ve.wait_ge(sem("mlp_mm"), n + 1)
                link(ve.tensor_scalar(hact[:, 0, :], bank[4][0:64, 0:256], V("hmlp", n, 64),
                                      V("hmlp", 3, 64), ALU.add, ALU.mult))
                link(ve.tensor_scalar(hact[:, 1, :], hact[:, 0, :], 1.0 / (2 * np.pi), MAGIC,
                                      ALU.mult, ALU.add))
                link(ve.tensor_scalar(hact[:, 1, :], hact[:, 1, :], MAGIC, None, ALU.subtract))
                link(ve.scalar_tensor_tensor(out=hact[:, 2, :], in0=hact[:, 1, :], scalar=-TWO_PI_HI,
                                             in1=hact[:, 0, :], op0=ALU.mult, op1=ALU.add))
                link(ve.scalar_tensor_tensor(out=hact[:, 2, :], in0=hact[:, 1, :], scalar=-TWO_PI_LO,
                                             in1=hact[:, 2, :], op0=ALU.mult, op1=ALU.add))
                ve.tensor_scalar(hact[:, 2, :], hact[:, 2, :], PI, -PI, ALU.min,
                                 ALU.max).then_inc(sem("mlp_arg"), 1)
                if n == 1:
                    ve.wait_ge(sem("csig"), 2)
                    for r, name in enumerate(("c", "cctx")):
                        at = VEC[name][0]
                        ins = ve.tensor_tensor(csil[:, :, r], csil[:, :, 2 + r], vec[:, at:at + KT],
                                               ALU.mult)
                    link(ins)
                    ve.memset(csil[:, :, 2:4], 0.0).then_inc(sem("csil_ready"), 1)
            ve.wait_ge(sem("win_loaded"), 16)
            for n in range(4):
                t, c = n // 2, n % 2
                cs = slice(c * 512, c * 512 + 512)
                ve.wait_ge(sem("taps_mm"), 2 * n + 2)
                if n >= 2:
                    ve.wait_ge(sem("taps_sum"), n - 1)
                    ve.wait_ge(sem("pool_step"), n - 1)
                fwd, bwd = htmp[:, n % 2, 0, :], htmp[:, n % 2, 1, :]
                ve.tensor_tensor(fwd, bank[4 * t + c][:, :], win[:, t, cs], ALU.mult)
                ins = ve.tensor_tensor(bwd, bank[4 * t + 2 + c][:, :], win[:, t, cs], ALU.mult)
                if t == 0:
                    link(ins)
                    ins = ve.memset(bwd[0:1, :], 0.0)
                ins.then_inc(sem("taps_win"), 1)
                ve.wait_ge(sem("taps_win"), n + 1)
                ve.tensor_tensor(hsum[:, t, cs], fwd, bwd, ALU.add).then_inc(sem("taps_sum"), 1)
            def turn(s):
                ve.wait_ge(sem("ada_turned"), s + 1)
                at = VEC["bada"][0] + s * KT
                bias = vec[:, at:at + KT].rearrange("p (g j) -> p j g", j=2)
                src = half(1, 0).rearrange("p (j g r) -> p j g r", j=2, g=4)
                for r in range(2):
                    dst = mod[:, s, :, r].rearrange("p (g j) -> p j g", j=2)
                    ins = ve.tensor_tensor(dst, src[:, :, :, r], bias, ALU.add)
                if s in (1, 4):
                    link(ins)
                    ins = ve.tensor_scalar(mod[:, s, :, :], mod[:, s, :, :], 1.0, None, ALU.add)
                if s == 4:
                    link(ins)
                    at = VEC["nf"][0]
                    ins = ve.tensor_tensor(mod[:, s, :, 1], mod[:, s, :, 0], vec[:, at:at + KT], ALU.mult)
                ins.then_inc(sem("mod_ready"), 1)

            ve.wait_ge(sem("rms"), 1)
            link(ve.reciprocal(rstd[:, :], rstd[:, :]))
            turn(0)
            for n, (a, c) in enumerate(PARTS):
                cs = slice(c * 512, c * 512 + 512)
                ve.wait_ge(sem("odd_ready"), n + 1)
                ve.wait_ge(sem("spec_mm"), SPECTRUM.index(4 * a + c) + 1)
                even, odd = bank[4 * a + c][:, :], spec[:, a, 1, cs]
                ve.tensor_tensor(spec[:, a, 0, cs], even, odd, ALU.add).then_inc(sem("spec_ready"), 1)
                ve.wait_ge(sem("spec_ready"), 2 * n + 1)
                first, second = (odd, even) if a else (even, odd)
                ve.tensor_tensor(odd, first, second, ALU.subtract).then_inc(sem("spec_ready"), 1)
            def normalised(dst, src, r):
                for k in range(KT):
                    ins = ve.scalar_tensor_tensor(out=dst[:, k, :], in0=src[:, k, :], scalar=V("nm", k),
                                                  in1=rstd[:, r * T:r * T + T], op0=ALU.mult, op1=ALU.mult)
                link(ins)

            normalised(hxx, xres, 0)
            turn(1)
            ve.wait_ge(sem("mod_ready"), 2)
            for r, dst in enumerate((hxx, hxc)):
                if r:
                    normalised(hxc, xctx, 1)
                for k in range(KT):
                    ve.tensor_scalar(dst[:, k, :], dst[:, k, :], mod[:, 1, k, r:r + 1],
                                     mod[:, 0, k, r:r + 1], ALU.mult, ALU.add).then_inc(sem("hx_ready"), 1)

            def unit_done(name, j):
                ve.wait_ge(sem("unit_done"), 4 * ROUNDS.index(name) + j + 1)

            for j in range(2, 4):
                unit_done("qk", j)
                ve.tensor_copy(kcx[:, :, (j - 2) * 256:(j - 2) * 256 + 256],
                               bank[4 + j][:, :].rearrange("p (t c) -> p t c", t=TT)).then_inc(sem("kc_ready"), 1)
            ve.wait_ge(sem("wr_loaded"), 16)
            ve.memset(rT[96:97, :], 1.0).then_inc(sem("low_ready"), 1)
            ve.wait_ge(sem("low_mm"), 1)
            ve.tensor_copy(rT[0:96, :], bank[4][0:96, :]).then_inc(sem("low_ready"), 1)
            for j in range(4):
                unit_done("v", j)
                ve.tensor_copy(vc[:, :, j * 256:j * 256 + 256],
                               bank[4 + j][:, :].rearrange("p (t c) -> p t c", t=TT)).then_inc(sem("evac_vc"), 1)

            def gate(n):
                dst = (gx if n < 4 else gc)[:, (n // 2) % 2, n % 2, :]
                ve.wait_ge(sem("gate_ln"), n + 1)
                ve.scalar_tensor_tensor(out=dst, in0=bank[4 + n % 4][:, :], scalar=0.0,
                                        in1=tmp[:, n % 4, :], op0=ALU.min,
                                        op1=ALU.subtract).then_inc(sem("g_ready"), 1)

            convs = {"hv": (0, uT), "hx1": (8, x1c), "hx0": (16, x0T)}

            def unit(name, j):
                if name in convs:
                    base, dst = convs[name]
                    mids[0] += 2
                    ve.wait_ge(sem("conv_mid"), mids[0])
                    for tap, a, b in ((0, 1, 0), (2, 0, 1)):
                        for m in range(2):
                            c = 2 * j + m
                            acc, src = grid(dst[:, c, :]), grid(half(j, m))
                            ins = ve.scalar_tensor_tensor(
                                out=acc[:, :, a:a + 63], in0=src[:, :, b:b + 63],
                                scalar=V("cw", 24 * tap + base + c), in1=acc[:, :, a:a + 63],
                                op0=ALU.mult, op1=ALU.add)
                        if tap == 0:
                            link(ins)
                    ins.then_inc(sem(f"evac_{name}"), 1)
                    if name == "hx1" and j == 3:
                        ve.wait_ge(sem("evac_hx1"), 4)
                        ve.tensor_tensor(uT, uT, x1c, ALU.mult).then_inc(sem("u_ready"), 1)
                elif name == "og":
                    ve.wait_ge(sem("og_sig"), j + 1)
                    dst = og[:, 2 * j:2 * j + 2, :].rearrange("p m t -> p (m t)")
                    ve.tensor_tensor(dst, dst, bank[j][:, :], ALU.mult).then_inc(sem("evac_og"), 1)

            def crest():
                for n in range(4):
                    ve.wait_ge(sem("crest_read"), n + 1)
                    ve.tensor_tensor(kupc[:, n // 2, n % 2, :], kupc[:, n // 2, n % 2, :],
                                     kcx[:, n // 2, :], ALU.mult).then_inc(sem("kupc_ready"), 1)

            def decay():
                for n in range(4):
                    ve.wait_ge(sem("exp_pos"), n + 1)
                    ve.wait_ge(sem("decay_read"), n + 1)
                    d, h = n // 2, 2 * (n % 2)
                    at = 63 if d == 0 else 0
                    link(ve.tensor_copy(
                        dec[:, d, h:h + 2, :],
                        qd[:, d, h:h + 2, :].rearrange("p h (c w) -> p h c w", w=CHUNK)[:, :, :, at]))
                    ve.tensor_tensor(qd[:, d, h:h + 2, :], qd[:, d, h:h + 2, :], qk[:, h:h + 2, :],
                                     ALU.mult)
                    ve.tensor_tensor(ki[:, d, h:h + 2, :], ki[:, d, h:h + 2, :], qk[:, 4 + h:6 + h, :],
                                     ALU.mult).then_inc(sem("qdki_ready"), 1)

            def rest():
                ve.wait_ge(sem("ktok_ready"), 2)
                for m, n in enumerate((2, 3, 0, 1)):
                    ve.wait_ge(sem("rest_read"), m + 1)
                    ve.tensor_tensor(kupx[:, n // 2, n % 2, :], kupx[:, n // 2, n % 2, :],
                                     kcx[:, n // 2, :], ALU.mult).then_inc(sem("kupx_ready"), 1)

            def uspec(c):
                cs = slice(c * 512, c * 512 + 512)
                ve.wait_ge(sem("u_spec"), c + 1)
                ve.wait_ge(sem("odd_ready"), 4 + 2 * c + 2)
                even, odd = [two(bank[b][:, :]) for b in (4, 6)], [u_odd(c, n) for n in range(2)]
                a, b, p, q = (two(tmp[:, n, :]) for n in range(4))
                ve.tensor_tensor(a, even[0], odd[0], ALU.add)
                link(ve.tensor_tensor(b, even[1], odd[1], ALU.add))
                ve.tensor_tensor(odd[0], even[0], odd[0], ALU.subtract)
                link(ve.tensor_tensor(odd[1], odd[1], even[1], ALU.subtract))
                for f, (a, b) in enumerate(((a, b), odd)):
                    re, im = two(spec[:, 0, f, cs]), two(spec[:, 1, f, cs])
                    ins = ve.tensor_tensor(p, a, re, ALU.mult)
                    if f == 0:
                        ins.then_inc(sem("u_read"), 1)
                    link(ve.tensor_tensor(q, b, im, ALU.mult))
                    ve.tensor_tensor(a, a, im, ALU.mult)
                    link(ve.tensor_tensor(b, b, re, ALU.mult))
                    ve.tensor_tensor(re, p, q, ALU.subtract)
                    link(ve.tensor_tensor(im, a, b, ALU.add))
                (re0, re1), (im0, im1) = ([spec[:, n, f, cs] for f in range(2)] for n in range(2))
                ve.tensor_tensor(re0, re0, re1, ALU.add)
                link(ve.tensor_tensor(im0, im0, im1, ALU.subtract))
                ve.scalar_tensor_tensor(out=re1, in0=re1, scalar=-2.0, in1=re0, op0=ALU.mult, op1=ALU.add)
                ve.scalar_tensor_tensor(out=im1, in0=im1, scalar=2.0, in1=im0, op0=ALU.mult,
                                        op1=ALU.add).then_inc(sem("prod_ready"), 1)

            def scores():
                ve.wait_ge(sem("pool_step"), 5)
                for h in range(HEADS):
                    ve.wait_ge(sem("att_mm"), h + 1)
                    ve.copy_predicated(att[:, h, :], C("mask").bitcast(U32),
                                       bank[4 + h][:, :]).then_inc(sem("att_ready"), 1)

            def inverse():
                for c in range(KT):
                    ve.wait_ge(sem("z_mm"), c - c % 2 + 2)
                    u = by_parity(uT[:, c, :])
                    ve.scalar_tensor_tensor(out=u, in0=u, scalar=V("hb", c),
                                            in1=half(4 + c // 2, c % 2).rearrange("p (o q) -> p o q", o=2),
                                            op0=ALU.mult, op1=ALU.add).then_inc(sem("z_read"), 1)
                ve.wait_ge(sem("z_read"), 8)
                ve.wait_ge(sem("evac_hx0"), 4)
                ve.tensor_tensor(uT, uT, x0T, ALU.mult).then_inc(sem("z_ready"), 1)

            def update(h):
                if h >= 2:
                    ve.wait_ge(sem("o_mm"), 2 * h - 2)
                st = sst[h % 2]
                upd = {(0, 0): half(4, 0), (1, 3): half(6, 1), (0, 1): half(6, 0), (1, 2): half(5, 0),
                       (0, 2): half(4, 1), (1, 1): half(7, 0)}
                ve.wait_ge(sem("upd_mm"), 6 * h + 6)
                for n in range(3):
                    for d, c, to in ((0, n, n), (1, 3 - n, 2 - n)):
                        prev = s0[:, h, d, :] if n == 0 else st[:, d, n - 1 if d == 0 else c, :]
                        ins = ve.scalar_tensor_tensor(out=st[:, d, to, :], in0=prev,
                                                      scalar=dec[:, d, h, c:c + 1], in1=upd[(d, c)],
                                                      op0=ALU.mult, op1=ALU.add)
                        if n == 2:
                            ins.then_inc(sem("state_ready"), 1)
                    if n < 2:
                        link(ins)

            def onorm():
                for n in range(2):
                    ve.wait_ge(sem("onorm_read"), n + 1)
                    dst = rso[:, 2 * n:2 * n + 2, :]
                    ins = ve.reciprocal(dst, dst)
                link(ins)
                for m in range(8):
                    ins = ve.scalar_tensor_tensor(out=act[:, m, :], in0=act[:, m, :],
                                                  scalar=V("gn", m % 2), in1=rso[:, m // 2, :],
                                                  op0=ALU.mult, op1=ALU.mult)
                link(ins)
                ve.wait_ge(sem("evac_og"), 4)
                ve.tensor_tensor(act, act, og, ALU.mult).then_inc(sem("act_ready"), 1)

            mids = [0]
            run_middle(dict(gate=gate, crest=crest, decay=decay, rest=rest, uspec=uspec, att=scores,
                            inverse=inverse, update=update, onorm=onorm, turn=turn), unit)
            for j in range(4):
                unit_done("gla", j)
                dst = sma[:, 2 * j:2 * j + 2, :].rearrange("p m t -> p (m t)")
                ve.tensor_tensor(dst, dst, bank[j][:, :], ALU.mult).then_inc(sem("evac_gla"), 1)
            for j in range(4):
                unit_done("hyo", j)
                dst = smb[:, 2 * j:2 * j + 2, :].rearrange("p m t -> p (m t)")
                link(ve.tensor_tensor(dst, dst, bank[j][:, :], ALU.mult))
                y = sma[:, 2 * j:2 * j + 2, :].rearrange("p m t -> p (m t)")
                ve.tensor_tensor(y, y, dst, ALU.add).then_inc(sem("evac_hyo"), 1)
            for j in range(4):
                unit_done("out", j)
                for m in range(2):
                    c = 2 * j + m
                    ins = ve.scalar_tensor_tensor(out=xres[:, c, :], in0=half(j, m),
                                                  scalar=mod[:, 2, c, 0:1], in1=xres[:, c, :],
                                                  op0=ALU.mult, op1=ALU.add)
                ins.then_inc(sem("evac_out"), 1)
            ve.memset(zero, 0.0).then_inc(sem("zero_ready"), 1)
            ve.wait_ge(sem("rms"), 2)
            link(ve.reciprocal(rstd[:, 0:T], rstd[:, 0:T]))
            for k in range(KT):
                ve.scalar_tensor_tensor(out=hxx[:, k, :], in0=xres[:, k, :], scalar=mod[:, 4, k, 1:2],
                                        in1=rstd[:, 0:T], op0=ALU.mult,
                                        op1=ALU.mult).then_inc(sem("hx2_scaled"), 1)
            ve.wait_ge(sem("logit_mm"), 1)
            link(ve.tensor_copy(logit, bank[1][:, 0:TT * E].rearrange("p (t e) -> p t e", t=TT)))
            for t in range(TT):
                ins = ve.max(m8[:, t, :], logit[:, t, :])
            link(ins)
            ve.tensor_scalar(nm, m8[:, :, 0], -1.0, None, ALU.mult).then_inc(sem("top_ready"), 1)
            for t in range(TT):
                ins = ve.max_index(i8[:, t, :], m8[:, t, :], logit[:, t, :])
            link(ins)
            link(ve.tensor_copy(if8, i8))
            experts = C("slot", 0, E)
            each = [P, TT, 4, E]
            link(ve.tensor_tensor(sk, experts.unsqueeze(1).unsqueeze(1).broadcast_to(each),
                                  if8[:, :, 0:4].unsqueeze(3).broadcast_to(each), ALU.is_equal))
            for q in range(3):
                ins = ve.tensor_reduce(sel[:, :, q * E:q * E + E], sk.rearrange("p t k e -> p t e k"),
                                       AX_X, ALU.add)
            ins.then_inc(sem("sel_ready"), 1)
            ve.wait_ge(sem("top_exp"), 2)
            link(ve.reciprocal(es, es))
            for t in range(TT):
                ins = ve.tensor_scalar(ew[:, t, :], ew[:, t, :], es[:, t:t + 1], None, ALU.mult)
            link(ins)
            ve.wait_ge(sem("count_mm"), 1)
            link(ve.tensor_copy(cnt[:, 0:1], bank[1][0:96, 64:65]))
            link(ve.tensor_scalar(cnt[:, 1:2], cnt[:, 0:1], 1.0 * SLOTS, 1.0, ALU.is_gt, ALU.add))
            link(ve.scalar_tensor_tensor(out=cnt[:, 2:3], in0=cnt[:, 0:1], scalar=2.0 * SLOTS,
                                         in1=cnt[:, 1:2], op0=ALU.is_gt, op1=ALU.add))
            ve.scalar_tensor_tensor(out=cnt[:, 3:4], in0=cnt[:, 0:1], scalar=3.0 * SLOTS,
                                    in1=cnt[:, 2:3], op0=ALU.is_gt, op1=ALU.add).then_inc(sem("pass_ready"), 1)
            link(ve.tensor_tensor(gk, sk, ew.unsqueeze(3).broadcast_to(each), ALU.mult))
            ve.tensor_reduce(gate_, gk.rearrange("p t k e -> p t e k"), AX_X,
                             ALU.add).then_inc(sem("gate_ready"), 1)
            ve.wait_ge(sem("turned_sel"), 1)
            link(ve.tensor_copy(selT, bank[2][0:32, 0:T]))
            ve.wait_ge(sem("place_mm"), 1)
            link(ve.tensor_scalar(posm, bank[0][0:32, 0:T], 16.0, FAR, ALU.mult, ALU.add))
            link(ve.tensor_tensor(posm, posm, selT, ALU.mult))
            link(ve.tensor_scalar(posm, posm, -FAR, None, ALU.add))
            ve.wait_ge(sem("start_mm"), 1)
            ve.tensor_copy(nitems, bank[1][0:1, 68:69]).then_inc(sem("list_ready"), 1)
            link(ve.tensor_copy(cnt[:, 4:5], bank[1][0:96, 66:67]))
            link(ve.tensor_tensor(cnt[:, 5:6], cnt[:, 4:5], cnt[:, 3:4], ALU.add))
            item = C("slot", 0, MAXI, p=96)
            ve.tensor_scalar(Q, item[0:E, :], cnt[0:E, 4:5], -1.0 * SLOTS, ALU.subtract, ALU.mult)
            link(ve.tensor_scalar(T3, item, cnt[:, 4:5], None, ALU.is_ge))
            link(ve.scalar_tensor_tensor(out=T3, in0=item, scalar=cnt[:, 5:6], in1=T3,
                                         op0=ALU.is_lt, op1=ALU.mult))
            ve.tensor_tensor(Q, Q, T3[0:E, :], ALU.mult)
            ve.wait_ge(sem("turned_gate"), 1)
            ve.tensor_copy(gateT, bank[3][0:32, 0:T]).then_inc(sem("items_ready"), 1)
            ve.memset(bounds[:, 0:1], 0)
            ve.wait_ge(sem("ends_mm"), 1)
            ve.tensor_scalar(lasts, bank[1][0:1, 96:128], -1.0, None, ALU.add).then_inc(sem("list_ready"), 1)
            ve.tensor_copy(bounds[:, 1:], bank[1][0:1, 96:128]).then_inc(sem("list_ready"), 1)
            ve.wait_ge(sem("itemcol_mm"), 1)
            ve.tensor_copy(posI, bank[0][:, 256:384].rearrange("p (t i) -> p t i", t=TT))
            link(ve.tensor_copy(gateI, bank[0][:, 384:512].rearrange("p (t i) -> p t i", t=TT)))

            slots = C("slot")

            def picks(i):
                for t in range(TT):
                    ins = ve.tensor_scalar(pick[:, t, :], slots, posI[:, t, bass.ds(i, 1)], None,
                                           ALU.is_equal)
                ins.then_inc(sem("pick_ready"), 1)

            def spreads(i):
                for t in range(TT):
                    ins = ve.tensor_scalar(spread[:, t, :], slots, posI[:, t, bass.ds(i, 1)],
                                           gateI[:, t, bass.ds(i, 1)], ALU.is_equal, ALU.mult)
                ins.then_inc(sem("spread_ready"), 1)

            def bias_select(i):
                ve.tensor_scalar(bsel, ones[0:96, 0:SLOTS], T3[:, bass.ds(i, 1)], None,
                                 ALU.mult).then_inc(sem("bsel_ready"), 1)

            picks(0)
            spreads(0)
            bias_select(0)
            ve.memset(aT, 0.0).then_inc(sem("aT_ready"), 1)
            ve.wait_ge(sem("list_ready"), 3)
            n = ve.value_load(nitems, min_val=E, max_val=48)
            with ve.Fori(0, n) as i:
                ve.wait_ge(sem("gathered"), i + 1)
                picks(i + 1)
                ve.wait_ge(sem("chunk_used"), CHUNKS * i + 8)
                ve.tensor_scalar(glu, bank[0][:, :], LIMIT, None, ALU.min).then_inc(sem("glu_ready"), 1)
                ve.tensor_scalar(lin, bank[1][:, :], LIMIT, -LIMIT, ALU.min,
                                 ALU.max).then_inc(sem("lin_ready"), 1)
                bias_select(i + 1)
                ve.wait_ge(sem("glu_ready"), i + 1)
                ve.wait_ge(sem("lin_ready"), i + 1)
                ve.scalar_tensor_tensor(out=lin, in0=lin, scalar=1.0, in1=glu, op0=ALU.add,
                                        op1=ALU.mult).then_inc(sem("gated"), 1)
                ve.wait_ge(sem("gated"), i + 1)
                ve.wait_ge(sem("sg_ready"), i + 1)
                ve.tensor_tensor(am, lin, sg, ALU.mult).then_inc(sem("a_ready"), 1)
                ve.wait_ge(sem("turned"), i + 1)
                ve.tensor_copy(aT.rearrange("p b h s -> p (b h s)"), bank[0][:, :]).then_inc(sem("aT_ready"), 1)
                ve.wait_ge(sem("spread_turned"), i + 1)
                spreads(i + 1)
            for c in range(KT):
                if c % 2 == 0:
                    ve.wait_ge(sem("scattered"), n + (c // 2 + 1))
                ve.scalar_tensor_tensor(out=xres[:, c, :], in0=half(4 + c // 2, c % 2),
                                        scalar=mod[:, 5, c, 0:1], in1=xres[:, c, :],
                                        op0=ALU.mult, op1=ALU.add).then_inc(sem("x2_ready"), 1)
            ve.wait_ge(sem("rms"), 3)
            link(ve.reciprocal(rstd[:, 0:T], rstd[:, 0:T]))
            for k in range(KT):
                ve.scalar_tensor_tensor(out=hxx[:, k, :], in0=xres[:, k, :], scalar=V("nfin", k),
                                        in1=rstd[:, 0:T], op0=ALU.mult,
                                        op1=ALU.mult).then_inc(sem("out_ready"), 1)

        @block.gpsimd
        def _(po):
            for n in range(4):
                t, c = n // 2, n % 2
                po.wait_ge(sem("taps_win"), n + 1)
                po.tensor_tensor(hdif[:, t, c * 512:c * 512 + 512], htmp[:, n % 2, 0, :],
                                 htmp[:, n % 2, 1, :], ALU.subtract).then_inc(sem("pool_step"), 1)
            po.wait_ge(sem("prod_ready"), 2)
            po.memset(region(14), 0.0).then_inc(sem("pool_step"), 1)
            po.wait_ge(sem("bup_loaded"), 3 * 16)
            po.tensor_copy(bp, bupsb).then_inc(sem("bup_split"), 1)
            for n, rows in enumerate((64, 32)):
                po.wait_ge(sem("bup_split"), 2 * n + 1)
                po.tensor_tensor(bupsb[0:rows, :], bupsb[0:rows, :], bp[0:rows, :],
                                 ALU.subtract).then_inc(sem("bup_split"), 1)
                po.wait_ge(sem("bup_split"), 2 * n + 2)
                po.tensor_copy(bp[0:rows, :], bupsb[0:rows, :]).then_inc(sem("bup_split"), 1)
            po.wait_ge(sem("evac_hyo"), 4)
            po.dma_start(bdn, bdown.rearrange("e (k n) -> e k n", n=256)).then_inc(sem("bdn_loaded"), 16)
            po.wait_ge(sem("unit_done"), 4 * len(ROUNDS))
            po.dma_start(wrt, wrouter).then_inc(sem("wrt_loaded"), 16)
            po.dma_start(brt, brouter).then_inc(sem("brt_loaded"), 16)


def by_parity(a):
    return a.reshape(P, 2, *a.shape[1:]).swapaxes(0, 1)


def shape_constants():
    c = np.zeros((P, NCON), np.float32)

    def put(name, a):
        at, width = CON[name]
        a = np.asarray(a, np.float64).reshape(len(a), width)
        c[:len(a), at:at + width] = a

    s, t = np.arange(P)[:, None], np.arange(P)[None]
    same = s // CHUNK == t // CHUNK
    put("ident", s == t)
    put("ones", np.ones((P, P)))
    upto, frm = (s <= t) & same, (s >= t) & same
    put("mask", np.concatenate([upto, frm, upto, frm], 1) / GNORM)
    put("rest", np.concatenate([(s > t) & same, (s < t) & same], 1) / GNORM)
    put("after", (s > t) / GNORM)
    put("before", (s < t) / GNORM)
    put("all16", np.ones((P, P)) / GNORM)
    n = by_parity(np.arange(T))
    ang = np.pi * n[:, :, None] * (2 * np.arange(P) + 1) / (2 * T)
    fwd = np.stack([np.cos(ang), -np.sin(ang)])
    put("dft", fwd.transpose(2, 0, 1, 3).reshape(P, -1))
    put("idft", fwd.transpose(3, 0, 1, 2).reshape(P, -1) / T)
    put("slot", np.tile(np.arange(SLOTS), (P, 2)))
    put("stack", s % E == np.arange(E))
    put("tri", np.arange(E)[:, None] < np.arange(96)[None] % E)
    pos = np.arange(T, dtype=np.float64)
    tn = (pos / (T - 1)).astype(np.float32)
    bands = (EMB - 1) // 2
    f = np.linspace(1e-4, bands - 1, bands).astype(np.float32)
    a = (np.float32(2 * np.pi / T) * pos.astype(np.float32)[:, None] * f[None]).astype(np.float32)
    z = np.concatenate([tn[:, None], np.cos(a, dtype=np.float64), -np.sin(a, dtype=np.float64)], 1)
    deltas = np.abs(np.linspace(np.log(1e-2) / 1.5, np.log(1e-2) / 0.3, D).astype(np.float32))
    w = np.exp(-tn[:, None].astype(np.float64) * deltas[None])
    z, w = (by_parity(v.astype(np.float32)) for v in (z, w))
    return c, z.reshape(T, EMB).T, w


def kernel(**inputs):
    import concourse.bacc as bacc
    from concourse.bass_utils import run_bass_kernel_spmd

    a = {k: np.asarray(v) for k, v in inputs.items()}
    for k in a:
        if a[k].shape[0] == 1 and k not in ("x", "c", "ctx"):
            a[k] = a[k][0]
    con, z, window = shape_constants()
    vecs = np.zeros((P, NVEC), np.float32)

    def put(name, v, rows=P):
        at, width = VEC[name]
        vecs[:rows, at:at + width] = v

    def cols(v):
        return v.reshape(-1, P).T

    put("c", cols(a["c"][0]))
    put("cctx", cols(a["c_ctx"]))
    put("nm", cols(a["norm_mix"]))
    put("nf", cols(a["norm_ffn"]))
    put("nfin", cols(a["norm_final"]))
    put("bada", cols(a["b_ada"]))
    order = np.concatenate([np.arange(2 * D, 3 * D), np.arange(D, 2 * D), np.arange(D)])
    put("cw", np.concatenate([cols(a["hy_conv_w"][i][order]) for i in range(3)], 1))
    put("cb", cols(a["hy_conv_b"][order]))
    put("hb", cols(a["hy_bias"]))
    put("gn", cols(a["gla_norm"]))
    put("hmlp", np.stack([a["hy_f_b1"], a["hy_f_b2"], a["hy_f_b3"], a["hy_sin_freq"]], 1), ORDER)
    hw = np.zeros((ORDER, 192), np.float32)
    hw[:EMB, 0:64] = a["hy_f_w1"]
    hw[:, 64:128] = a["hy_f_w2"]
    hw[:, 128:192] = a["hy_f_w3"]
    w_in, w_ada = a["w_in"], a["w_ada"]
    blocks = {"qk": w_in[:, 0:1024], "v": w_in[:, 1024:2048], "og": w_in[:, 2048:3072],
              "hx0": w_in[:, 3104:4128], "hx1": w_in[:, 4128:5152], "hv": w_in[:, 5152:6176],
              "ma": w_in[:, 6176:7200], "mb": w_in[:, 7200:8224],
              "gla": a["w_gla_out"], "hyo": a["w_hy_out"], "out": a["w_out"]}
    for s in range(6):
        blocks[f"ada{s}"] = w_ada[:, s * D:s * D + D]
    wmix = np.stack([blocks[r].reshape(KT, P, 4, 256).transpose(2, 1, 0, 3).reshape(4, P, KT * 256)
                     for r in ROUNDS])
    xt = np.concatenate([a["x"][0], a["ctx"][0]], 0).T.reshape(KT, P, 2 * T)
    wgk = np.zeros((97, 2, 512), np.float32)
    for g in (0, 32, 64):
        wgk[g:g + 16, 0], wgk[g + 16:g + 32, 1] = a["w_gk_f"], a["w_gk_b"]
    wgk[96, 0], wgk[96, 1] = a["b_gk_f"], a["b_gk_b"]
    wup = a["w_up"].reshape(E, KT, P, 2, 512, 2).transpose(0, 1, 2, 3, 5, 4).reshape(E, KT, P, 2048)
    wdown = a["w_down"].reshape(E, 4, 2, P, D).transpose(0, 1, 3, 2, 4).reshape(E, 4, P, 2 * D)
    bup = a["b_up"].reshape(E, 2, 512, 2).transpose(0, 1, 3, 2).reshape(E, 2048)
    arrays = {
        "vecs": vecs, "cons": con, "xt": xt, "zt": z, "hw": hw, "hw4": a["hy_f_w4"], "window": window,
        "wmix": wmix, "wr": w_in[:, 3072:3104].reshape(KT, P, 32).transpose(1, 0, 2), "wgk": wgk,
        "wrouter": a["w_router"].reshape(KT, P, E).transpose(1, 0, 2), "brouter": a["b_router"][None],
        "wexp": np.concatenate([wup, wdown], 1), "bup": bup, "bdown": a["b_down"],
    }
    nc = bacc.Bacc("TRN2", target_bir_lowering=False, num_devices=1)
    sent, args = {}, []
    for name, v in arrays.items():
        sent[f"in_{name}"] = np.ascontiguousarray(v)
        args.append(nc.dram_tensor(f"in_{name}", v.shape, F32, kind="ExternalInput").ap())
    args.append(nc.dram_tensor("out_t", (KT, P, T), F32, kind="ExternalOutput").ap())
    build_program(nc, *args)
    r = run_bass_kernel_spmd(nc, [sent], core_ids=[0])
    return np.ascontiguousarray(r.results[0]["out_t"].reshape(D, T).T)[None]
```
